# Optimizing a Trainium2 kernel written in Bass

```python
import jax, jax.numpy as jnp
from jax import lax
import numpy as np
import math

D_MODEL = 2048
BATCH = 1
SEQ = 256
DEPTH = 1

EPS = 1e-6
N_BRANCH = 3
BRANCH_WIDTH = D_MODEL // 4
SGU_GROUPS = 8
SGU_GROUP_DIM = BRANCH_WIDTH // SGU_GROUPS
SGU_CHUNK = 128
MOBA_HEADS = 8
MOBA_HEAD_DIM = BRANCH_WIDTH // MOBA_HEADS
MOBA_BLOCK = 256
MOBA_TOPK = 3
MOBA_QBLOCK = 64
POOL_WINDOWS = (2, 4, 8, 16)
POOL_GROUPS = 4
POOL_GROUP_DIM = BRANCH_WIDTH // POOL_GROUPS
IN_SPLIT_POINTS = tuple(BRANCH_WIDTH * i for i in range(1, 7))
IN_WIDTH = 6 * BRANCH_WIDTH + N_BRANCH * D_MODEL
D_FF = 11 * D_MODEL // 4
CONV_WIDTH = 3
N_MOD = 6


def rms_norm(x, g):
    xf = x.astype(jnp.float32)
    y = xf * lax.rsqrt(jnp.mean(xf * xf, axis=-1, keepdims=True) + EPS)
    return (y * g.astype(jnp.float32)).astype(x.dtype)

def alibi_slopes(n_heads):
    return jnp.exp2(-(8.0 / n_heads) * jnp.arange(1, n_heads + 1, dtype=jnp.float32))

def spatial_gating(u, v, norm_g, w_s, b_s):
    Bsz, S, _ = u.shape
    vf = v.astype(jnp.float32)
    mu = jnp.mean(vf, axis=-1, keepdims=True)
    var = jnp.mean(jnp.square(vf - mu), axis=-1, keepdims=True)
    vn = (vf - mu) * lax.rsqrt(var + EPS) * norm_g.astype(jnp.float32)
    vc = vn.reshape(Bsz, S // SGU_CHUNK, SGU_CHUNK, SGU_GROUPS, SGU_GROUP_DIM)
    mask = jnp.tril(jnp.ones((SGU_CHUNK, SGU_CHUNK), jnp.float32))
    w = w_s.astype(jnp.float32) * mask
    mixed = jnp.einsum('gts,bcsgd->bctgd', w, vc) + b_s.astype(jnp.float32).T[None, None, :, :, None]
    return u * mixed.reshape(Bsz, S, BRANCH_WIDTH).astype(u.dtype)

def moba_attention(q, k, v):
    Bsz, S, _ = q.shape
    H, Dh, BLK, QB = MOBA_HEADS, MOBA_HEAD_DIM, MOBA_BLOCK, MOBA_QBLOCK
    nb = -(-S // BLK)
    pad = nb * BLK - S

    def heads(t):
        return t.reshape(Bsz, S, H, Dh).transpose(0, 2, 1, 3)

    qh = heads(q)
    kb = jnp.pad(heads(k), ((0, 0), (0, 0), (0, pad), (0, 0))).reshape(Bsz, H, nb, BLK, Dh)
    vb = jnp.pad(heads(v), ((0, 0), (0, 0), (0, pad), (0, 0))).reshape(Bsz, H, nb, BLK, Dh)
    kmean = jnp.mean(kb.astype(jnp.float32), axis=3)
    slopes = alibi_slopes(H)[None, :, None, None]
    k_sel = min(MOBA_TOPK, nb)
    scale = Dh ** -0.5
    bi = jnp.arange(Bsz)[:, None, None, None]
    hi = jnp.arange(H)[None, :, None, None]
    key_off = jnp.arange(BLK)
    n_q = S // QB
    q_chunks = qh.reshape(Bsz, H, n_q, QB, Dh).transpose(2, 0, 1, 3, 4)

    def attend(args):
        qc, ci = args
        t = ci * QB + jnp.arange(QB)
        own = (ci * QB) // BLK
        blk_scores = jnp.einsum('bhqd,bhnd->bhqn', qc.astype(jnp.float32), kmean)
        blk_scores = jnp.where(jnp.arange(nb) < own, blk_scores, -jnp.inf)
        _, idx = lax.top_k(blk_scores, k_sel)
        ksel = kb[bi, hi, idx]
        vsel = vb[bi, hi, idx]
        s_past = jnp.einsum('bhqd,bhqjsd->bhqjs', qc, ksel,
                            preferred_element_type=jnp.float32) * scale
        pos_past = idx[..., None] * BLK + key_off
        dist_past = (t[None, None, :, None, None] - pos_past).astype(jnp.float32)
        s_past = s_past - slopes[..., None] * dist_past
        valid = (jnp.arange(k_sel) < own)[:, None]
        s_past = jnp.where(valid, s_past, -jnp.inf).reshape(Bsz, H, QB, k_sel * BLK)
        k_own = lax.dynamic_index_in_dim(kb, own, axis=2, keepdims=False)
        v_own = lax.dynamic_index_in_dim(vb, own, axis=2, keepdims=False)
        dist_own = t[:, None] - (own * BLK + key_off)[None, :]
        s_own = jnp.einsum('bhqd,bhsd->bhqs', qc, k_own,
                           preferred_element_type=jnp.float32) * scale
        s_own = s_own - slopes * dist_own.astype(jnp.float32)
        s_own = jnp.where(dist_own >= 0, s_own, -jnp.inf)
        p = jax.nn.softmax(jnp.concatenate([s_past, s_own], axis=-1), axis=-1)
        p_past = p[..., :k_sel * BLK].reshape(Bsz, H, QB, k_sel, BLK).astype(v.dtype)
        p_own = p[..., k_sel * BLK:].astype(v.dtype)
        o = (jnp.einsum('bhqjs,bhqjsd->bhqd', p_past, vsel, preferred_element_type=jnp.float32)
             + jnp.einsum('bhqs,bhsd->bhqd', p_own, v_own, preferred_element_type=jnp.float32))
        return o.astype(v.dtype)

    out = lax.map(attend, (q_chunks, jnp.arange(n_q)))
    return out.transpose(1, 0, 3, 2, 4).reshape(Bsz, S, H * Dh)

def multiscale_pool(z, pool_w, pool_scale):
    Bsz, S, _ = z.shape
    zf = z.astype(jnp.float32).reshape(Bsz, S, POOL_GROUPS, POOL_GROUP_DIM)
    cs = jnp.pad(jnp.cumsum(zf, axis=1), ((0, 0), (1, 0), (0, 0), (0, 0)))
    t = jnp.arange(S)
    means = []
    for gi, w in enumerate(POOL_WINDOWS):
        lo = jnp.maximum(t + 1 - w, 0)
        win_sum = cs[:, 1:, gi] - jnp.take(cs[:, :, gi], lo, axis=1)
        count = jnp.minimum(t + 1, w).astype(jnp.float32)
        means.append(win_sum / count[None, :, None])
    pooled = jnp.stack(means, axis=2) - zf
    y = jnp.einsum('bsgc,gcd->bsgd', pooled, pool_w.astype(jnp.float32))
    return (y.reshape(Bsz, S, BRANCH_WIDTH) * pool_scale.astype(jnp.float32)).astype(z.dtype)

def token_mixing(h, w_in, b_in, sgu_norm_g, sgu_w, sgu_b, pool_w, pool_scale,
                 w_sgu_out, w_moba_out, w_pool_out, w_out):
    p = h @ w_in + b_in
    u, v, q, k, v_att, z_pool, gates = jnp.split(p, IN_SPLIT_POINTS, axis=-1)
    y_sgu = spatial_gating(jax.nn.gelu(u), jax.nn.gelu(v), sgu_norm_g, sgu_w, sgu_b)
    y_moba = moba_attention(q, k, v_att)
    y_pool = multiscale_pool(z_pool, pool_w, pool_scale)
    g_sgu, g_moba, g_pool = jnp.split(jax.nn.sigmoid(gates), N_BRANCH, axis=-1)
    merged = (g_sgu * (y_sgu @ w_sgu_out) + g_moba * (y_moba @ w_moba_out)
              + g_pool * (y_pool @ w_pool_out))
    return merged @ w_out

def conv_ffn(h, w_up, w_conv, b_conv, w_down):
    z = h @ w_up
    z1 = jnp.pad(z[:, :-1], ((0, 0), (1, 0), (0, 0)))
    z2 = jnp.pad(z[:, :-2], ((0, 0), (2, 0), (0, 0)))
    z = w_conv[0] * z2 + w_conv[1] * z1 + w_conv[2] * z + b_conv
    gate, val = jnp.split(z, 2, axis=-1)
    return (jax.nn.gelu(gate) * val) @ w_down

def first_inputs(seed: int = 0) -> dict:
    key = jax.random.key(seed)
    ks = jax.random.split(key, 24)
    f32 = jnp.float32
    L, D = DEPTH, D_MODEL

    def nrm(k, shape, s):
        return jax.random.normal(k, shape, f32) * s

    return {
        "x": nrm(ks[0], (BATCH, SEQ, D), 1.0),
        "c": nrm(ks[1], (BATCH, D), 1.0),
        "g_pre_mix": 1.0 + nrm(ks[2], (L, D), 0.02),
        "g_post_mix": 1.0 + nrm(ks[3], (L, D), 0.02),
        "g_pre_ffn": 1.0 + nrm(ks[4], (L, D), 0.02),
        "g_post_ffn": 1.0 + nrm(ks[5], (L, D), 0.02),
        "w_ada": nrm(ks[6], (L, D, N_MOD * D), D ** -0.5),
        "b_ada": nrm(ks[7], (L, N_MOD * D), 0.01),
        "w_in": nrm(ks[8], (L, D, IN_WIDTH), D ** -0.5),
        "b_in": nrm(ks[9], (L, IN_WIDTH), 0.01),
        "sgu_norm_g": 1.0 + nrm(ks[10], (L, BRANCH_WIDTH), 0.02),
        "sgu_w": nrm(ks[11], (L, SGU_GROUPS, SGU_CHUNK, SGU_CHUNK), SGU_CHUNK ** -0.5),
        "sgu_b": 1.0 + nrm(ks[12], (L, SGU_GROUPS, SGU_CHUNK), 0.02),
        "pool_w": nrm(ks[13], (L, POOL_GROUPS, POOL_GROUP_DIM, POOL_GROUP_DIM), POOL_GROUP_DIM ** -0.5),
        "pool_scale": 1.0 + nrm(ks[14], (L, BRANCH_WIDTH), 0.02),
        "w_sgu_out": nrm(ks[15], (L, BRANCH_WIDTH, D), BRANCH_WIDTH ** -0.5),
        "w_moba_out": nrm(ks[16], (L, BRANCH_WIDTH, D), BRANCH_WIDTH ** -0.5),
        "w_pool_out": nrm(ks[17], (L, BRANCH_WIDTH, D), BRANCH_WIDTH ** -0.5),
        "w_out": nrm(ks[18], (L, D, D), D ** -0.5),
        "w_up": nrm(ks[19], (L, D, 2 * D_FF), D ** -0.5),
        "w_conv": nrm(ks[20], (L, CONV_WIDTH, 2 * D_FF), CONV_WIDTH ** -0.5),
        "b_conv": nrm(ks[21], (L, 2 * D_FF), 0.01),
        "w_down": nrm(ks[22], (L, D_FF, D), D_FF ** -0.5),
    }

def first_block(x, c, g_pre_mix, g_post_mix, g_pre_ffn, g_post_ffn, w_ada, b_ada,
              w_in, b_in, sgu_norm_g, sgu_w, sgu_b, pool_w, pool_scale,
              w_sgu_out, w_moba_out, w_pool_out, w_out, w_up, w_conv, b_conv, w_down):
    cond = jax.nn.silu(c)
    for l in range(DEPTH):
        mod = cond @ w_ada[l] + b_ada[l]
        sh1, sc1, gt1, sh2, sc2, gt2 = [m[:, None, :] for m in jnp.split(mod, N_MOD, axis=-1)]
        h = rms_norm(x, g_pre_mix[l]) * (1.0 + sc1) + sh1
        y = token_mixing(h, w_in[l], b_in[l], sgu_norm_g[l], sgu_w[l], sgu_b[l],
                         pool_w[l], pool_scale[l], w_sgu_out[l], w_moba_out[l],
                         w_pool_out[l], w_out[l])
        x = x + gt1 * rms_norm(y, g_post_mix[l])
        h = rms_norm(x, g_pre_ffn[l]) * (1.0 + sc2) + sh2
        y = conv_ffn(h, w_up[l], w_conv[l], b_conv[l], w_down[l])
        x = x + gt2 * rms_norm(y, g_post_ffn[l])
    return x


_first_inputs = first_inputs


def first_inputs(seed=0):
    import zlib

    import numpy as np

    out = dict(_first_inputs(seed))
    spreads = {}
    factors = {'g_pre_mix': 4.216,
     'g_post_mix': 5.079,
     'g_pre_ffn': 12.708,
     'g_post_ffn': 22.698,
     'b_ada': 3.645,
     'b_in': 8.0,
     'sgu_norm_g': 45.712,
     'sgu_b': 33.688,
     'pool_scale': 28.601,
     'b_conv': 29.729}
    for name, (base, spread) in spreads.items():
        noise = np.random.default_rng([zlib.crc32(name.encode()), seed]).standard_normal(out[name].shape)
        drawn = base * np.exp(spread * noise) if base else spread * noise
        out[name] = __import__('jax').numpy.asarray(drawn.astype(out[name].dtype))
    for name, factor in factors.items():
        out[name] = (out[name] * factor).astype(out[name].dtype)
    return out


_narrow_inputs = first_inputs


def first_inputs(seed=0):

    out = dict(_narrow_inputs(seed))
    wider = {'g_post_ffn': 3.3, 'sgu_norm_g': 4.29, 'sgu_b': 4.15, 'pool_scale': 4.15}
    for name, times in wider.items():
        mean = out[name].mean()
        out[name] = (mean + times * (out[name] - mean)).astype(out[name].dtype)
    return out


N_META = 16
MLA_HEADS = 16
Q_LORA = 512
KV_LORA = 512
QK_NOPE = 128
QK_ROPE = 64
V_HEAD = 128
ROPE_THETA = 10000.0
Q_BLOCK = 128
SSM_WIDTH = 1024
SSM_GROUP = 16
SSM_GROUPS = SSM_WIDTH // SSM_GROUP
SSM_STATE = 64
DT_MIN = 1e-3
DT_MAX = 1e-1
N_BRANCH_2 = 2
D_FF_2 = -(-8 * D_MODEL // (3 * 256)) * 256
OFF_Q = Q_LORA
OFF_KV = OFF_Q + KV_LORA
OFF_KR = OFF_KV + QK_ROPE
OFF_U = OFF_KR + SSM_WIDTH
IN_WIDTH_2 = OFF_U + N_BRANCH_2 * D_MODEL


def rms_norm_2(x, g):
    xf = x.astype(jnp.float32)
    y = xf * lax.rsqrt(jnp.mean(xf * xf, axis=-1, keepdims=True) + EPS)
    return y.astype(x.dtype) * g.astype(x.dtype)

def rope_tables(length):
    half = QK_ROPE // 2
    freqs = ROPE_THETA ** (-jnp.arange(half, dtype=jnp.float32) / half)
    ang = jnp.arange(length, dtype=jnp.float32)[:, None] * freqs[None, :]
    return jnp.cos(ang), jnp.sin(ang)

def apply_rope(x, cos, sin):
    half = QK_ROPE // 2
    x1, x2 = x[..., :half], x[..., half:]
    c, s = cos.astype(x.dtype), sin.astype(x.dtype)
    return jnp.concatenate([x1 * c - x2 * s, x2 * c + x1 * s], axis=-1)

def mla_attention(q_nope, q_rope, k_nope, k_rope, v):
    length = q_nope.shape[1]
    scale = (QK_NOPE + QK_ROPE) ** -0.5
    outs = []
    for start in range(0, length, Q_BLOCK):
        end = min(start + Q_BLOCK, length)
        s = (jnp.einsum('bqhd,bkhd->bhqk', q_nope[:, start:end], k_nope[:, :end])
             + jnp.einsum('bqhr,bkr->bhqk', q_rope[:, start:end], k_rope[:, :end]))
        s = s.astype(jnp.float32) * scale
        q_pos = jnp.arange(start, end)[:, None]
        k_pos = jnp.arange(end)[None, :]
        s = jnp.where(k_pos <= q_pos, s, -jnp.inf)
        p = jax.nn.softmax(s, axis=-1).astype(v.dtype)
        outs.append(jnp.einsum('bhqk,bkhd->bqhd', p, v[:, :end]))
    return jnp.concatenate(outs, axis=1)

def s5_scan(u, lam_re, lam_im, log_step, b_re, b_im, c_re, c_im, d):
    f32 = jnp.float32
    step = jnp.exp(log_step.astype(f32))[:, None]
    lr, li = lam_re.astype(f32), lam_im.astype(f32)
    mag = jnp.exp(lr * step)
    ab_re, ab_im = mag * jnp.cos(li * step), mag * jnp.sin(li * step)
    den = lr * lr + li * li
    nr, ni = ab_re - 1.0, ab_im
    coef_re = (nr * lr + ni * li) / den
    coef_im = (ni * lr - nr * li) / den
    br, bi = b_re.astype(f32), b_im.astype(f32)
    bb_re = coef_re[..., None] * br - coef_im[..., None] * bi
    bb_im = coef_re[..., None] * bi + coef_im[..., None] * br
    uf = u.astype(f32)
    bu_re = jnp.einsum('blgp,gnp->blgn', uf, bb_re)
    bu_im = jnp.einsum('blgp,gnp->blgn', uf, bb_im)
    a_re = jnp.broadcast_to(ab_re, bu_re.shape)
    a_im = jnp.broadcast_to(ab_im, bu_im.shape)

    def combine(e1, e2):
        a1r, a1i, b1r, b1i = e1
        a2r, a2i, b2r, b2i = e2
        return (a2r * a1r - a2i * a1i,
                a2r * a1i + a2i * a1r,
                a2r * b1r - a2i * b1i + b2r,
                a2r * b1i + a2i * b1r + b2i)

    _, _, x_re, x_im = lax.associative_scan(combine, (a_re, a_im, bu_re, bu_im), axis=1)
    y = (jnp.einsum('blgn,gpn->blgp', x_re, c_re.astype(f32))
         - jnp.einsum('blgn,gpn->blgp', x_im, c_im.astype(f32))
         + d.astype(f32) * uf)
    return y

def second_inputs(seed: int = 0) -> dict:
    key = jax.random.key(seed)
    ks = jax.random.split(key, 32)
    f32 = jnp.float32
    nrm = lambda k, shape, scale: jax.random.normal(k, shape, f32) * scale
    gain = lambda k, shape: 1.0 + 0.02 * jax.random.normal(k, shape, f32)
    G, N, P = SSM_GROUPS, SSM_STATE, SSM_GROUP
    lam_re = -0.5 * jnp.exp(0.05 * jax.random.normal(ks[9], (DEPTH, G, N), f32))
    lam_im = jnp.broadcast_to(math.pi * jnp.arange(N, dtype=f32), (DEPTH, G, N))
    log_step = jax.random.uniform(ks[10], (DEPTH, G), f32, math.log(DT_MIN), math.log(DT_MAX))
    return {
        "x": nrm(ks[0], (BATCH, SEQ, D_MODEL), 1.0),
        "meta_tokens": nrm(ks[1], (N_META, D_MODEL), 1.0),
        "norm_mix": gain(ks[2], (DEPTH, D_MODEL)),
        "w_in": nrm(ks[3], (DEPTH, D_MODEL, IN_WIDTH_2), D_MODEL ** -0.5),
        "norm_q": gain(ks[4], (DEPTH, Q_LORA)),
        "w_q_up": nrm(ks[5], (DEPTH, Q_LORA, MLA_HEADS * (QK_NOPE + QK_ROPE)), Q_LORA ** -0.5),
        "norm_kv": gain(ks[6], (DEPTH, KV_LORA)),
        "w_kv_up": nrm(ks[7], (DEPTH, KV_LORA, MLA_HEADS * (QK_NOPE + V_HEAD)), KV_LORA ** -0.5),
        "w_attn_proj": nrm(ks[8], (DEPTH, MLA_HEADS * V_HEAD, D_MODEL), (MLA_HEADS * V_HEAD) ** -0.5),
        "ssm_lambda_re": lam_re,
        "ssm_lambda_im": lam_im,
        "ssm_log_step": log_step,
        "ssm_b_re": nrm(ks[11], (DEPTH, G, N, P), (2 * P) ** -0.5),
        "ssm_b_im": nrm(ks[12], (DEPTH, G, N, P), (2 * P) ** -0.5),
        "ssm_c_re": nrm(ks[13], (DEPTH, G, P, N), N ** -0.5),
        "ssm_c_im": nrm(ks[14], (DEPTH, G, P, N), N ** -0.5),
        "ssm_d": nrm(ks[15], (DEPTH, G, P), 1.0),
        "w_glu_val": nrm(ks[16], (DEPTH, SSM_WIDTH, D_MODEL), SSM_WIDTH ** -0.5),
        "w_glu_gate": nrm(ks[17], (DEPTH, SSM_WIDTH, D_MODEL), SSM_WIDTH ** -0.5),
        "w_out": nrm(ks[18], (DEPTH, D_MODEL, D_MODEL), D_MODEL ** -0.5),
        "norm_ffn": gain(ks[19], (DEPTH, D_MODEL)),
        "w_ffn_gate": nrm(ks[20], (DEPTH, D_MODEL, D_FF_2), D_MODEL ** -0.5),
        "w_ffn_up": nrm(ks[21], (DEPTH, D_MODEL, D_FF_2), D_MODEL ** -0.5),
        "w_ffn_down": nrm(ks[22], (DEPTH, D_FF_2, D_MODEL), D_FF_2 ** -0.5),
        "norm_final": gain(ks[23], (D_MODEL,)),
    }

def second_block(x, meta_tokens, norm_mix, w_in, norm_q, w_q_up, norm_kv, w_kv_up, w_attn_proj,
              ssm_lambda_re, ssm_lambda_im, ssm_log_step, ssm_b_re, ssm_b_im, ssm_c_re, ssm_c_im,
              ssm_d, w_glu_val, w_glu_gate, w_out, norm_ffn, w_ffn_gate, w_ffn_up, w_ffn_down,
              norm_final):
    bsz = x.shape[0]
    meta = jnp.broadcast_to(meta_tokens[None].astype(x.dtype), (bsz, N_META, D_MODEL))
    h = jnp.concatenate([meta, x], axis=1)
    length = h.shape[1]
    cos, sin = rope_tables(length)
    for l in range(DEPTH):
        n = rms_norm_2(h, norm_mix[l])
        z = n @ w_in[l]
        q_lat, kv_lat, k_r, u, gates = jnp.split(z, [OFF_Q, OFF_KV, OFF_KR, OFF_U], axis=-1)
        q = (rms_norm_2(q_lat, norm_q[l]) @ w_q_up[l]).reshape(bsz, length, MLA_HEADS, QK_NOPE + QK_ROPE)
        kv = (rms_norm_2(kv_lat, norm_kv[l]) @ w_kv_up[l]).reshape(bsz, length, MLA_HEADS, QK_NOPE + V_HEAD)
        q_nope = q[..., :QK_NOPE]
        q_rope = apply_rope(q[..., QK_NOPE:], cos[:, None, :], sin[:, None, :])
        k_nope, v = kv[..., :QK_NOPE], kv[..., QK_NOPE:]
        k_rope = apply_rope(k_r, cos, sin)
        attn = mla_attention(q_nope, q_rope, k_nope, k_rope, v).reshape(bsz, length, MLA_HEADS * V_HEAD)
        attn_out = attn @ w_attn_proj[l]
        y = s5_scan(u.reshape(bsz, length, SSM_GROUPS, SSM_GROUP),
                    ssm_lambda_re[l], ssm_lambda_im[l], ssm_log_step[l],
                    ssm_b_re[l], ssm_b_im[l], ssm_c_re[l], ssm_c_im[l], ssm_d[l])
        y = jax.nn.gelu(y.reshape(bsz, length, SSM_WIDTH).astype(h.dtype))
        ssm_out = (y @ w_glu_val[l]) * jax.nn.sigmoid(y @ w_glu_gate[l])
        g = gates.reshape(bsz, length, N_BRANCH_2, D_MODEL)
        mixed = jax.nn.sigmoid(g[:, :, 0]) * attn_out + jax.nn.sigmoid(g[:, :, 1]) * ssm_out
        h = h + mixed @ w_out[l]
        m = rms_norm_2(h, norm_ffn[l])
        h = h + (jax.nn.silu(m @ w_ffn_gate[l]) * (m @ w_ffn_up[l])) @ w_ffn_down[l]
    out = rms_norm_2(h, norm_final)
    return out[:, N_META:]


def setup_inputs(seed=0):
    out = dict(first_inputs(seed))
    for name, value in second_inputs(seed + 1).items():
        if name != "x":
            out[name + "_2"] = value
    return out


def reference(
    x, c, g_pre_mix, g_post_mix, g_pre_ffn, g_post_ffn, w_ada, b_ada, w_in, b_in, sgu_norm_g,
    sgu_w, sgu_b, pool_w, pool_scale, w_sgu_out, w_moba_out, w_pool_out, w_out, w_up, w_conv,
    b_conv, w_down, meta_tokens_2, norm_mix_2, w_in_2, norm_q_2, w_q_up_2, norm_kv_2, w_kv_up_2,
    w_attn_proj_2, ssm_lambda_re_2, ssm_lambda_im_2, ssm_log_step_2, ssm_b_re_2, ssm_b_im_2,
    ssm_c_re_2, ssm_c_im_2, ssm_d_2, w_glu_val_2, w_glu_gate_2, w_out_2, norm_ffn_2,
    w_ffn_gate_2, w_ffn_up_2, w_ffn_down_2, norm_final_2,
):
    x = first_block(
        x, c, g_pre_mix, g_post_mix, g_pre_ffn, g_post_ffn, w_ada, b_ada, w_in, b_in,
        sgu_norm_g, sgu_w, sgu_b, pool_w, pool_scale, w_sgu_out, w_moba_out, w_pool_out, w_out,
        w_up, w_conv, b_conv, w_down,
    )
    return second_block(
        x, meta_tokens_2, norm_mix_2, w_in_2, norm_q_2, w_q_up_2, norm_kv_2, w_kv_up_2,
        w_attn_proj_2, ssm_lambda_re_2, ssm_lambda_im_2, ssm_log_step_2, ssm_b_re_2, ssm_b_im_2,
        ssm_c_re_2, ssm_c_im_2, ssm_d_2, w_glu_val_2, w_glu_gate_2, w_out_2, norm_ffn_2,
        w_ffn_gate_2, w_ffn_up_2, w_ffn_down_2, norm_final_2,
    )


_drawn_inputs = setup_inputs


def setup_inputs(seed=0):
    import zlib

    import numpy as np

    out = dict(_drawn_inputs(seed))
    spreads = {}
    factors = {'meta_tokens_2': 8.0,
     'norm_mix_2': 8.0,
     'w_in_2': 4.114,
     'norm_q_2': 8.0,
     'w_q_up_2': 8.0,
     'norm_kv_2': 8.0,
     'w_kv_up_2': 7.282,
     'w_attn_proj_2': 7.275,
     'ssm_lambda_re_2': 64.0,
     'ssm_lambda_im_2': 64.0,
     'ssm_log_step_2': 64.0,
     'ssm_b_re_2': 64.0,
     'ssm_b_im_2': 64.0,
     'ssm_c_re_2': 64.0,
     'ssm_c_im_2': 64.0,
     'ssm_d_2': 5.05,
     'w_glu_val_2': 4.436,
     'w_glu_gate_2': 8.0,
     'w_out_2': 3.797,
     'norm_ffn_2': 64.0,
     'norm_final_2': 7.662}
    for name, (base, spread) in spreads.items():
        noise = np.random.default_rng([zlib.crc32(name.encode()), seed]).standard_normal(out[name].shape)
        drawn = base * np.exp(spread * noise) if base else spread * noise
        out[name] = __import__('jax').numpy.asarray(drawn.astype(out[name].dtype))
    for name, factor in factors.items():
        out[name] = (out[name] * factor).astype(out[name].dtype)
    return out
```

```python
from contextlib import ExitStack, contextmanager

import numpy as np
import concourse.bass as bass
from concourse import mybir

F32 = mybir.dt.float32
F32R = mybir.dt.float32r
ALU = mybir.AluOpType
ACT = mybir.ActivationFunctionType
AX = mybir.AxisListType

P = 128
D = 2048
KD = D // P
S = 256
TT = S // P
META = 16
L = S + META
C = 512
GK = 4
BW = 512
NMOD = 6
FF = 5632
KF = FF // P
FC = FF // 256
EPS = 1e-6
HEADS1, DH1 = 8, 64
HEADS2, NOPE, ROPE = 16, 128, 64
SCALE1 = DH1 ** -0.5
SCALE2 = (NOPE + ROPE) ** -0.5
LAT = 512
SSM = 1024
KS = SSM // P
NST = 32
TQ, TP = 17, 16
NEG = -1.0e30
TWO_PI = float(2 * np.pi)
CH_GATES2 = 18 + 12 + 4 + FC + 4 + 4
DOWN_TILES = [4] * 8 + [3] * 4

G_IN1, G_MERGE, G_OUT1, G_UP, G_DOWN = 72, 12, 16, 88, 48
G_IN2, G_HEADS, G_PROJ, G_GLU, G_OUT2 = 48, 16, 16, 16, 16
N_GROUPS = G_IN1 + G_MERGE + G_OUT1 + G_UP + G_DOWN + G_IN2 + G_HEADS + G_PROJ + G_GLU + G_OUT2 + G_UP + G_DOWN
G_BEFORE_HEADS = G_IN1 + G_MERGE + G_OUT1 + G_UP + G_DOWN + G_IN2
BLK_ROUND = 8 + 2 + 2 + 4 * 5 + 2 + 8 + 8 + KD + 7 + 2
N_ADA = NMOD * D // C * (KD // GK)


class Tally:

    def __init__(self):
        self.base, self.k, self.i, self.per = 0, 0, None, 0

    @property
    def n(self):
        if self.i is None:
            return self.base + self.k
        return self.i * self.per + (self.base + self.k)

    @property
    def slot(self):
        return self.base + self.k

    def on_bank(self, b):
        if self.i is None:
            return (self.base + self.k + 1 - b) // 2
        return self.i * (self.per // 2) + (self.base + self.k + 1 - b) // 2

    def early(self, n):
        return self.i is None and self.base + self.k < n

    def add(self, n=1):
        self.k += n


@contextmanager
def engine_loop(eng, times, *tallies):
    with eng.Fori(0, times) as i:
        for t, per in tallies:
            t.base, t.k, t.i, t.per = t.base + t.k, 0, i, per
        yield i
        for t, per in tallies:
            assert t.k == per, [(a.k, b) for a, b in tallies]
    for t, per in tallies:
        t.base, t.k, t.i = t.base + per * times, 0, None


class Chain:

    def __init__(self, eng, sem):
        self.eng, self.sem, self.t = eng, sem, Tally()

    def __call__(self, ins):
        ins.then_inc(self.sem, 1)
        self.t.add()
        self.eng.wait_ge(self.sem, self.t.n)


def block_program(nc, a, out):
    with ExitStack() as ctx:
        base = (nc.sbuf_base + 63) // 64 * 64
        K = 1024

        def at(name, shape, kb, dt=F32):
            size = int(np.prod(shape[1:])) * 4
            assert base + kb * K + size <= nc.sbuf_usable_end, (name, kb)
            return nc.alloc_sbuf_tensor_at(name, shape, dt, offset=base + int(kb * K))

        sems = {}

        def sem(name):
            if name not in sems:
                sems[name] = ctx.enter_context(nc.semaphore(name))
            return sems[name]

        raw = at("w_raw", [P, 4, GK, C], 0)
        whi = at("w_hi", [P, 2, GK, C], 32, F32R)
        wlo = at("w_lo", [P, 2, GK, C], 48, F32R)
        x = at("x_res", [P, TT, D], 64)
        pos = [80.0]

        def small(name, shape, dt=F32):
            t = at(name, shape, pos[0], dt)
            pos[0] += (int(np.prod(shape[1:])) * 4 + 31) // 32 * 32 / K
            return t

        ident = small("ident", [P, P])
        brow = small("bias_rows", [P, 2, C])
        wconv = small("conv_taps", [P, FC, 4, 4])
        rope = small("rope_tab", [P, 2, 3, 32])
        cond = small("cond", [P, KD])
        ssq = small("sumsq", [P, 8])
        rstd = small("rstd", [P, 8])
        mhalf = small("minus_half", [P, 8])
        sgub = small("sgu_b", [P, 8])
        pscale = small("pool_scale", [P, 4])
        nmax = small("neg_max", [P, 2])
        rsum = small("row_sum", [P, 2])
        rinv = small("row_inv", [P, 2])
        ssmd = small("ssm_d", [P, KS])
        bmask = small("ssm_bmask", [P, 2])
        cmask = small("ssm_cmask", [P, 2])
        tril = small("tril", [P, P])
        U = 87.75
        assert pos[0] <= U, pos

        def u(name, shape, kb, dt=F32):
            return at(name, shape, U + kb, dt)

        modrow = u("mod_row", [1, NMOD * D], 0)
        badarow = u("b_ada_row", [1, NMOD * D], 48)
        h1T = [u("h1T_hi", [P, KD, S], 0, F32R), u("h1T_lo", [P, KD, S], 16, F32R)]
        pg = u("proj", [P, 18, TT, C], 32)
        h1 = u("h1", [P, TT, D], 56)
        rowA1, rowB1, rowT1 = u("rowA1", [P, D], 72), u("rowB1", [P, D], 80), u("rowT1", [P, D], 88)
        y3T = [u("y3T_hi", [P, 3, 4, S], 0, F32R), u("y3T_lo", [P, 3, 4, S], 12, F32R)]
        wsT = u("sgu_wT", [P, 8, P], 24)
        wsn = u("sgu_w", [P, 8, P], 28)
        qkT = u("qkT", [P, 2, 4, P], 28)
        poolm = u("pool_m", [P, 4, TT, S], 104)
        dist = u("alibi_dist", [P, TT, S], 112)
        poolw = u("pool_w", [P, 4, P], 114)
        sgug = u("sgu_g", [P, BW], 116)
        sc1 = u("scores1", [P, 2, S], 116)
        pT1 = u("probsT1", [P, 2, S], 118)
        pooledT = u("pooledT", [P, 4, S], 32)
        yp = u("pool_y", [P, 4, S], 24)
        merged = u("merged", [P, TT, D], 32)
        mgT = [u("mgT_hi", [P, KD, S], 56, F32R), u("mgT_lo", [P, KD, S], 72, F32R)]
        mtmp = u("merge_tmp", [P, TT, C], 48)
        y1 = u("y1", [P, TT, D], 88)
        rowA2, rowB2 = u("rowA2", [P, D], 104), u("rowB2", [P, D], 112)
        rowC2 = u("rowC2", [P, D], 56)
        h2T = [u("h2T_hi", [P, KD, S], 0, F32R), u("h2T_lo", [P, KD, S], 16, F32R)]
        hid = [u("hid_hi", [P, KF, S], 32, F32R), u("hid_lo", [P, KF, S], 76, F32R)]
        y2 = u("y2", [P, TT, D], 0)
        rowA3, rowB3 = u("rowA3", [P, D], 16), u("rowB3", [P, D], 24)
        n2 = u("n2", [P, TT, D], 0)
        nmeta = u("n_meta", [META, D], 24)
        sqmeta = u("sq_meta", [META, D], 104)
        nT = [u("nT_hi", [P, KD, L], 32, F32R), u("nT_lo", [P, KD, L], 49, F32R)]
        gates2 = u("gates2", [P, TT, 2 * D], 66)
        qlat = u("q_lat", [P, TT, LAT], 0)
        kvlat = u("kv_lat", [P, 3, LAT], 4)
        krn = u("k_rope", [P, 3, 2, ROPE], 10)
        krw = u("kr_w", [P, KD, ROPE], 12)
        krwh = u("kr_w_hi", [P, KD, ROPE], 16, F32R)
        krwl = u("kr_w_lo", [P, KD, ROPE], 20, F32R)
        grow2 = u("g_rows2", [P, 2, LAT], 25)
        ropet = u("rope_tmp", [P, 4, 4, 32], 29)
        qlT = [u("qlT_hi", [P, 4, S], 98, F32R), u("qlT_lo", [P, 4, S], 102, F32R)]
        kvT = [u("kvT_hi", [P, 4, L], 106, F32R), u("kvT_lo", [P, 4, L], 110.25, F32R)]
        krT = u("krT", [P, L], 114.5)
        mask2 = u("mask2", [P, TT, L], 115.5625)
        latsq = u("lat_sq", [P, LAT], 117.75)
        uT = u("uT", [P, KS, L], 12.5)
        X0 = 64 - U
        Qt = u("phase_q", [P, 2, NST, TQ], X0)
        Pt = u("phase_p", [P, 2, NST, TP], X0 + 4.25)
        bb = u("bb", [P, 2, NST, 16], X0 + 8.25)
        scol = u("ssm_cols", [P, 12, NST], X0 + 12.25)
        bcT = u("ssm_bcT", [P, 4, P], X0 + 13.75)
        cnat = u("ssm_c", [P, 2, KS, 64], 21)
        braw = u("ssm_b", [P, 2, NST, 16], 0)
        btmp = u("ssm_bt", [P, 2, NST, 16], 4)
        ptmp = u("phase_tmp2", [P, 2, NST, 8], 8)
        ys = u("ys", [P, KS, S], 0)
        Wt = [u("phase_a", [P, 2, L], 8), u("phase_b", [P, 2, L], 10.125)]
        vv = u("ssm_v", [P, 2, L], 25)
        zz = u("ssm_z", [P, 2, L], 27.125)
        xx = u("ssm_x", [P, 2, L], 29.25)
        blk = u("ssm_blk", [P, 4, P], 117.75)
        wtmp = u("phase_tmp", [P, L], 64.5)
        ysT = [u("ysT_hi", [P, KS, S], 32, F32R), u("ysT_lo", [P, KS, S], 40, F32R)]
        att2 = u("att2", [P, TT, D], 32)
        qnT = u("qnT", [P, 2, S], 48)
        qrn = u("q_rope", [P, TT, 2, ROPE], 50)
        qrT = u("qrT", [P, S], 51)
        knT = u("knT", [P, 2, L], 52)
        vn2 = u("v2", [P, 3, 2 * NOPE], 54.25)
        sc2 = u("scores2", [P, 2, L], 57.25)
        pT2 = u("probsT2", [P, 2, 3 * P], 59.5)
        qrt = u("q_rope_tmp", [P, 4, 4, 32], 62.5)
        attT = [u("attT_hi", [P, KD, S], 98, F32R), u("attT_lo", [P, KD, S], 8, F32R)]
        mix2 = u("mix2", [P, TT, D], 48)
        gtmp = u("glu_tmp", [P, 2, TT, C], 24)
        mxT = [u("mxT_hi", [P, KD, S], 66, F32R), u("mxT_lo", [P, KD, S], 82, F32R)]
        m2 = u("m2", [P, TT, D], 98)
        rowM = u("rowM", [P, D], 48)
        junk2 = u("junk2", [P, D], 64)
        junk3 = u("junk3", [P, D], 32)
        fin = u("fin", [P, TT, D], 0)
        rowF = u("rowF", [P, D], 16)

        acc = [ctx.enter_context(nc.psum_tensor(f"acc{i}", [P, 2, C], F32)) for i in range(2)]
        tp = [ctx.enter_context(nc.psum_tensor(f"tp{i}", [P, C], F32)) for i in range(2)]
        ms = [ctx.enter_context(nc.psum_tensor(f"ms{i}", [P, C], F32)) for i in range(2)]

        block = ctx.enter_context(nc.Block())

        raw_in = [sem(f"raw_in{i}") for i in range(4)]
        ada_used, hi_made, lo_made, pe_used = sem("ada_used"), sem("hi_made"), sem("lo_made"), sem("pe_used")
        acc_free = sem("acc_free")
        tp_full, tp_hi = sem("tp_full"), sem("tp_hi")
        tp_free = [sem("tp_free0"), sem("tp_free1")]
        score_banks = [acc[0][:, 0], acc[0][:, 1], acc[1][:, 0], acc[1][:, 1]]
        vt = brow[:].rearrange("p a b -> p (a b)")[:, 0:2 * L].rearrange("p (r l) -> p r l", r=2)
        uj = brow[:].rearrange("p a b -> p (a b)")[:, 2 * L:3 * L]
        zc = brow[:].rearrange("p a b -> p (a b)").rearrange("p (f s) -> p f s", f=4)

        def cols(t, n, w=C):
            return t[:, :, n * w:(n + 1) * w]

        def bank(n):
            return acc[n % 2]

        @block.sync
        def _(sp):
            def load(slot, src):
                sp.dma_start(raw[:, slot].rearrange("p k c -> p (k c)"), src).then_inc(raw_in[slot], 16)

            def row(t, g):
                return t[bass.ds(g, 1)].rearrange("g p n -> (g p) n")

            for j in range(4):
                load(j, a["ada_stream"][j])
            with sp.Fori(1, N_ADA // 4) as i:
                for j in range(4):
                    sp.wait_ge(ada_used, (i - 1) * 4 + j + 1)
                    load(j, row(a["ada_stream"], i * 4 + j))
            for j in range(4):
                sp.wait_ge(ada_used, N_ADA - 3 + j)
                load(j, a["w_stream"][j])
            with sp.Fori(1, N_GROUPS // 4) as i:
                for j in range(4):
                    sp.wait_ge(lo_made, (i - 1) * 4 + j + 1)
                    load(j, row(a["w_stream"], i * 4 + j))
            sp.wait_ge(sem("fin"), 1)
            sp.dma_start(out.rearrange("o (t p) d -> p (o t) d", p=P), fin[:]).then_inc(sem("out"), 16)
            sp.wait_ge(sem("out"), 16)

        @block.gpsimd
        def _(pool):
            chain = Chain(pool, sem("pool_chain"))
            norms = Tally()
            g = nc.gpsimd

            def fetch(name, dst, src):
                pool.dma_start(dst, src).then_inc(sem("ld_" + name), 16)

            def bc(row):
                return row.partition_broadcast(P)

            def rsqrt_mean(width, parts):
                pool.wait_ge(sem("ssq"), norms.n + 1)
                norms.add()
                for np_, c0, c1 in parts:
                    chain(g.tensor_scalar(rstd[:np_, c0:c1], ssq[:np_, c0:c1], 1.0 / width, EPS, ALU.mult, ALU.add))
                    ins = g.tensor_tensor(rstd[:np_, c0:c1], rstd[:np_, c0:c1], mhalf[:np_, c0:c1], ALU.pow)
                    chain(ins)
                pool.sem_inc(sem("rstd"), 1)

            chain(g.memset(mhalf[:], -0.5))
            fetch("cond", cond[:], a["c"])
            fetch("bada", badarow[:], a["b_ada"])
            fetch("ident", ident[:], a["ident"])
            fetch("x", x[:], a["x"].rearrange("(t p) d -> p t d", p=P))
            fetch("wconv", wconv[:], a["conv"])
            fetch("small", sgub[:], a["sgu_b"])
            fetch("small", pscale[:], a["pool_scale"])
            fetch("small", rope[:], a["rope"])
            fetch("small", ssmd[:], a["ssm_d"])
            fetch("small", bmask[:], a["bmask"])
            fetch("small", cmask[:], a["cmask"])
            fetch("tril", tril[:], a["tril"])
            fetch("c1", poolm[:], a["pool_m"])
            fetch("c1", dist[:], a["dist"])
            fetch("c1", poolw[:], a["pool_w"])
            fetch("c1", sgug[:], bc(a["sgu_g"]))
            pool.wait_ge(sem("mod_evac"), NMOD * D // C)
            pool.dma_start(a["mod_dram"], modrow[:]).then_inc(sem("mod_saved"), 16)
            pool.wait_ge(sem("mod_saved"), 16)
            mod = [a["mod_dram"][0, i * D:(i + 1) * D] for i in range(NMOD)]
            fetch("rows1", rowA1[:], bc(mod[1]))
            fetch("rows1", rowB1[:], bc(mod[0]))
            fetch("rows1", rowT1[:], bc(a["g_pre_mix"]))
            rsqrt_mean(D, [(P, 0, 2)])
            for j in range(2):
                fetch(f"brow{j}", brow[:, j], bc(a["b_in"][0, j * C:(j + 1) * C]))
            with pool.Fori(1, 9) as i:
                for j in range(2):
                    pool.wait_ge(acc_free, i * 2 + j - 1)
                    fetch(f"brow{j}", brow[:, j], bc(a["b_in"][0, bass.ds(i * 2 * C + j * C, C)]))
            pool.wait_ge(pe_used, G_IN1)
            fetch("sguw", wsn[:], a["sgu_w"])
            pool.wait_ge(sem("ld_sguw"), 16)
            pool.wait_ge(sem("ld_tril"), 16)
            chain(g.tensor_tensor(wsn[:], wsn[:], tril[:].unsqueeze(1).to_broadcast([P, 8, P]), ALU.mult))
            pool.sem_inc(sem("sguw_m"), 1)
            rsqrt_mean(BW, [(P, 0, 2)])
            pool.wait_ge(sem("mix_in"), 1)
            fetch("rows2", rowA2[:], bc(mod[2]))
            fetch("rows2", rowB2[:], bc(a["g_post_mix"]))
            rsqrt_mean(D, [(P, 0, 2)])
            pool.wait_ge(sem("x1"), 1)
            fetch("rows3", rowA2[:], bc(mod[4]))
            fetch("rows3", rowB2[:], bc(a["g_pre_ffn"]))
            fetch("rows3", rowC2[:], bc(mod[3]))
            rsqrt_mean(D, [(P, 0, 2)])
            pool.wait_ge(pe_used, G_IN1 + G_MERGE + G_OUT1 + G_UP)
            fetch("rows4", rowA3[:], bc(mod[5]))
            fetch("rows4", rowB3[:], bc(a["g_post_ffn"]))
            rsqrt_mean(D, [(P, 0, 2)])
            pool.wait_ge(sem("x2"), 1)
            fetch("rows5", rowA3[:], bc(a["norm_mix"]))
            fetch("rows5", nmeta[:], a["meta"])
            pool.dma_start(a["x_dram"], x[:]).then_inc(sem("x_saved"), 16)
            rsqrt_mean(D, [(P, 0, 2), (META, 2, 3)])
            pool.wait_ge(sem("nT"), 1)
            fetch("kr", krw[:], a["w_kr"])
            fetch("kr", grow2[:, 0], bc(a["norm_q"]))
            fetch("kr", grow2[:, 1], bc(a["norm_kv"]))
            pool.wait_ge(sem("x_saved"), 16)
            for j, name in enumerate(("lam_re", "lam_im", "log_step")):
                fetch("ssm", scol[:, j], a[name])
            rsqrt_mean(LAT, [(P, 0, 2)])
            rsqrt_mean(LAT, [(P, 3, 5), (META, 5, 6)])
            fetch("mask2", mask2[:], a["mask2"])
            pool.wait_ge(sem("latT"), 1)
            fetch("ssm_w", braw[:, 0], a["ssm_b_re"])
            fetch("ssm_w", braw[:, 1], a["ssm_b_im"])
            fetch("ssm_w", cnat[:, 0], a["ssm_c_re"])
            fetch("ssm_w", cnat[:, 1], a["ssm_c_im"])
            lr, li, mag, sn, cs = (scol[:, j] for j in (0, 1, 4, 7, 8))
            t5, t6, t9, t10, t11 = (scol[:, j] for j in (5, 6, 9, 10, 11))
            tt, ts = g.tensor_tensor, g.tensor_scalar
            pool.wait_ge(sem("trig"), 2)
            chain(g.memset(t6, -1.0))
            chain(tt(t9, lr, lr, ALU.mult))
            chain(tt(t10, li, li, ALU.mult))
            chain(tt(t9, t9, t10, ALU.add))
            chain(tt(t9, t9, t6, ALU.pow))
            chain(tt(t10, mag, cs, ALU.mult))
            chain(ts(t10, t10, 1.0, None, ALU.subtract))
            chain(tt(t11, mag, sn, ALU.mult))
            chain(tt(t5, t10, lr, ALU.mult))
            chain(tt(t6, t11, li, ALU.mult))
            chain(tt(t5, t5, t6, ALU.add))
            chain(tt(t5, t5, t9, ALU.mult))
            chain(tt(t6, t11, lr, ALU.mult))
            chain(tt(t10, t10, li, ALU.mult))
            chain(tt(t6, t6, t10, ALU.subtract))
            chain(tt(t6, t6, t9, ALU.mult))
            pool.wait_ge(sem("ld_ssm_w"), 64)
            cre, cim = (c.unsqueeze(2).to_broadcast([P, NST, 16]) for c in (t5, t6))
            chain(tt(bb[:, 0], cre, braw[:, 0], ALU.mult))
            chain(tt(btmp[:, 0], cim, braw[:, 1], ALU.mult))
            chain(tt(bb[:, 0], bb[:, 0], btmp[:, 0], ALU.subtract))
            chain(tt(bb[:, 1], cre, braw[:, 1], ALU.mult))
            chain(tt(btmp[:, 1], cim, braw[:, 0], ALU.mult))
            chain(tt(bb[:, 1], bb[:, 1], btmp[:, 1], ALU.add))
            chain(ts(cnat[:, 1], cnat[:, 1], -1.0, None, ALU.mult))

            def cmul(dst, u_, v_, t):
                tt(t, u_[1], v_[1], ALU.mult)
                chain(tt(dst[0], u_[0], v_[0], ALU.mult))
                chain(tt(dst[0], dst[0], t, ALU.subtract))
                tt(t, u_[0], v_[1], ALU.mult)
                chain(tt(dst[1], u_[1], v_[0], ALU.mult))
                chain(tt(dst[1], dst[1], t, ALU.add))

            def powers(tab, e):
                chain(g.memset(tab[:, 0, :, 0:1], 1.0))
                chain(g.memset(tab[:, 1, :, 0:1], 0.0))
                n = 1
                while n < 16:
                    wide = [c.unsqueeze(2).to_broadcast([P, NST, n]) for c in e]
                    cmul((tab[:, 0, :, n:2 * n], tab[:, 1, :, n:2 * n]), wide,
                         (tab[:, 0, :, 0:n], tab[:, 1, :, 0:n]), ptmp[:, 0, :, 0:n])
                    nxt = (ptmp[:, 1, :, 0], ptmp[:, 1, :, 1]) if n in (1, 4) else (ptmp[:, 1, :, 2], ptmp[:, 1, :, 3])
                    cmul(nxt, e, e, ptmp[:, 1, :, 4])
                    e, n = nxt, 2 * n
                return e

            e1 = (cs, sn)
            e16 = powers(Qt, e1)
            chain(g.tensor_copy(Qt[:, 0, :, 16], e16[0]))
            chain(g.tensor_copy(Qt[:, 1, :, 16], e16[1]))
            e17 = (ptmp[:, 1, :, 6], ptmp[:, 1, :, 7])
            cmul(e17, e16, e1, ptmp[:, 1, :, 5])
            powers(Pt, e17)

            def table(s):
                w = Wt[s % 2][:].rearrange("p r (c t) -> p r c t", t=TQ)
                pv = [Pt[:, r, s].unsqueeze(2).to_broadcast([P, TP, TQ]) for r in range(2)]
                qv = [Qt[:, r, s].unsqueeze(1).to_broadcast([P, TP, TQ]) for r in range(2)]
                cmul((w[:, 0], w[:, 1]), pv, qv, wtmp[:].rearrange("p (c t) -> p c t", t=TQ))
                pool.sem_inc(sem("w_made"), 1)

            pool.wait_ge(pe_used, G_BEFORE_HEADS)
            table(0)
            table(1)
            for j in range(KS):
                if j:
                    pool.wait_ge(tp_full, BLK_ROUND + 6 * (j - 1))
                for r in range(2):
                    chain(tt(blk[:, r].rearrange("p (q g c) -> p q g c", q=4, g=2),
                             bb[:, r, 4 * j:4 * j + 4].unsqueeze(2).to_broadcast([P, 4, 2, 16]),
                             bmask[:].unsqueeze(1).unsqueeze(3).to_broadcast([P, 4, 2, 16]), ALU.mult))
                    chain(tt(blk[:, 2 + r].rearrange("p (g c) -> p g c", g=2),
                             cnat[:, r, j].unsqueeze(1).to_broadcast([P, 2, 64]),
                             cmask[:].unsqueeze(2).to_broadcast([P, 2, 64]), ALU.mult))
                pool.sem_inc(sem("blk"), 1)
                for q in range(4):
                    s = 4 * j + q
                    pool.wait_ge(sem("z_made"), s + 1)
                    if s:
                        pool.wait_ge(sem("y_part"), s)
                    w = Wt[s % 2]
                    cmul((xx[:, 0], xx[:, 1]), (zz[:, 0], zz[:, 1]), (w[:, 0], w[:, 1]), wtmp[:])
                    pool.sem_inc(sem("xs"), 1)
                    if s + 2 < NST:
                        table(s + 2)
            pool.wait_ge(sem("ssm_done"), 1)
            fetch("xre", x[:], a["x_dram"])
            pool.wait_ge(sem("mixT"), 1)
            fetch("rowM", rowM[:], bc(a["norm_ffn"]))
            rsqrt_mean(D, [(P, 0, 2)])
            pool.wait_ge(pe_used, N_GROUPS - G_DOWN)
            fetch("rowF", rowF[:], bc(a["norm_final"]))
            rsqrt_mean(D, [(P, 0, 2)])

        @block.scalar
        def _(act):
            chain = Chain(act, sem("act_chain"))
            m, rounds, his = Tally(), Tally(), Tally()
            sc = nc.scalar

            def split():
                s = m.slot
                up = 0 if m.i is None else m.i * (m.per // 4)
                act.wait_ge(raw_in[s % 4], (up + (N_ADA + s) // 4 + 1) * 16)
                if not m.early(2):
                    act.wait_ge(pe_used, m.n - 1)
                sc.activation(whi[:, s % 2], raw[:, s % 4], ACT.Copy).then_inc(hi_made, 1)
                m.add()

            def turn_hi(dst, w=2 * S):
                act.wait_ge(tp_full, rounds.n + 1)
                sc.activation(dst, tp[rounds.slot % 2][:, 0:w], ACT.Copy).then_inc(tp_hi, 1)
                rounds.add()

            def turns_hi(dst, n):
                for k in range(n // 2):
                    turn_hi(dst[:, 2 * k:2 * k + 2, :].rearrange("p a b -> p (a b)"))

            def squares(src, junk, where, cs, more=False):
                for k, c in enumerate(cs):
                    ins = sc.activation(junk(k), src(k), ACT.Square, accum_out=ssq[:where, c:c + 1])
                    if k < len(cs) - 1 or more:
                        chain(ins)
                return ins

            act.wait_ge(sem("ld_cond"), 16)
            sc.activation(cond[:], cond[:], ACT.Silu).then_inc(sem("cond"), 1)
            act.wait_ge(sem("mod_saved"), 16)
            act.wait_ge(sem("ld_x"), 16)
            squares(lambda k: x[:, k], lambda k: h1[:, k], P, (0, 1)).then_inc(sem("ssq"), 1)
            split()
            split()
            turns_hi(h1T[0], KD)
            chunk = Tally()

            def in1(cn, func):
                for _ in range(4):
                    split()
                act.wait_ge(acc_free, chunk.n + 1)
                chunk.add()
                if func:
                    v = pg[:, bass.ds(cn, 1)].rearrange("p a t c -> p (a t c)")
                    sc.activation(v, v, func).then_inc(sem("p_act"), 1)

            in1(0, ACT.Gelu_apprx_tanh)
            in1(1, ACT.Gelu_apprx_tanh)
            with engine_loop(act, 2, (m, 8), (chunk, 2)) as i:
                for j in range(2):
                    in1(0, None)
            with engine_loop(act, 6, (m, 8), (chunk, 2)) as i:
                for j in range(2):
                    in1(i * 2 + 6 + j, ACT.Sigmoid)
            act.wait_ge(sem("v_cent"), 1)
            squares(lambda k: pg[:, 1, k], lambda k: pT1[:].rearrange("p a b -> p (a b)"), P, (0, 1)).then_inc(sem("ssq"), 1)
            rounds.add(2)
            for k in range(2):
                turn_hi(y3T[0][:, 0, 2 * k:2 * k + 2].rearrange("p a b -> p (a b)"))
            for k in range(4):
                act.wait_ge(sem("pool_y"), k + 1)
                chain(sc.activation(yp[:, k], ms[k % 2][:, S:2 * S], ACT.Copy, scale=pscale[:, k:k + 1]))
                sc.activation(y3T[0][:, 2, k], yp[:, k], ACT.Copy).then_inc(sem("yp_hi"), 1)

            units = Tally()

            def exps(sct, w):
                act.wait_ge(sem("max"), units.n + 1)
                s = units.slot % 2
                sc.activation(sct[:, s, 0:w], sct[:, s, 0:w], ACT.Exp, bias=nmax[:, s:s + 1],
                              accum_out=rsum[:, s:s + 1]).then_inc(sem("exp"), 1)
                units.add()

            for hp in range(4):
                rounds.add(1)
                for h in range(2):
                    for qt in range(2):
                        exps(sc1, (qt + 1) * P)
                        rounds.add(1)
            for k in range(2):
                turn_hi(y3T[0][:, 1, 2 * k:2 * k + 2].rearrange("p a b -> p (a b)"))
            for _ in range(G_MERGE):
                split()
            turns_hi(mgT[0], KD)
            with engine_loop(act, 2, (m, 8)) as i:
                for _ in range(8):
                    split()
            act.wait_ge(sem("y1"), 1)
            squares(lambda k: y1[:, k], lambda k: junk2[:], P, (0, 1)).then_inc(sem("ssq"), 1)
            act.wait_ge(sem("x1"), 1)
            squares(lambda k: x[:, k], lambda k: junk2[:], P, (0, 1)).then_inc(sem("ssq"), 1)
            turns_hi(h2T[0], KD)
            upc = Tally()
            act.wait_ge(sem("ld_wconv"), 16)

            def up1(c, last=False):
                act.wait_ge(pe_used, upc.n * 4 + (G_IN1 + G_MERGE + G_OUT1 + 4))
                if not upc.early(1):
                    act.wait_ge(sem("hid_lo"), upc.n)
                for f in range(4):
                    ins = sc.activation(zc[:, f], bank(upc.slot)[:].rearrange("p a (b s) -> p (a b) s", s=S)[:, f],
                                        ACT.Identity, scale=wconv[:, bass.ds(c, 1), f, 2:3].rearrange("p a b -> p (a b)"),
                                        bias=wconv[:, bass.ds(c, 1), f, 3:4].rearrange("p a b -> p (a b)"))
                ins.then_inc(sem("z_mid"), 1)
                if not last:
                    split()
                act.wait_ge(sem("z_conv"), upc.n + 1)
                sc.activation(zc[:, 0:2], zc[:, 0:2], ACT.Gelu_apprx_tanh).then_inc(sem("z_gelu"), 1)
                if not last:
                    split()
                act.wait_ge(sem("z_mul"), upc.n + 1)
                sc.activation(hid[0][:, bass.ds(c * 2, 2), :], zc[:, 0:2], ACT.Copy).then_inc(sem("hid_hi"), 1)
                if not last:
                    split()
                    split()
                upc.add()

            for _ in range(4):
                split()
            up1(0)
            up1(1)
            with engine_loop(act, FC // 2 - 2, (m, 8), (upc, 2)) as i:
                for j in range(2):
                    up1(i * 2 + 2 + j)
            up1(FC - 2)
            up1(FC - 1, True)
            with engine_loop(act, 2, (m, 24)) as i:
                for _ in range(24):
                    split()
            act.wait_ge(sem("y2"), 1)
            squares(lambda k: y2[:, k], lambda k: junk3[:], P, (0, 1)).then_inc(sem("ssq"), 1)
            act.wait_ge(sem("x2"), 1)
            squares(lambda k: x[:, k], lambda k: junk3[:], P, (0, 1), True)
            act.wait_ge(sem("ld_rows5"), 32)
            squares(lambda k: nmeta[:], lambda k: sqmeta[:], META, (2,)).then_inc(sem("ssq"), 1)
            for k in range(KD):
                turn_hi(nT[0][:, k], L)
            act.wait_ge(sem("ld_kr"), 48)
            sc.activation(krwh[:], krw[:], ACT.Copy).then_inc(sem("krw_hi"), 1)
            for _ in range(8):
                split()
            act.wait_ge(sem("lat"), 1)
            squares(lambda k: qlat[:, k], lambda k: latsq[:], P, (0, 1)).then_inc(sem("ssq"), 1)
            act.wait_ge(sem("lat"), 2)
            act.wait_ge(sem("ssq"), 7)
            squares(lambda k: kvlat[:, k], lambda k: latsq[:], P, (3, 4), True)
            squares(lambda k: kvlat[:META, 2], lambda k: latsq[:META, :], META, (5,)).then_inc(sem("ssq"), 1)
            for _ in range(8):
                split()
            rounds.add(1)
            for k in range(2):
                turn_hi(qlT[0][:, 2 * k:2 * k + 2].rearrange("p a b -> p (a b)"))
            for k in range(4):
                turn_hi(kvT[0][:, k], L)
            act.wait_ge(sem("phase"), 1)
            sc.activation(scol[:, 7], scol[:, 7], ACT.Sin).then_inc(sem("trig"), 1)
            sc.activation(scol[:, 8], scol[:, 8], ACT.Sin).then_inc(sem("trig"), 1)
            gate = Tally()

            def gates(n):
                for _ in range(4):
                    split()
                act.wait_ge(acc_free, gate.n + CH_GATES2 + 1)
                v = gates2[:, :, bass.ds(n * C, C)]
                sc.activation(v, v, ACT.Sigmoid).then_inc(sem("g_act"), 1)
                gate.add()

            with engine_loop(act, 4, (m, 8), (gate, 2)) as i:
                for j in range(2):
                    gates(i * 2 + j)

            def turn_copy(parts):
                act.wait_ge(tp_full, rounds.n + 1)
                t = tp[rounds.slot % 2]
                for dst, np_, c0, c1 in parts:
                    ins = sc.activation(dst, t[:np_, c0:c1], ACT.Copy)
                ins.then_inc(tp_free[rounds.slot % 2], 1)
                rounds.add()

            def head_pair():
                split()
                split()
                act.wait_ge(pe_used, m.n - 2)
                sc.activation(qnT[:].rearrange("p h s -> p (h s)"), acc[0][:, 0], ACT.Copy)
                sc.activation(vn2[:, 0:2], ms[0][:].rearrange("p (t d) -> p t d", t=2), ACT.Copy).then_inc(sem("qnT"), 1)
                turn_copy([(qrT[:], P, 0, S)])
                turn_copy([(bcT[:].rearrange("p a b -> p (a b)"), P, 0, C)])
                exps(sc2, META + P)
                for n in range(4):
                    w = (n % 2 + 1) * P
                    s = n % 2
                    turn_copy([(pT2[:, s, 0:w], P, 0, w), (pT2[:META, s, 2 * P:3 * P], META, 2 * P, 3 * P)])
                    if n < 3:
                        exps(sc2, META + ((n + 1) % 2 + 1) * P)

            with engine_loop(act, 4, (m, 4), (units, 8), (rounds, 12)) as i:
                for j in range(2):
                    head_pair()
            turns_hi(attT[0], KD)
            act.wait_ge(sem("att_turned"), 1)
            chain(sc.activation(ys[:], ys[:], ACT.Gelu_apprx_tanh))
            sc.activation(ysT[0][:], ys[:], ACT.Copy).then_inc(sem("ys_hi"), 1)
            with engine_loop(act, 2, (m, 8)) as i:
                for _ in range(8):
                    split()
            glu = Tally()
            with engine_loop(act, 2, (m, 8), (glu, 2)) as i:
                for j in range(2):
                    for _ in range(4):
                        split()
                    act.wait_ge(pe_used, m.n - 2)
                    sc.activation(gtmp[:, j], bank(1)[:], ACT.Sigmoid).then_inc(sem("glu_sig"), 1)
                    glu.add()
            turns_hi(mxT[0], KD)
            with engine_loop(act, 2, (m, 8)) as i:
                for _ in range(8):
                    split()
            act.wait_ge(sem("x3"), 1)
            squares(lambda k: x[:, k], lambda k: m2[:, k], P, (0, 1)).then_inc(sem("ssq"), 1)
            turns_hi(h2T[0], KD)
            up2c = Tally()

            def up2(c):
                for _ in range(4):
                    split()
                act.wait_ge(pe_used, m.n - 2)
                act.wait_ge(sem("hid_lo"), up2c.n + FC)
                sc.activation(zc[:, 0:2], bank(up2c.slot)[:, 0].rearrange("p (f s) -> p f s", s=S),
                              ACT.Silu).then_inc(sem("z_silu"), 1)
                act.wait_ge(sem("z_mul"), up2c.n + FC + 1)
                sc.activation(hid[0][:, bass.ds(c * 2, 2), :], zc[:, 0:2], ACT.Copy).then_inc(sem("hid_hi"), 1)
                up2c.add()

            with engine_loop(act, FC // 2, (m, 8), (up2c, 2)) as i:
                for j in range(2):
                    up2(i * 2 + j)
            with engine_loop(act, 1, (m, 24)) as i:
                for _ in range(24):
                    split()
            for _ in range(22):
                split()
            act.wait_ge(sem("x4"), 1)
            squares(lambda k: x[:, k], lambda k: fin[:, k], P, (0, 1)).then_inc(sem("ssq"), 1)

        @block.vector
        def _(dve):
            chain = Chain(dve, sem("dve_chain"))
            m, chunks, rounds, los, norms = Tally(), Tally(), Tally(), Tally(), Tally()
            v = nc.vector

            def split():
                s = m.slot
                dve.wait_ge(hi_made, m.n + 1)
                v.tensor_tensor(wlo[:, s % 2], raw[:, s % 4], whi[:, s % 2].bitcast(F32), ALU.subtract).then_inc(lo_made, 1)
                m.add()

            def finish(n=4):
                for _ in range(n):
                    split()
                dve.wait_ge(pe_used, m.n - 2)
                b = bank(chunks.slot)
                chunks.add()
                return b

            def turn_lo(lo, hi, w=2 * S):
                dve.wait_ge(tp_hi, los.n + 1)
                v.tensor_tensor(lo, tp[rounds.slot % 2][:, 0:w], hi.bitcast(F32), ALU.subtract).then_inc(tp_free[rounds.slot % 2], 1)
                los.add()
                rounds.add()

            def turns_lo(dst, n):
                for k in range(n // 2):
                    lo, hi = (d[:, 2 * k:2 * k + 2, :].rearrange("p a b -> p (a b)") for d in (dst[1], dst[0]))
                    turn_lo(lo, hi)

            def turn_copy(parts):
                dve.wait_ge(tp_full, rounds.n + 1)
                t = tp[rounds.slot % 2]
                for dst, np_, c0, c1 in parts:
                    ins = v.tensor_copy(dst, t[:np_, c0:c1])
                ins.then_inc(tp_free[rounds.slot % 2], 1)
                rounds.add()

            def turned():
                for b in range(2):
                    dve.wait_ge(tp_free[b], rounds.on_bank(b))

            def rstd_wait():
                dve.wait_ge(sem("rstd"), norms.n + 1)
                norms.add()

            def scaled(dst, src, c, row, np_=P):
                return v.scalar_tensor_tensor(dst, src, rstd[:np_, c:c + 1], row, ALU.mult, ALU.mult)

            dve.wait_ge(sem("ld_bada"), 16)
            modc = Tally()

            def mod(c):
                for j in range(2):
                    dve.wait_ge(ada_used, (modc.n + 1) * 4)
                    o = modrow[:, bass.ds((c + j) * C, C)]
                    v.tensor_tensor(o, ms[j][0:1, :], badarow[:, bass.ds((c + j) * C, C)], ALU.add).then_inc(sem("mod_evac"), 1)
                    modc.add()

            with engine_loop(dve, 12, (modc, 2)) as i:
                mod(i * 2)
            dve.wait_ge(sem("ld_rows1"), 48)
            chain(v.scalar_tensor_tensor(rowA1[:], rowA1[:], 1.0, rowT1[:], ALU.add, ALU.mult))
            rstd_wait()
            for t in range(TT):
                chain(scaled(h1[:, t], x[:, t], t, rowA1[:]))
            for t in range(TT):
                v.tensor_tensor(h1[:, t], h1[:, t], rowB1[:], ALU.add).then_inc(sem("h1"), 1)
            split()
            split()
            turns_lo(h1T, KD)

            def in1(turn, j):
                cn = turn * 2 + j
                b = finish()
                dve.wait_ge(sem(f"ld_brow{j}"), (turn + 1) * 16)
                o = pg[:, bass.ds(cn, 1)].rearrange("p a t c -> p (a t) c")
                ins = v.tensor_tensor(o, b[:], brow[:, j:j + 1, :].to_broadcast([P, TT, C]), ALU.add)
                ins.then_inc(acc_free, 1)

            with engine_loop(dve, 9, (m, 8), (chunks, 2)) as i:
                for j in range(2):
                    in1(i, j)
            dve.wait_ge(sem("ld_c1"), 64)
            dve.wait_ge(sem("ld_small"), 96)
            dve.wait_ge(sem("p_act"), 2)
            for t in range(TT):
                chain(v.reduce_sum(ssq[:, 6 + t:7 + t], pg[:, 1, t], AX.X))
                chain(v.tensor_scalar(ssq[:, 6 + t:7 + t], ssq[:, 6 + t:7 + t], 1.0 / BW, None, ALU.mult))
                ins = v.tensor_scalar(pg[:, 1, t], pg[:, 1, t], ssq[:, 6 + t:7 + t], None, ALU.subtract)
                chain(ins)
            dve.sem_inc(sem("v_cent"), 1)
            for r in range(2):
                turn_copy([(wsT[:, 4 * r:4 * r + 4].rearrange("p a b -> p (a b)"), P, 0, C)])
            rstd_wait()
            for t in range(TT):
                ins = scaled(pg[:, 1, t], pg[:, 1, t], t, sgug[:])
                chain(ins)
            dve.sem_inc(sem("v_norm"), 1)
            for t in range(TT):
                dve.wait_ge(sem("sgu_mix"), t + 1)
                o = pg[:, 1, t].rearrange("p (g d) -> p g d", g=8)
                chain(v.tensor_tensor(o, ms[t][:].rearrange("p (g d) -> p g d", g=8),
                                      sgub[:].unsqueeze(2).to_broadcast([P, 8, 64]), ALU.add))
                chain(v.tensor_tensor(pg[:, 0, t], pg[:, 1, t], pg[:, 0, t], ALU.mult))
            dve.sem_inc(sem("y_sgu"), 1)
            for k in range(2):
                turn_lo(*(d[:, 0, 2 * k:2 * k + 2].rearrange("p a b -> p (a b)") for d in (y3T[1], y3T[0])))
            for k in range(4):
                dve.wait_ge(sem("pooled"), k + 1)
                v.tensor_copy(pooledT[:, k], ms[k % 2][:, 0:S]).then_inc(sem("pooledT"), 1)
            for k in range(4):
                dve.wait_ge(sem("yp_hi"), k + 1)
                v.tensor_tensor(y3T[1][:, 2, k], yp[:, k], y3T[0][:, 2, k].bitcast(F32), ALU.subtract).then_inc(sem("yp_lo"), 1)

            units = Tally()

            def softmax_in(sct, w, scale, bias, slope, bk=None):
                s = units.slot % 2
                dve.wait_ge(sem("sc_full"), units.n + 1)
                if bk is None:
                    bk = score_banks[units.slot % 4]
                if slope is None:
                    chain(v.scalar_tensor_tensor(sct[:, s, 0:w], bk[:, 0:w], scale, bias, ALU.mult, ALU.add))
                else:
                    chain(v.tensor_scalar(sct[:, s, 0:w], bk[:, 0:w], scale, None, ALU.mult))
                    chain(v.scalar_tensor_tensor(sct[:, s, 0:w], bias, slope, sct[:, s, 0:w], ALU.mult, ALU.add))
                chain(v.reduce_max(nmax[:, s:s + 1], sct[:, s, 0:w], AX.X))
                v.tensor_scalar(nmax[:, s:s + 1], nmax[:, s:s + 1], -1.0, None, ALU.mult).then_inc(sem("max"), 1)
                units.add()

            outs = Tally()

            def unit_out(parts, dst, src):
                s = outs.slot % 2
                if parts:
                    turn_copy(parts)
                else:
                    dve.wait_ge(sem("exp"), outs.n + 1)
                chain(v.reciprocal(rinv[:, s:s + 1], rsum[:, s:s + 1]))
                dve.wait_ge(sem("pv"), outs.n + 1)
                v.tensor_scalar(dst, src, rinv[:, s:s + 1], None, ALU.mult).then_inc(sem("o_free"), 1)
                outs.add()

            slopes = [2.0 ** (-(8.0 / HEADS1) * (h + 1)) for h in range(HEADS1)]
            for hp in range(4):
                turn_copy([(qkT[:, hp % 2].rearrange("p a b -> p (a b)"), P, 0, C)])

                def unit(n):
                    h, qt = divmod(n, 2)
                    w = (qt + 1) * P
                    softmax_in(sc1, w, SCALE1, dist[:, qt, 0:w], slopes[2 * hp + h])

                unit(0)
                for n in range(4):
                    h, qt = divmod(n, 2)
                    w = (qt + 1) * P
                    if n < 3:
                        unit(n + 1)
                    head = 2 * hp + h
                    unit_out([(pT1[:, outs.slot % 2, 0:w], P, 0, w)], pg[:, 1, qt, head * DH1:(head + 1) * DH1],
                             ms[outs.slot % 2][:, 0:DH1])
            for k in range(2):
                turn_lo(*(d[:, 1, 2 * k:2 * k + 2].rearrange("p a b -> p (a b)") for d in (y3T[1], y3T[0])))
            dve.sem_inc(sem("mix_in"), 1)
            dve.wait_ge(sem("p_act"), 14)
            for n in range(4):
                for br in range(3):
                    b = finish(1)
                    gt = pg[:, 6 + 4 * br + n]
                    o = cols(merged, n)
                    if br == 0:
                        chain(v.tensor_tensor(o, b[:], gt, ALU.mult))
                        dve.sem_inc(acc_free, 1)
                    else:
                        chain(v.tensor_tensor(mtmp[:], b[:], gt, ALU.mult))
                        dve.sem_inc(acc_free, 1)
                        chain(v.tensor_tensor(o, o, mtmp[:], ALU.add))
            dve.sem_inc(sem("merged"), 1)
            turns_lo(mgT, KD)

            def copy_out(dst, turns):
                with engine_loop(dve, turns, (m, 8), (chunks, 2)) as i:
                    for j in range(2):
                        b = finish()
                        v.tensor_copy(dst[:, :, bass.ds((i * 2 + j) * C, C)], b[:]).then_inc(acc_free, 1)
                dve.wait_ge(acc_free, chunks.n)

            copy_out(y1, 2)
            dve.sem_inc(sem("y1"), 1)

            def post(y, ra, rb, rows):
                dve.wait_ge(sem(rows), 32)
                chain(v.tensor_tensor(ra[:], ra[:], rb[:], ALU.mult))
                rstd_wait()
                for t in range(TT):
                    chain(scaled(y[:, t], y[:, t], t, ra[:]))
                chain(v.tensor_tensor(x[:], x[:], y[:], ALU.add))

            post(y1, rowA2, rowB2, "ld_rows2")
            dve.sem_inc(sem("x1"), 1)
            dve.wait_ge(sem("ld_rows3"), 48)
            chain(v.scalar_tensor_tensor(rowA2[:], rowA2[:], 1.0, rowB2[:], ALU.add, ALU.mult))
            rstd_wait()
            for t in range(TT):
                chain(scaled(y1[:, t], x[:, t], t, rowA2[:]))
            for t in range(TT):
                chain(v.tensor_tensor(y1[:, t], y1[:, t], rowC2[:], ALU.add))
            dve.sem_inc(sem("h2"), 1)
            turns_lo(h2T, KD)
            upc = Tally()

            def up1(c, last=False):
                b = bank(chunks.slot)[:].rearrange("p a (b s) -> p (a b) s", s=S)
                chunks.add()
                dve.wait_ge(sem("z_mid"), upc.n + 1)
                for tap in (1, 0):
                    sh = 2 - tap
                    for f in range(4):
                        wv = wconv[:, bass.ds(c, 1), f, tap:tap + 1].rearrange("p a b -> p (a b)")
                        ins = v.scalar_tensor_tensor(zc[:, f, sh:S], b[:, f, 0:S - sh], wv, zc[:, f, sh:S],
                                                     ALU.mult, ALU.add)
                    chain(ins)
                dve.sem_inc(acc_free, 1)
                dve.sem_inc(sem("z_conv"), 1)
                if not last:
                    split()
                dve.wait_ge(sem("z_gelu"), upc.n + 1)
                chain(v.tensor_tensor(zc[:, 0:2], zc[:, 0:2], zc[:, 2:4], ALU.mult))
                dve.sem_inc(sem("z_mul"), 1)
                if not last:
                    split()
                dve.wait_ge(sem("hid_hi"), upc.n + 1)
                hi, lo = (d[:, bass.ds(c * 2, 2), :] for d in hid)
                v.tensor_tensor(lo, zc[:, 0:2], hi.bitcast(F32), ALU.subtract).then_inc(sem("hid_lo"), 1)
                if not last:
                    split()
                    split()
                upc.add()

            for _ in range(4):
                split()
            with engine_loop(dve, FC // 2 - 1, (m, 8), (chunks, 2), (upc, 2), (chain.t, 2 * 3)) as i:
                for j in range(2):
                    up1(i * 2 + j)
            up1(FC - 2)
            up1(FC - 1, True)
            with engine_loop(dve, 2, (m, 24), (chunks, 2)) as i:
                for j in range(2):
                    b = finish(12)
                    v.tensor_copy(y2[:, :, bass.ds((i * 2 + j) * C, C)], b[:]).then_inc(acc_free, 1)
            dve.wait_ge(acc_free, chunks.n)
            dve.sem_inc(sem("y2"), 1)
            post(y2, rowA3, rowB3, "ld_rows4")
            dve.sem_inc(sem("x2"), 1)
            dve.wait_ge(sem("ld_rows5"), 32)
            rstd_wait()
            for t in range(TT):
                chain(scaled(n2[:, t], x[:, t], t, rowA3[:]))
            chain(scaled(nmeta[:], nmeta[:], 2, rowA3[:META, :], META))
            dve.sem_inc(sem("n2"), 1)
            for k in range(KD):
                turn_lo(nT[1][:, k], nT[0][:, k], L)
            turned()
            dve.sem_inc(sem("nT"), 1)
            dve.wait_ge(sem("krw_hi"), 1)
            v.tensor_tensor(krwl[:], krw[:], krwh[:].bitcast(F32), ALU.subtract).then_inc(sem("krw_lo"), 1)

            def rotate(dst, src, cos, sin, tmp):
                x1, x2 = half_of(src, 0), half_of(src, 1)
                chain(v.tensor_tensor(tmp[0], x1, cos, ALU.mult))
                chain(v.tensor_tensor(tmp[1], x2, sin, ALU.mult))
                chain(v.tensor_tensor(tmp[2], x2, cos, ALU.mult))
                chain(v.tensor_tensor(tmp[3], x1, sin, ALU.mult))
                chain(v.tensor_tensor(half_of(dst, 0), tmp[0], tmp[1], ALU.subtract))
                chain(v.tensor_tensor(half_of(dst, 1), tmp[2], tmp[3], ALU.add))

            def half_of(t, k):
                h = ROPE // 2
                return t[:, :, k * h:(k + 1) * h] if len(t.shape) == 3 else t[:, :, :, k * h:(k + 1) * h]

            dve.wait_ge(sem("kr"), 1)
            for np_, t0, t1 in ((P, 0, 2), (META, 2, 3)):
                src = ms[1][:np_, t0 * ROPE:t1 * ROPE].rearrange("p (t d) -> p t d", d=ROPE)
                rotate(krn[:np_, t0:t1, 0], src, rope[:np_, 0, t0:t1], rope[:np_, 1, t0:t1],
                       [ropet[:np_, q, t0:t1] for q in range(4)])
                chain(v.tensor_copy(krn[:np_, t0:t1, 1], krn[:np_, t0:t1, 0]))
            dve.sem_inc(sem("kr_rot"), 1)
            b = finish()
            chain(v.tensor_copy(qlat[:], b[:]))
            dve.sem_inc(acc_free, 1)
            dve.sem_inc(sem("lat"), 1)
            b = finish()
            chain(v.tensor_copy(kvlat[:, 0:2], b[:]))
            chain(v.tensor_copy(kvlat[:META, 2], ms[0][:META, :]))
            dve.sem_inc(acc_free, 1)
            dve.sem_inc(sem("lat"), 1)
            rstd_wait()
            for t in range(TT):
                chain(scaled(qlat[:, t], qlat[:, t], t, grow2[:, 0]))
            rstd_wait()
            for t in range(TT):
                chain(scaled(kvlat[:, t], kvlat[:, t], 3 + t, grow2[:, 1]))
            chain(scaled(kvlat[:META, 2], kvlat[:META, 2], 5, grow2[:META, 1], META))
            dve.sem_inc(sem("latn"), 1)
            for n in range(2):
                b = finish()
                chain(v.tensor_copy(uT[:, 4 * n:4 * n + 4, META:L], b[:].rearrange("p a (b s) -> p (a b) s", s=S)))
                chain(v.tensor_copy(uT[:, 4 * n:4 * n + 4, 0:META],
                                    ms[(n + 1) % 2][:, 0:4 * META].rearrange("p (f s) -> p f s", s=META)))
                dve.sem_inc(acc_free, 1)
            turn_copy([(krT[:], P, 0, L)])
            for k in range(2):
                turn_lo(*(d[:, 2 * k:2 * k + 2].rearrange("p a b -> p (a b)") for d in (qlT[1], qlT[0])))
            for k in range(4):
                turn_lo(kvT[1][:, k], kvT[0][:, k], L)
            turned()
            dve.sem_inc(sem("latT"), 1)
            lr, li, stp, mag, phi, kk, sn, cs, t9, t10 = (scol[:, j] for j in (0, 1, 3, 4, 5, 6, 7, 8, 9, 10))
            tt, ts, stt = v.tensor_tensor, v.tensor_scalar, v.scalar_tensor_tensor
            magic = 12582912.0

            def exp(dst, z):
                chain(ts(kk, z, 1.4426950408889634, None, ALU.mult))
                chain(ts(kk, kk, 127.0, -127.0, ALU.min, ALU.max))
                chain(ts(kk, kk, magic, None, ALU.add))
                chain(ts(kk, kk, magic, None, ALU.subtract))
                hi_ = 0.693359375
                chain(stt(t9, kk, -hi_, z, ALU.mult, ALU.add))
                chain(stt(t9, kk, 2.12194440054690583e-4, t9, ALU.mult, ALU.add))
                chain(ts(t9, t9, 0.5, -0.5, ALU.min, ALU.max))
                chain(ts(t10, t9, 1.0 / 40320, None, ALU.mult))
                for f in (5040, 720, 120, 24, 6, 2, 1):
                    chain(stt(t10, t10, 1.0 / f, t9, ALU.add, ALU.mult))
                chain(ts(t10, t10, 1.0, None, ALU.add))
                chain(ts(kk, kk, 127.0, None, ALU.add))
                chain(v.tensor_copy(t9.bitcast(mybir.dt.int32), kk))
                chain(ts(t9.bitcast(mybir.dt.int32), t9.bitcast(mybir.dt.int32), 23, None, ALU.logical_shift_left))
                chain(tt(dst, t10, t9, ALU.mult))

            dve.wait_ge(sem("ld_ssm"), 48)
            exp(stp, scol[:, 2])
            chain(tt(mag, lr, stp, ALU.mult))
            exp(mag, mag)
            chain(tt(phi, li, stp, ALU.mult))
            chain(ts(kk, phi, 1.0 / TWO_PI, None, ALU.mult))
            chain(ts(kk, kk, magic, None, ALU.add))
            chain(ts(kk, kk, magic, None, ALU.subtract))
            c1 = 6.28125
            c2 = float(np.float32(np.round((TWO_PI - c1) * 2 ** 21) / 2 ** 21))
            c3 = float(np.float32(TWO_PI - c1 - c2))
            chain(stt(phi, kk, -c1, phi, ALU.mult, ALU.add))
            chain(stt(phi, kk, -c2, phi, ALU.mult, ALU.add))
            chain(stt(phi, kk, -c3, phi, ALU.mult, ALU.add))
            lim = 3.1415925
            chain(ts(sn, phi, lim, -lim, ALU.min, ALU.max))
            chain(ts(phi, phi, float(np.pi / 2), None, ALU.add))
            chain(ts(kk, phi, float(np.pi), None, ALU.is_gt))
            chain(stt(phi, kk, -TWO_PI, phi, ALU.mult, ALU.add))
            chain(ts(cs, phi, lim, -lim, ALU.min, ALU.max))
            dve.sem_inc(sem("phase"), 1)
            with engine_loop(dve, 4, (m, 8), (chunks, 2)) as i:
                for j in range(2):
                    b = finish()
                    v.tensor_copy(gates2[:, :, bass.ds((i * 2 + j) * C, C)], b[:]).then_inc(acc_free, 1)
            dve.wait_ge(sem("ld_mask2"), 16)
            dve.wait_ge(sem("g_act"), 8)
            pair, tile = Tally(), Tally()

            def y_sum(j):
                dve.wait_ge(sem("y_part"), tile.n)
                chain(stt(ys[:, bass.ds(j, 1), :].rearrange("p a b -> p (a b)"),
                          uT[:, bass.ds(j, 1), META:L].rearrange("p a b -> p (a b)"),
                          ssmd[:, bass.ds(j, 1)], ms[1][:, META:L], ALU.mult, ALU.add))
                dve.sem_inc(sem("y_sum"), 1)

            def rotate_in():
                dve.wait_ge(sem("bu"), tile.n + 1)
                dve.wait_ge(sem("w_made"), tile.n + 1)
                bre, bim = acc[1][:, 0, 0:L], acc[1][:, 1, 0:L]
                wr, wi = (Wt[tile.slot % 2][:, r] for r in range(2))
                tt(vv[:, 0], bre, wr, ALU.mult)
                tt(vt[:, 0], bim, wi, ALU.mult)
                tt(vv[:, 1], bim, wr, ALU.mult)
                chain(tt(vt[:, 1], bre, wi, ALU.mult))
                tt(vv[:, 0], vv[:, 0], vt[:, 0], ALU.add)
                chain(tt(vv[:, 1], vv[:, 1], vt[:, 1], ALU.subtract))
                dve.sem_inc(sem("bu_free"), 1)

            def scans(s):
                if not tile.early(1):
                    dve.wait_ge(sem("xs"), tile.n)
                mg = scol[:, 4, bass.ds(s, 1)].to_broadcast([P, L])
                for r in range(2):
                    ins = v.tensor_tensor_scan(zz[:, r], mg, vv[:, r], 0.0, ALU.mult, ALU.add)
                chain(ins)
                dve.sem_inc(sem("z_made"), 1)
                tile.add()

            def head_pair(i, j):
                first = pair.early(1)
                v.tensor_copy(uj, uT[:, bass.ds(i * 2 + j, 1), :].rearrange("p a b -> p (a b)")).then_inc(sem("uj"), 1)
                finish(2)
                chunks.add()
                qsrc = acc[0][:, 1, 0:2 * P].rearrange("p (t h d) -> p t h d", t=2, d=ROPE)
                cosb, sinb = (rope[:, r, 0:2].unsqueeze(2).to_broadcast([P, 2, 2, 32]) for r in range(2))
                rotate(qrn[:], qsrc, cosb, sinb,
                       [qrt[:, q].rearrange("p (t h) d -> p t h d", h=2) for q in range(4)])
                dve.sem_inc(sem("q_rope"), 1)
                v.tensor_copy(knT[:], acc[1][:, :, 0:L])
                v.tensor_copy(vn2[:META, 2], acc[0][:META, 1, 2 * P:4 * P]).then_inc(acc_free, 1)
                dve.sem_inc(acc_free, 1)
                pair.add()

                def unit(n):
                    qt = n % 2
                    w = META + (qt + 1) * P
                    softmax_in(sc2, w, SCALE2, mask2[:, qt, 0:w], None, acc[0][:, n % 2])

                unit(0)
                if not first:
                    y_sum(i * 2 + j - 1)
                rotate_in()
                for n in range(4):
                    h, qt = divmod(n, 2)
                    if n < 3:
                        unit(n + 1)
                    scans((i * 2 + j) * 4 + n)
                    unit_out(None, att2[:, qt, bass.ds((i * 2 + j) * 2 * P + h * P, P)], ms[0][:, 0:P])
                    if n < 3:
                        rotate_in()
                rounds.add(6)

            for j in range(2):
                head_pair(0, j)
            with engine_loop(dve, 3, (m, 4), (chunks, 4), (pair, 2), (units, 8), (outs, 8), (rounds, 12), (tile, 8),
                             (chain.t, 62)) as i:
                for j in range(2):
                    head_pair(i + 1, j)
            y_sum(KS - 1)
            dve.sem_inc(sem("ssm_done"), 1)
            dve.wait_ge(sem("o_free"), outs.n)
            dve.sem_inc(sem("att"), 1)
            turns_lo(attT, KD)
            turned()
            dve.sem_inc(sem("att_turned"), 1)
            dve.wait_ge(sem("ys_hi"), 1)
            v.tensor_tensor(ysT[1][:], ys[:], ysT[0][:].bitcast(F32), ALU.subtract).then_inc(sem("ys_lo"), 1)
            with engine_loop(dve, 2, (m, 8), (chunks, 2), (chain.t, 2)) as i:
                for j in range(2):
                    b = finish()
                    n = (i * 2 + j) * C
                    chain(tt(mix2[:, :, bass.ds(n, C)], b[:], gates2[:, :, bass.ds(n, C)], ALU.mult))
                    dve.sem_inc(acc_free, 1)
            gl = Tally()
            with engine_loop(dve, 2, (m, 8), (chunks, 4), (gl, 2), (chain.t, 6)) as i:
                for j in range(2):
                    finish(2)
                    finish(2)
                    n = (i * 2 + j) * C
                    dve.wait_ge(sem("glu_sig"), gl.n + 1)
                    gl.add()
                    chain(tt(gtmp[:, j], bank(0)[:], gtmp[:, j], ALU.mult))
                    dve.sem_inc(acc_free, 2)
                    chain(tt(gtmp[:, j], gtmp[:, j], gates2[:, :, bass.ds(D + n, C)], ALU.mult))
                    o = mix2[:, :, bass.ds(n, C)]
                    chain(tt(o, o, gtmp[:, j], ALU.add))
            dve.sem_inc(sem("mix2"), 1)
            turns_lo(mxT, KD)
            turned()
            dve.sem_inc(sem("mixT"), 1)

            def add_to_x(times, groups):
                with engine_loop(dve, times, (m, 2 * groups), (chunks, 2)) as i:
                    for j in range(2):
                        b = finish(groups)
                        o = x[:, :, bass.ds((i * 2 + j) * C, C)]
                        tt(o, b[:], o, ALU.add).then_inc(acc_free, 1)

            dve.wait_ge(sem("ld_xre"), 16)
            add_to_x(2, 4)
            dve.wait_ge(acc_free, chunks.n)
            dve.sem_inc(sem("x3"), 1)
            dve.wait_ge(sem("ld_rowM"), 16)
            rstd_wait()
            for t in range(TT):
                chain(scaled(m2[:, t], x[:, t], t, rowM[:]))
            dve.sem_inc(sem("m2"), 1)
            turns_lo(h2T, KD)
            up2 = Tally()
            with engine_loop(dve, FC // 2, (m, 8), (chunks, 2), (up2, 2), (chain.t, 2)) as i:
                for j in range(2):
                    b = finish()
                    dve.wait_ge(sem("z_silu"), up2.n + 1)
                    chain(tt(zc[:, 0:2], b[:, 1].rearrange("p (f s) -> p f s", s=S), zc[:, 0:2], ALU.mult))
                    dve.sem_inc(acc_free, 1)
                    dve.sem_inc(sem("z_mul"), 1)
                    dve.wait_ge(sem("hid_hi"), up2.n + FC + 1)
                    hi, lo = (d[:, bass.ds((i * 2 + j) * 2, 2), :] for d in hid)
                    v.tensor_tensor(lo, zc[:, 0:2], hi.bitcast(F32), ALU.subtract).then_inc(sem("hid_lo"), 1)
                    up2.add()
            add_to_x(1, 12)
            b = finish(12)
            tt(cols(x, 2), b[:], cols(x, 2), ALU.add).then_inc(acc_free, 1)
            for _ in range(10):
                split()
            dve.wait_ge(pe_used, N_GROUPS)
            tt(cols(x, 3), bank(1)[:], cols(x, 3), ALU.add).then_inc(acc_free, 1)
            chunks.add()
            dve.wait_ge(acc_free, chunks.n)
            dve.sem_inc(sem("x4"), 1)
            dve.wait_ge(sem("ld_rowF"), 16)
            rstd_wait()
            for t in range(TT):
                chain(scaled(fin[:, t], x[:, t], t, rowF[:]))
            dve.sem_inc(sem("fin"), 1)

        @block.tensor
        def _(pe):
            m, chunks, rounds = Tally(), Tally(), Tally()
            mm, tr = nc.tensor.matmul, nc.tensor.transpose

            def begin_chunk():
                if not chunks.early(2):
                    pe.wait_ge(acc_free, chunks.n - 1)
                b = bank(chunks.slot)
                chunks.add()
                return b

            def begin_group():
                pe.wait_ge(lo_made, m.n + 1)
                return m.slot % 2

            def end_group(ins):
                ins.then_inc(pe_used, 1)
                m.add()

            def three(o, sh, sl, mh, ml, start, stop, share=False):
                mm(o, sl, mh, start=start, stop=False, skip_group_check=share)
                mm(o, sh, ml, start=False, stop=False, skip_group_check=share)
                return mm(o, sh, mh, start=False, stop=stop, skip_group_check=share)

            def rows_chunk(xT, tiles, groups, off=0, k0=0, meta=None):
                b = begin_chunk()
                k = 0
                kt = sum(groups)
                for n in groups:
                    s = begin_group()
                    for t in range(tiles):
                        for q in range(n):
                            c0 = off + t * P
                            ins = three(b[:, t], xT[0][:, k0 + k + q, c0:c0 + P], xT[1][:, k0 + k + q, c0:c0 + P],
                                        whi[:, s, q], wlo[:, s, q], k + q == 0, k + q == kt - 1)
                    if meta is not None:
                        for q in range(n):
                            ins = three(meta[0:META, :], xT[0][:, k + q, 0:META], xT[1][:, k + q, 0:META],
                                        whi[:, s, q], wlo[:, s, q], k + q == 0, k + q == kt - 1)
                    k += n
                    end_group(ins)

            def cols_chunk(xT, off=0, meta=None):
                b = begin_chunk()[:].rearrange("p a (b s) -> p (a b) s", s=S)
                for g in range(KD // GK):
                    s = begin_group()
                    for f in range(4):
                        for q in range(GK):
                            k = g * GK + q
                            wh, wl = whi[:, s, q, f * P:(f + 1) * P], wlo[:, s, q, f * P:(f + 1) * P]
                            ins = three(b[:, f], wh, wl, xT[0][:, k, off:off + S], xT[1][:, k, off:off + S],
                                        k == 0 and f % 2 == 0, k == KD - 1, True)
                            if meta is not None:
                                ins = three(meta[:, f * META:(f + 1) * META], wh, wl, xT[0][:, k, 0:META],
                                            xT[1][:, k, 0:META], k == 0 and f == 0, k == KD - 1, True)
                    end_group(ins)

            def turn(blocks):
                if not rounds.early(2):
                    pe.wait_ge(tp_free[rounds.slot % 2], rounds.on_bank(rounds.slot % 2))
                t = tp[rounds.slot % 2]
                for src, c in blocks:
                    n = src.shape[0]
                    w = int(np.prod(src.shape[1:]))
                    ins = tr(t[0:w, c:c + n], src, ident[0:n, 0:n])
                ins.then_inc(tp_full, 1)
                rounds.add()

            def turns(src, n):
                for k in range(n // 2):
                    turn([(src[:, t, (2 * k + q) * P:(2 * k + q + 1) * P], q * S + t * P) for q in range(2) for t in range(TT)])

            def turned():
                for b in range(2):
                    pe.wait_ge(tp_free[b], rounds.on_bank(b))

            pe.wait_ge(sem("cond"), 1)
            modc = Tally()

            def mods(i):
                for n in range(2):
                    if not modc.early(2):
                        pe.wait_ge(sem("mod_evac"), modc.n - 1)
                    for g in range(4):
                        pe.wait_ge(raw_in[g], (modc.n + 1) * 16)
                        for q in range(GK):
                            k = g * GK + q
                            ins = mm(ms[n][0:1, :], cond[:, k:k + 1], raw[:, g, q], start=k == 0, stop=k == KD - 1)
                        ins.then_inc(ada_used, 1)
                    modc.add()

            mods(0)
            with engine_loop(pe, 11, (modc, 2)) as i:
                mods(i)
            pe.wait_ge(sem("ld_ident"), 16)
            pe.wait_ge(sem("h1"), 2)
            turns(h1, KD)
            turned()
            rows_chunk(h1T, TT, [4] * 4)
            rows_chunk(h1T, TT, [4] * 4)
            with engine_loop(pe, 8, (m, 8), (chunks, 2)) as i:
                for _ in range(2):
                    rows_chunk(h1T, TT, [4] * 4)
            pe.wait_ge(sem("sguw_m"), 1)
            for r in range(2):
                turn([(wsn[:, 4 * r + q], q * P) for q in range(4)])
            turned()
            pe.wait_ge(sem("v_norm"), 1)
            for t in range(TT):
                for g in range(8):
                    ins = mm(ms[t][:, g * 64:(g + 1) * 64], wsT[:, g], pg[:, 1, t, g * 64:(g + 1) * 64], start=True, stop=True)
                ins.then_inc(sem("sgu_mix"), 1)
            pe.wait_ge(sem("y_sgu"), 1)
            for k in range(2):
                turn([(pg[:, 0, t, (2 * k + q) * P:(2 * k + q + 1) * P], q * S + t * P) for q in range(2) for t in range(TT)])
            for k in range(4):
                if k >= 2:
                    pe.wait_ge(sem("yp_hi"), k - 1)
                for s_ in range(TT):
                    ins = mm(ms[k % 2][:, 0:S], pg[:, 5, s_, k * P:(k + 1) * P], poolm[:, k, s_], start=s_ == 0, stop=s_ == TT - 1)
                ins.then_inc(sem("pooled"), 1)
                pe.wait_ge(sem("pooledT"), k + 1)
                mm(ms[k % 2][:, S:2 * S], poolw[:, k], pooledT[:, k], start=True, stop=True).then_inc(sem("pool_y"), 1)
            pe.wait_ge(sem("yp_hi"), 4)
            pe.wait_ge(acc_free, chunks.n)
            units, outs = Tally(), Tally()
            for hp in range(4):
                turn([(pg[:, 2 + w_, t, hp * P:(hp + 1) * P], (2 * w_ + t) * P) for w_ in range(2) for t in range(TT)])
                turned()

                def scores(n):
                    h, qt = divmod(n, 2)
                    r0 = h * DH1
                    bk = score_banks[units.slot % 4]
                    if not units.early(4):
                        pe.wait_ge(sem("max"), units.n - 3)
                    mm(bk[:, 0:(qt + 1) * P], qkT[r0:r0 + DH1, hp % 2, qt],
                       qkT[r0:r0 + DH1, hp % 2, 2:3 + qt], start=True, stop=True).then_inc(sem("sc_full"), 1)
                    units.add()

                scores(0)
                for n in range(4):
                    h, qt = divmod(n, 2)
                    if n < 3:
                        scores(n + 1)
                    head, s = 2 * hp + h, outs.slot % 2
                    pe.wait_ge(sem("exp"), outs.n + 1)
                    turn([(sc1[:, s, q * P:(q + 1) * P], q * P) for q in range(qt + 1)])
                    turned()
                    if not outs.early(2):
                        pe.wait_ge(sem("o_free"), outs.n - 1)
                    for q in range(qt + 1):
                        ins = mm(ms[s][:, 0:DH1], pT1[:, s, q * P:(q + 1) * P], pg[:, 4, q, head * DH1:(head + 1) * DH1],
                                 start=q == 0, stop=q == qt)
                    ins.then_inc(sem("pv"), 1)
                    outs.add()
            pe.wait_ge(sem("o_free"), 16)
            for k in range(2):
                turn([(pg[:, 1, t, (2 * k + q) * P:(2 * k + q + 1) * P], q * S + t * P) for q in range(2) for t in range(TT)])
            turned()
            pe.wait_ge(sem("yp_lo"), 4)
            for n in range(4):
                for br in range(3):
                    rows_chunk([t[:, br] for t in y3T], TT, [4])
            pe.wait_ge(sem("merged"), 1)
            turns(merged, KD)
            turned()
            with engine_loop(pe, 2, (m, 8), (chunks, 2)) as i:
                for _ in range(2):
                    rows_chunk(mgT, TT, [4] * 4)
            pe.wait_ge(sem("h2"), 1)
            turns(y1, KD)
            turned()

            def up():
                with engine_loop(pe, FC // 2, (m, 8), (chunks, 2)) as i:
                    for _ in range(2):
                        cols_chunk(h2T)

            def down(hid_count):
                pe.wait_ge(sem("hid_lo"), hid_count)
                with engine_loop(pe, 2, (m, 24), (chunks, 2)) as i:
                    for _ in range(2):
                        rows_chunk(hid, TT, DOWN_TILES)

            up()
            down(FC)
            pe.wait_ge(sem("n2"), 1)
            for k in range(KD):
                c = slice(k * P, (k + 1) * P)
                turn([(nmeta[:, c], 0), (n2[:, 0, c], META), (n2[:, 1, c], META + P)])
            turned()
            pe.wait_ge(sem("krw_lo"), 1)
            for t, (c0, n) in enumerate(((META, P), (META + P, P), (0, META))):
                for k in range(KD):
                    ins = three(ms[1][0:n, t * ROPE:(t + 1) * ROPE], nT[0][:, k, c0:c0 + n], nT[1][:, k, c0:c0 + n],
                                krwh[:, k], krwl[:, k], k == 0, k == KD - 1)
            ins.then_inc(sem("kr"), 1)
            rows_chunk(nT, TT, [4] * 4, META)
            rows_chunk(nT, TT, [4] * 4, META, meta=ms[0])
            pe.wait_ge(sem("kr_rot"), 1)
            for n in range(2):
                cols_chunk(nT, META, ms[(n + 1) % 2])
            turn([(krn[:META, 2].rearrange("p a b -> p (a b)"), 0), (krn[:, 0].rearrange("p a b -> p (a b)"), META),
                  (krn[:, 1].rearrange("p a b -> p (a b)"), META + P)])
            pe.wait_ge(sem("latn"), 1)
            for k in range(2):
                turn([(qlat[:, t, (2 * k + q) * P:(2 * k + q + 1) * P], q * S + t * P) for q in range(2) for t in range(TT)])
            for k in range(4):
                c = slice(k * P, (k + 1) * P)
                turn([(kvlat[:META, 2, c], 0), (kvlat[:, 0, c], META), (kvlat[:, 1, c], META + P)])
            with engine_loop(pe, 4, (m, 8), (chunks, 2)) as i:
                for _ in range(2):
                    rows_chunk(nT, TT, [4] * 4, META)
            pair, tile = Tally(), Tally()
            turned()

            def outputs():
                q = tile.slot % 4
                pe.wait_ge(sem("xs"), tile.n + 1)
                if q == 0 and not tile.early(1):
                    pe.wait_ge(sem("y_sum"), tile.i * (tile.per // 4) + tile.slot // 4 if tile.i is not None else tile.slot // 4)
                for r in range(2):
                    ins = mm(ms[1][q * 32:(q + 1) * 32, 0:L], bcT[:, 2 + r, q * 32:(q + 1) * 32], xx[:, r],
                             start=r == 0, stop=r == 1)
                ins.then_inc(sem("y_part"), 1)
                tile.add()

            inputs_ = Tally()

            def inputs():
                q = inputs_.slot % 4
                if not inputs_.early(1):
                    pe.wait_ge(sem("bu_free"), inputs_.n)
                rows = slice(q * 32, (q + 1) * 32)
                for r in range(2):
                    ins = mm(acc[1][:, r, 0:L], bcT[rows, r], uj[rows], start=True, stop=True)
                ins.then_inc(sem("bu"), 1)
                inputs_.add()

            def head_pair(i, j):
                first = pair.early(1)
                begin_chunk()
                s = begin_group()
                for h in range(2):
                    for q in range(GK):
                        three(acc[0][:, 0, h * S:(h + 1) * S], whi[:, s, q, h * P:(h + 1) * P], wlo[:, s, q, h * P:(h + 1) * P],
                              qlT[0][:, q], qlT[1][:, q], q == 0, q == GK - 1)
                for t in range(TT):
                    for q in range(GK):
                        ins = three(acc[0][:, 1, t * P:(t + 1) * P], qlT[0][:, q, t * P:(t + 1) * P], qlT[1][:, q, t * P:(t + 1) * P],
                                    whi[:, s, q, 2 * P:3 * P], wlo[:, s, q, 2 * P:3 * P], q == 0, q == GK - 1)
                end_group(ins)
                begin_chunk()
                s = begin_group()
                if not first:
                    pe.wait_ge(sem("bu_free"), inputs_.n)
                    pe.wait_ge(sem("o_free"), outs.n)
                for h in range(2):
                    for q in range(GK):
                        three(acc[1][:, h, 0:L], whi[:, s, q, h * P:(h + 1) * P], wlo[:, s, q, h * P:(h + 1) * P],
                              kvT[0][:, q], kvT[1][:, q], q == 0, q == GK - 1)
                for c0, n, o in ((META, P, ms[0][:, 0:S]), (META + P, P, ms[0][:, S:2 * S]),
                                 (0, META, acc[0][0:META, 1, 2 * P:4 * P])):
                    for q in range(GK):
                        ins = three(o, kvT[0][:, q, c0:c0 + n], kvT[1][:, q, c0:c0 + n],
                                    whi[:, s, q, 2 * P:4 * P], wlo[:, s, q, 2 * P:4 * P], q == 0, q == GK - 1)
                end_group(ins)
                if not first:
                    outputs()
                pe.wait_ge(sem("q_rope"), pair.n + 1)
                turn([(qrn[:, t].rearrange("p a b -> p (a b)"), t * P) for t in range(TT)])
                pe.wait_ge(sem("blk"), pair.n + 1)
                turn([(blk[:, r], r * P) for r in range(4)])
                turned()
                pe.wait_ge(acc_free, chunks.n)
                pe.wait_ge(sem("qnT"), pair.n + 1)
                pair.add()

                def scores(n):
                    h, qt = divmod(n, 2)
                    w = META + (qt + 1) * P
                    bk = acc[0][:, n % 2]
                    if n >= 2:
                        pe.wait_ge(sem("max"), units.n - 1)
                    mm(bk[:, 0:w], qnT[:, h, qt * P:(qt + 1) * P], knT[:, h, 0:w], start=True, stop=False)
                    mm(bk[:, 0:w], qrT[h * ROPE:(h + 1) * ROPE, qt * P:(qt + 1) * P],
                       krT[h * ROPE:(h + 1) * ROPE, 0:w], start=False, stop=True).then_inc(sem("sc_full"), 1)
                    units.add()

                scores(0)
                pe.wait_ge(sem("uj"), pair.n)
                inputs()
                for n in range(4):
                    h, qt = divmod(n, 2)
                    if n < 3:
                        scores(n + 1)
                    s = outs.slot % 2
                    pe.wait_ge(sem("exp"), outs.n + 1)
                    turn([(sc2[:, s, META + q * P:META + (q + 1) * P], q * P) for q in range(qt + 1)]
                         + [(sc2[:, s, 0:META], 2 * P)])
                    turned()
                    pe.wait_ge(sem("o_free"), outs.n)
                    o = ms[0][:, 0:P]
                    for q in range(qt + 1):
                        mm(o, pT2[:, s, q * P:(q + 1) * P], vn2[:, q, h * P:(h + 1) * P], start=q == 0, stop=False)
                    mm(o, pT2[:META, s, 2 * P:3 * P], vn2[:META, 2, h * P:(h + 1) * P],
                       start=False, stop=True).then_inc(sem("pv"), 1)
                    outs.add()
                    if n < 3:
                        inputs()
                        outputs()

            for j in range(2):
                head_pair(0, j)
            with engine_loop(pe, 3, (m, 4), (chunks, 4), (pair, 2), (units, 8), (outs, 8), (rounds, 12), (tile, 8),
                             (inputs_, 8)) as i:
                for j in range(2):
                    head_pair(i + 1, j)
            outputs()
            pe.wait_ge(sem("att"), 1)
            turns(att2, KD)
            turned()
            with engine_loop(pe, 2, (m, 8), (chunks, 2)) as i:
                for _ in range(2):
                    rows_chunk(attT, TT, [4] * 4)
            pe.wait_ge(sem("ys_lo"), 1)
            with engine_loop(pe, 2, (m, 8), (chunks, 4)) as i:
                for _ in range(4):
                    rows_chunk(ysT, TT, [4] * 2)
            pe.wait_ge(sem("mix2"), 1)
            turns(mix2, KD)
            turned()
            with engine_loop(pe, 2, (m, 8), (chunks, 2)) as i:
                for _ in range(2):
                    rows_chunk(mxT, TT, [4] * 4)
            pe.wait_ge(sem("m2"), 1)
            turns(m2, KD)
            turned()
            up()
            down(2 * FC)


def kernel(**inputs):
    from concourse import bacc
    from concourse.bass_utils import run_bass_kernel_spmd

    f = {k: np.asarray(v) for k, v in inputs.items()}
    g = {k: (v[0] if v.ndim > 1 and v.shape[0] == 1 else v) for k, v in f.items()}

    def groups(w, tiles=None, width=C):
        k, n = w.shape
        tiles = tiles or [GK] * (k // (P * GK))
        res = []
        for c in range(0, n, width):
            k0 = 0
            for t in tiles:
                b = np.zeros((P, GK, C), w.dtype)
                b[:, :t, :width] = w[k0 * P:(k0 + t) * P, c:c + width].reshape(t, P, width).transpose(1, 0, 2)
                res.append(b.reshape(P, GK * C))
                k0 += t
        return res

    def pairs(a_, b_, w=256):
        k = a_.shape[0]
        return np.stack([a_.reshape(k, -1, w), b_.reshape(k, -1, w)], 2).reshape(k, -1)

    def interleave(*lists):
        return [x_ for t in zip(*lists) for x_ in t]

    def by(lst, n):
        return [lst[i:i + n] for i in range(0, len(lst), n)]

    def flat(ll):
        return [x_ for l_ in ll for x_ in l_]

    w_up, w_in2 = g["w_up"], g["w_in_2"]
    wq = g["w_q_up_2"].reshape(LAT, HEADS2 // 2, 2, NOPE + ROPE)
    wq = np.concatenate([wq[..., :NOPE].reshape(LAT, HEADS2 // 2, -1), wq[..., NOPE:].reshape(LAT, HEADS2 // 2, -1),
                         np.zeros((LAT, HEADS2 // 2, P), wq.dtype)], -1).reshape(LAT, -1)
    wkv = g["w_kv_up_2"].reshape(LAT, HEADS2 // 2, 2, 2, NOPE).transpose(0, 1, 3, 2, 4).reshape(LAT, -1)
    off_kr, off_u = 2 * LAT, 2 * LAT + ROPE
    stream = (groups(g["w_in"])
              + interleave(groups(g["w_sgu_out"]), groups(g["w_moba_out"]), groups(g["w_pool_out"]))
              + groups(g["w_out"])
              + groups(pairs(w_up[:, :FF], w_up[:, FF:]))
              + groups(g["w_down"], DOWN_TILES)
              + groups(w_in2[:, :2 * LAT]) + groups(w_in2[:, off_u:])
              + interleave(groups(wq), groups(wkv))
              + groups(g["w_attn_proj_2"])
              + flat(interleave(by(groups(g["w_glu_val_2"]), 2), by(groups(g["w_glu_gate_2"]), 2)))
              + groups(g["w_out_2"])
              + groups(pairs(g["w_ffn_gate_2"], g["w_ffn_up_2"]))
              + groups(g["w_ffn_down_2"], DOWN_TILES))
    assert len(stream) == N_GROUPS
    feed = {"w_stream": np.stack(stream), "ada_stream": np.stack(groups(g["w_ada"]))}
    feed["x"] = f["x"][0]
    feed["c"] = f["c"][0].reshape(KD, P).T
    for name in ("b_ada", "b_in"):
        feed[name] = g[name].reshape(1, -1)
    for name in ("g_pre_mix", "g_post_mix", "g_pre_ffn", "g_post_ffn"):
        feed[name] = g[name]
    feed["sgu_g"] = g["sgu_norm_g"]
    feed["norm_mix"], feed["norm_q"], feed["norm_kv"] = g["norm_mix_2"], g["norm_q_2"], g["norm_kv_2"]
    feed["norm_ffn"], feed["norm_final"] = g["norm_ffn_2"], f["norm_final_2"]
    feed["meta"] = f["meta_tokens_2"]
    taps = np.concatenate([g["w_conv"], g["b_conv"][None]], 0).reshape(4, 2, FC, 2, P)
    feed["conv"] = taps.transpose(4, 2, 1, 3, 0).reshape(P, FC, 4, 4)
    feed["sgu_w"] = g["sgu_w"].transpose(1, 0, 2)
    feed["sgu_b"] = g["sgu_b"].T
    feed["pool_scale"] = g["pool_scale"].reshape(4, P).T
    feed["pool_w"] = g["pool_w"].transpose(1, 0, 2)
    feed["w_kr"] = w_in2[:, off_kr:off_kr + ROPE].reshape(KD, P, ROPE).transpose(1, 0, 2)
    feed["ssm_d"] = g["ssm_d_2"].reshape(KS, P).T
    st = lambda v: v.reshape(NST, P, *v.shape[2:])
    feed["lam_re"], feed["lam_im"] = st(g["ssm_lambda_re_2"]).T, st(g["ssm_lambda_im_2"]).T
    feed["log_step"] = st(np.repeat(g["ssm_log_step_2"][:, None], 64, 1)).T
    feed["ssm_b_re"], feed["ssm_b_im"] = (st(g[f"ssm_b_{r}_2"]).transpose(1, 0, 2) for r in ("re", "im"))
    feed["ssm_c_re"], feed["ssm_c_im"] = (g[f"ssm_c_{r}_2"].reshape(KS, P, 64).transpose(1, 0, 2) for r in ("re", "im"))
    one = np.float32
    feed["ident"] = np.eye(P, dtype=one)
    tok = np.arange(S)
    pm = np.zeros((4, S, S), one)
    for wi, w in enumerate((2, 4, 8, 16)):
        inside = (tok[:, None] <= tok[None]) & (tok[:, None] > tok[None] - w)
        pm[wi] = inside / np.minimum(tok + 1, w)[None] - np.eye(S)
    feed["pool_m"] = pm.reshape(4, TT, P, S).transpose(2, 0, 1, 3)
    dq = (tok[None] - tok[:, None]).astype(one)
    feed["dist"] = np.where(dq <= 0, dq, NEG).astype(one).reshape(TT, P, S).transpose(1, 0, 2)
    feed["tril"] = np.tril(np.ones((P, P), one))
    pos = np.arange(L)
    m2 = np.where(pos[None] <= tok[:, None] + META, 0.0, NEG).astype(one)
    feed["mask2"] = m2.reshape(TT, P, L).transpose(1, 0, 2)
    half = ROPE // 2
    freqs = (one(10000.0) ** (-np.arange(half, dtype=one) / one(half))).astype(one)
    ang = pos.astype(one)[:, None] * freqs[None]
    tab = np.zeros((P, 2, 3, half), one)
    for r, fn in enumerate((np.cos, np.sin)):
        v = fn(ang.astype(np.float64)).astype(one)
        tab[:, r, 0], tab[:, r, 1], tab[:META, r, 2] = v[META:META + P], v[META + P:], v[:META]
    feed["rope"] = tab
    gi = np.arange(P)
    feed["bmask"] = (gi[:, None] // 64 == np.arange(2)[None]).astype(one)
    feed["cmask"] = (gi[:, None] // 16 % 2 == np.arange(2)[None]).astype(one)

    nc = bacc.Bacc("TRN2", target_bir_lowering=False, num_devices=1)
    feed = {k: np.ascontiguousarray(v) for k, v in feed.items()}
    aps = {k: nc.dram_tensor(k, v.shape, F32, kind="ExternalInput").ap() for k, v in feed.items()}
    aps["x_dram"] = nc.dram_tensor("x_dram", (P, TT, D), F32, kind="Internal").ap()
    aps["mod_dram"] = nc.dram_tensor("mod_dram", (1, NMOD * D), F32, kind="Internal").ap()
    out = nc.dram_tensor("out", (1, S, D), F32, kind="ExternalOutput").ap()
    block_program(nc, aps, out)
    res = run_bass_kernel_spmd(nc, [feed], core_ids=[0])
    return res.results[0]["out"]
```

```python
from contextlib import ExitStack, contextmanager

import numpy as np
import concourse.bass as bass
from concourse import mybir

F32 = mybir.dt.float32
F32R = mybir.dt.float32r
ALU = mybir.AluOpType
ACT = mybir.ActivationFunctionType
AX = mybir.AxisListType

P = 128
D = 2048
KD = D // P
S = 256
TT = S // P
META = 16
L = S + META
C = 512
GK = 4
BW = 512
NMOD = 6
FF = 5632
KF = FF // P
FC = FF // 256
EPS = 1e-6
HEADS1, DH1 = 8, 64
HEADS2, NOPE, ROPE = 16, 128, 64
SCALE1 = DH1 ** -0.5
SCALE2 = (NOPE + ROPE) ** -0.5
LAT = 512
SSM = 1024
KS = SSM // P
NST = 32
TQ, TP = 17, 16
NEG = -1.0e30
TWO_PI = float(2 * np.pi)
CH_OUT1 = 18 + 12
CH_DOWN1 = 18 + 12 + 4 + FC
SSQ_LAT = 2 + 2 + 3 + 1
CH_DOWN2 = CH_DOWN1 + 4 + 4 + 8 + 16 + 4 + 8 + 4 + FC
NORMS_META = 6
CH_GATES2 = 18 + 12 + 4 + FC + 4 + 4
DOWN_TILES = [4] * 8 + [3] * 4

G_IN1, G_MERGE, G_OUT1, G_UP, G_DOWN = 72, 12, 16, 88, 48
G_IN2, G_HEADS, G_PROJ, G_GLU, G_OUT2 = 48, 16, 16, 16, 16
N_GROUPS = G_IN1 + G_MERGE + G_OUT1 + G_UP + G_DOWN + G_IN2 + G_HEADS + G_PROJ + G_GLU + G_OUT2 + G_UP + G_DOWN
G_BEFORE_HEADS = G_IN1 + G_MERGE + G_OUT1 + G_UP + G_DOWN + G_IN2
MOD_ROUND1 = 8
MOD_ROUND2 = MOD_ROUND1 + 1 + 2 + 2 + 4 * 5 + 2 + 8 + 8
BLK_ROUND = MOD_ROUND2 + 1 + KD + 1 + 7 + 2
N_FRONT = 2 * D // C * (KD // GK)
A_IN, A_OUT = 3 * D // C * (KD // GK), D // C * (KD // GK)


class Tally:

    def __init__(self):
        self.base, self.k, self.i, self.per = 0, 0, None, 0

    @property
    def n(self):
        if self.i is None:
            return self.base + self.k
        return self.i * self.per + (self.base + self.k)

    @property
    def slot(self):
        return self.base + self.k

    def on_bank(self, b):
        if self.i is None:
            return (self.base + self.k + 1 - b) // 2
        return self.i * (self.per // 2) + (self.base + self.k + 1 - b) // 2

    def early(self, n):
        return self.i is None and self.base + self.k < n

    def add(self, n=1):
        self.k += n


@contextmanager
def engine_loop(eng, times, *tallies):
    with eng.Fori(0, times) as i:
        for t, per in tallies:
            t.base, t.k, t.i, t.per = t.base + t.k, 0, i, per
        yield i
        for t, per in tallies:
            assert t.k == per, [(a.k, b) for a, b in tallies]
    for t, per in tallies:
        t.base, t.k, t.i = t.base + per * times, 0, None


class Chain:

    def __init__(self, eng, sem):
        self.eng, self.sem, self.t = eng, sem, Tally()

    def __call__(self, ins):
        ins.then_inc(self.sem, 1)
        self.t.add()
        self.eng.wait_ge(self.sem, self.t.n)


def block_program(nc, a, out):
    with ExitStack() as ctx:
        base = (nc.sbuf_base + 63) // 64 * 64
        K = 1024

        def at(name, shape, kb, dt=F32):
            size = int(np.prod(shape[1:])) * 4
            assert base + kb * K + size <= nc.sbuf_usable_end, (name, kb)
            return nc.alloc_sbuf_tensor_at(name, shape, dt, offset=base + int(kb * K))

        sems = {}

        def sem(name):
            if name not in sems:
                sems[name] = ctx.enter_context(nc.semaphore(name))
            return sems[name]

        raw = at("w_raw", [P, 4, GK, C], 0)
        whi = at("w_hi", [P, 2, GK, C], 32, F32R)
        wlo = at("w_lo", [P, 2, GK, C], 48, F32R)
        x = at("x_res", [P, TT, D], 64)
        pos = [80.0]

        def small(name, shape, dt=F32):
            t = at(name, shape, pos[0], dt)
            pos[0] += (int(np.prod(shape[1:])) * 4 + 31) // 32 * 32 / K
            return t

        ident = small("ident", [P, P])
        brow = small("bias_rows", [P, 2, C])
        wconv = small("conv_taps", [P, FC, 4, 4])
        rope = small("rope_tab", [P, 2, 3, 32])
        mcol = small("mod_cols", [P, (NMOD - 2) * D // P])
        ones = small("ones", [P, 1])
        cond = small("cond", [P, KD])
        ssq = small("sumsq", [P, 8])
        rstd = small("rstd", [P, 8])
        mhalf = small("minus_half", [P, 8])
        sgub = small("sgu_b", [P, 8])
        pscale = small("pool_scale", [P, 4])
        nmax = small("neg_max", [P, 2])
        rsum = small("row_sum", [P, 2])
        rinv = small("row_inv", [P, 2])
        ssmd = small("ssm_d", [P, KS])
        bmask = small("ssm_bmask", [P, 2])
        cmask = small("ssm_cmask", [P, 2])
        tril = small("tril", [P, P])
        U = 87.8125
        assert pos[0] <= U, pos

        def u(name, shape, kb, dt=F32):
            return at(name, shape, U + kb, dt)

        ada1 = [u(f"ada1_{j}", [P, GK, C], 104 + 8 * j) for j in range(2)]
        macc1 = [u(f"mod_sum1_{j}", [P, C], 96 + 2 * j) for j in range(3)]
        ada2 = [u(f"ada2_{j}", [P, GK, C], 8 * j) for j in range(2)]
        macc2 = [u(f"mod_sum2_{j}", [P, C], 16 + 2 * j) for j in range(4)]
        modr2 = u("mod_rows2", [D // P, P], 40)
        h1T = [u("h1T_hi", [P, KD, S], 0, F32R), u("h1T_lo", [P, KD, S], 16, F32R)]
        pg = u("proj", [P, 18, TT, C], 32)
        h1 = u("h1", [P, TT, D], 56)
        row1, rowT1 = u("row1", [P, 2, D], 32), u("rowT1", [P, D], 48)
        y3T = [u("y3T_hi", [P, 3, 4, S], 0, F32R), u("y3T_lo", [P, 3, 4, S], 12, F32R)]
        wsT = u("sgu_wT", [P, 8, P], 24)
        wsn = u("sgu_w", [P, 8, P], 28)
        qkT = u("qkT", [P, 2, 4, P], 28)
        poolm = u("pool_m", [P, 4, TT, S], 104)
        dist = u("alibi_dist", [P, TT, S], 112)
        poolw = u("pool_w", [P, 4, P], 114)
        sgug = u("sgu_g", [P, BW], 116)
        sc1 = u("scores1", [P, 2, S], 116)
        pT1 = u("probsT1", [P, 2, S], 118)
        pooledT = u("pooledT", [P, 4, S], 32)
        yp = u("pool_y", [P, 4, S], 24)
        merged = u("merged", [P, TT, D], 32)
        mgT = [u("mgT_hi", [P, KD, S], 56, F32R), u("mgT_lo", [P, KD, S], 72, F32R)]
        mtmp = u("merge_tmp", [P, TT, C], 48)
        y1 = u("y1", [P, TT, D], 88)
        rowA2, rowB2 = u("rowA2", [P, D], 104), u("rowB2", [P, D], 112)
        rowS2, rowG2, rowC2 = u("rowS2", [P, D], 32), u("rowG2", [P, D], 24), u("rowC2", [P, D], 48)
        h2T = [u("h2T_hi", [P, KD, S], 0, F32R), u("h2T_lo", [P, KD, S], 16, F32R)]
        hid = [u("hid_hi", [P, KF, S], 32, F32R), u("hid_lo", [P, KF, S], 76, F32R)]
        y2 = u("y2", [P, TT, D], 0)
        rowA3, rowB3 = u("rowA3", [P, D], 16), u("rowB3", [P, D], 24)
        n2 = u("n2", [P, TT, D], 0)
        nmeta = u("n_meta", [META, D], 104)
        sqmeta = u("sq_meta", [META, D], 112)
        nT = [u("nT_hi", [P, KD, L], 32, F32R), u("nT_lo", [P, KD, L], 49, F32R)]
        gates2 = u("gates2", [P, TT, 2 * D], 66)
        qlat = u("q_lat", [P, TT, LAT], 0)
        kvlat = u("kv_lat", [P, 3, LAT], 4)
        krn = u("k_rope", [P, 3, 2, ROPE], 10)
        krw = u("kr_w", [P, KD, ROPE], 80)
        krwh = u("kr_w_hi", [P, KD, ROPE], 84, F32R)
        krwl = u("kr_w_lo", [P, KD, ROPE], 88, F32R)
        grow2 = u("g_rows2", [P, 2, LAT], 25)
        ropet = u("rope_tmp", [P, 4, 4, 32], 29)
        qlT = [u("qlT_hi", [P, 4, S], 98, F32R), u("qlT_lo", [P, 4, S], 102, F32R)]
        kvT = [u("kvT_hi", [P, 4, L], 106, F32R), u("kvT_lo", [P, 4, L], 110.25, F32R)]
        krT = u("krT", [P, L], 114.5)
        mask2 = u("mask2", [P, TT, L], 115.5625)
        latsq = u("lat_sq", [P, LAT], 117.75)
        uT = u("uT", [P, KS, L], 12.5)
        X0 = 64 - U
        Qt = u("phase_q", [P, 2, NST, TQ], X0)
        Pt = u("phase_p", [P, 2, NST, TP], X0 + 4.25)
        bb = u("bb", [P, 2, NST, 16], X0 + 8.25)
        scol = u("ssm_cols", [P, 12, NST], X0 + 12.25)
        bcT = u("ssm_bcT", [P, 4, P], X0 + 13.75)
        cnat = u("ssm_c", [P, 2, KS, 64], 21)
        braw = u("ssm_b", [P, 2, NST, 16], 0)
        btmp = u("ssm_bt", [P, 2, NST, 16], 4)
        ptmp = u("phase_tmp2", [P, 2, NST, 8], 8)
        ys = u("ys", [P, KS, S], 0)
        Wt = [u("phase_a", [P, 2, L], 8), u("phase_b", [P, 2, L], 10.125)]
        vv = u("ssm_v", [P, 2, L], 25)
        zz = u("ssm_z", [P, 2, L], 27.125)
        xx = u("ssm_x", [P, 2, L], 29.25)
        blk = u("ssm_blk", [P, 4, P], 117.75)
        wtmp = u("phase_tmp", [P, L], 64.5)
        ysT = [u("ysT_hi", [P, KS, S], 32, F32R), u("ysT_lo", [P, KS, S], 40, F32R)]
        att2 = u("att2", [P, TT, D], 32)
        qnT = u("qnT", [P, 2, S], 48)
        qrn = u("q_rope", [P, TT, 2, ROPE], 50)
        qrT = u("qrT", [P, S], 51)
        knT = u("knT", [P, 2, L], 52)
        vn2 = u("v2", [P, 3, 2 * NOPE], 54.25)
        sc2 = u("scores2", [P, 2, L], 57.25)
        pT2 = u("probsT2", [P, 2, 3 * P], 59.5)
        qrt = u("q_rope_tmp", [P, 4, 4, 32], 62.5)
        attT = [u("attT_hi", [P, KD, S], 98, F32R), u("attT_lo", [P, KD, S], 8, F32R)]
        mix2 = u("mix2", [P, TT, D], 48)
        gtmp = u("glu_tmp", [P, 2, TT, C], 24)
        mxT = [u("mxT_hi", [P, KD, S], 66, F32R), u("mxT_lo", [P, KD, S], 82, F32R)]
        m2 = u("m2", [P, TT, D], 98)
        rowM = u("rowM", [P, D], 48)
        junk2 = u("junk2", [P, D], 64)
        junk3 = u("junk3", [P, D], 32)
        fin = u("fin", [P, TT, D], 0)
        rowF = u("rowF", [P, D], 16)

        acc = [ctx.enter_context(nc.psum_tensor(f"acc{i}", [P, 2, C], F32)) for i in range(2)]
        tp = [ctx.enter_context(nc.psum_tensor(f"tp{i}", [P, C], F32)) for i in range(2)]
        ms = [ctx.enter_context(nc.psum_tensor(f"ms{i}", [P, C], F32)) for i in range(2)]

        block = ctx.enter_context(nc.Block())

        raw_in = [sem(f"raw_in{i}") for i in range(4)]
        ada_used, hi_made, lo_made, pe_used = sem("ada_used"), sem("hi_made"), sem("lo_made"), sem("pe_used")
        ada_in = [sem("ada_in0"), sem("ada_in1")]
        mod_used, mod_acc, mod_sum = sem("mod_used"), sem("mod_acc"), sem("mod_sum")
        acc_free = sem("acc_free")
        tp_full, tp_hi = sem("tp_full"), sem("tp_hi")
        tp_free = [sem("tp_free0"), sem("tp_free1")]
        score_banks = [acc[0][:, 0], acc[0][:, 1], acc[1][:, 0], acc[1][:, 1]]
        vt = brow[:].rearrange("p a b -> p (a b)")[:, 0:2 * L].rearrange("p (r l) -> p r l", r=2)
        sqj = brow[:, 0]
        uj = brow[:].rearrange("p a b -> p (a b)")[:, 2 * L:3 * L]
        modr1 = wconv[0:3 * D // P].rearrange("p a b c -> p (a b c)")[:, 0:P]
        zc = brow[:].rearrange("p a b -> p (a b)").rearrange("p (f s) -> p f s", f=4)

        def cols(t, n, w=C):
            return t[:, :, n * w:(n + 1) * w]

        def bank(n):
            return acc[n % 2]

        @block.sync
        def _(sp):
            def load(slot, src):
                sp.dma_start(raw[:, slot].rearrange("p k c -> p (k c)"), src).then_inc(raw_in[slot], 16)

            def row(t, g):
                return t[bass.ds(g, 1)].rearrange("g p n -> (g p) n")

            for j in range(4):
                load(j, a["ada_stream"][j])
            with sp.Fori(1, N_FRONT // 4) as i:
                for j in range(4):
                    sp.wait_ge(ada_used, (i - 1) * 4 + j + 1)
                    load(j, row(a["ada_stream"], i * 4 + j))
            for j in range(4):
                sp.wait_ge(ada_used, N_FRONT - 3 + j)
                load(j, a["w_stream"][j])

            def load_ada(dst, slot, src):
                sp.dma_start(dst[slot][:].rearrange("p k c -> p (k c)"), src).then_inc(ada_in[slot], 16)

            for j in range(2):
                load_ada(ada1, j, a["ada_stream"][N_FRONT + j])
            with sp.Fori(0, 3) as i:
                for s in range(16):
                    sp.wait_ge(lo_made, i * 16 + s + 1)
                    load(s % 4, row(a["w_stream"], i * 16 + s + 4))
                    if s % 4 < 3:
                        r = s // 4 * 3 + s % 4
                        sp.wait_ge(mod_used, i * 12 + r + 1)
                        load_ada(ada1, r % 2, row(a["ada_stream"], i * 12 + r + N_FRONT + 2))
            for s in range(16):
                sp.wait_ge(lo_made, 48 + s + 1)
                load(s % 4, a["w_stream"][48 + s + 4])
                r = 36 + s // 4 * 3 + s % 4
                if s % 4 < 3 and r + 2 < A_IN:
                    sp.wait_ge(mod_used, r + 1)
                    load_ada(ada1, r % 2, a["ada_stream"][N_FRONT + r + 2])
            with sp.Fori(0, 5) as i:
                for j in range(4):
                    sp.wait_ge(lo_made, i * 4 + j + 65)
                    load(j, row(a["w_stream"], i * 4 + j + 68))
            sp.wait_ge(pe_used, G_IN1 + G_MERGE)
            for j in range(2):
                load_ada(ada2, j, a["ada_stream"][N_FRONT + A_IN + j])
            for s in range(G_OUT1):
                g_ = G_IN1 + G_MERGE + s
                sp.wait_ge(lo_made, g_ + 1)
                load(s % 4, a["w_stream"][g_ + 4])
                if s + 2 < A_OUT:
                    sp.wait_ge(mod_used, A_IN + s + 1)
                    load_ada(ada2, s % 2, a["ada_stream"][N_FRONT + A_IN + s + 2])
            with sp.Fori(0, (N_GROUPS - G_IN1 - G_MERGE - G_OUT1 - 4) // 4) as i:
                for j in range(4):
                    sp.wait_ge(lo_made, i * 4 + (G_IN1 + G_MERGE + G_OUT1 + j + 1))
                    load(j, row(a["w_stream"], i * 4 + (G_IN1 + G_MERGE + G_OUT1 + j + 4)))
            for t in range(TT):
                sp.wait_ge(sem("fin"), t + 1)
                sp.dma_start(out[0, t * P:(t + 1) * P], fin[:, t]).then_inc(sem("out"), 16)
            sp.wait_ge(sem("out"), 16 * TT)

        @block.gpsimd
        def _(pool):
            chain = Chain(pool, sem("pool_chain"))
            norms = Tally()
            g = nc.gpsimd

            def fetch(name, dst, src):
                pool.dma_start(dst, src).then_inc(sem("ld_" + name), 16)

            def bc(row):
                return row.partition_broadcast(P)

            def rsqrt_mean(width, parts):
                pool.wait_ge(sem("ssq"), norms.n + 1)
                norms.add()
                for np_, c0, c1 in parts:
                    chain(g.tensor_scalar(rstd[:np_, c0:c1], ssq[:np_, c0:c1], 1.0 / width, EPS, ALU.mult, ALU.add))
                    ins = g.tensor_tensor(rstd[:np_, c0:c1], rstd[:np_, c0:c1], mhalf[:np_, c0:c1], ALU.pow)
                    chain(ins)
                pool.sem_inc(sem("rstd"), 1)

            chain(g.memset(mhalf[:], -0.5))
            g.memset(ones[:], 1.0).then_inc(sem("ones"), 1)
            fetch("cond", cond[:], a["c"])
            fetch("x", x[:], a["x"].rearrange("(t p) d -> p t d", p=P))
            fetch("rows1", row1[:].rearrange("p a b -> p (a b)"), bc(a["b_ada"][0]))
            fetch("rows1", rowT1[:], bc(a["g_pre_mix"]))
            fetch("ident", ident[:], a["ident"])
            fetch("mcol", mcol[:], a["b_ada_cols"])
            fetch("small", sgub[:], a["sgu_b"])
            fetch("small", pscale[:], a["pool_scale"])
            fetch("small", rope[:], a["rope"])
            fetch("small", ssmd[:], a["ssm_d"])
            fetch("small", bmask[:], a["bmask"])
            fetch("small", cmask[:], a["cmask"])
            fetch("tril", tril[:], a["tril"])
            rsqrt_mean(D, [(P, 0, 2)])
            for j in range(2):
                fetch(f"brow{j}", brow[:, j], bc(a["b_in"][0, j * C:(j + 1) * C]))
            with pool.Fori(1, 9) as i:
                for j in range(2):
                    pool.wait_ge(acc_free, i * 2 + j - 1)
                    fetch(f"brow{j}", brow[:, j], bc(a["b_in"][0, bass.ds(i * 2 * C + j * C, C)]))
            pool.wait_ge(mod_used, A_IN)
            fetch("c1", poolm[:], a["pool_m"])
            fetch("c1", dist[:], a["dist"])
            fetch("c1", poolw[:], a["pool_w"])
            fetch("c1", sgug[:], bc(a["sgu_g"]))
            pool.wait_ge(pe_used, G_IN1)
            fetch("sguw", wsn[:], a["sgu_w"])
            pool.wait_ge(sem("ld_sguw"), 16)
            pool.wait_ge(sem("ld_tril"), 16)
            chain(g.tensor_tensor(wsn[:], wsn[:], tril[:].unsqueeze(1).to_broadcast([P, 8, P]), ALU.mult))
            pool.sem_inc(sem("sguw_m"), 1)
            mod = [None, None] + [a["mod_dram"][i] for i in range(NMOD - 2)]

            def save_mod(rnd, src, n0, n1):
                pool.wait_ge(tp_free[rnd % 2], rnd // 2 + 1)
                pool.dma_start(a["mod_dram"][n0:n1].rearrange("a (b p) -> (a b) p", p=P), src).then_inc(sem("mod_saved"), 16)

            save_mod(MOD_ROUND1, modr1, 0, 3)
            pool.wait_ge(sem("mod_saved"), 16)
            fetch("wconv", wconv[:], a["conv"])
            rsqrt_mean(BW, [(P, 0, 2)])
            pool.wait_ge(sem("mix_in"), 1)
            def rsqrt_chunks(so_far):
                pool.wait_ge(sem("ysq"), so_far + 4)
                q = ssq[:].rearrange("p (t c) -> p t c", c=4)
                chain(g.tensor_tensor(rstd[:, 0:2], q[:, :, 0], q[:, :, 1], ALU.add))
                chain(g.tensor_tensor(rstd[:, 0:2], rstd[:, 0:2], q[:, :, 2], ALU.add))
                chain(g.tensor_tensor(rstd[:, 0:2], rstd[:, 0:2], q[:, :, 3], ALU.add))
                chain(g.tensor_scalar(rstd[:, 0:2], rstd[:, 0:2], 1.0 / D, EPS, ALU.mult, ALU.add))
                chain(g.tensor_tensor(rstd[:, 0:2], rstd[:, 0:2], mhalf[:, 0:2], ALU.pow))
                pool.sem_inc(sem("rstd"), 1)

            fetch("rows2", rowA2[:], bc(mod[2]))
            fetch("rows2", rowB2[:], bc(a["g_post_mix"]))
            pool.wait_ge(sem("mgT"), 1)
            fetch("rows3", rowS2[:], bc(mod[4]))
            fetch("rows3", rowG2[:], bc(a["g_pre_ffn"]))
            fetch("rows3", rowC2[:], bc(mod[3]))
            rsqrt_chunks(0)
            for t in range(TT):
                rsqrt_mean(D, [(P, t, t + 1)])
            save_mod(MOD_ROUND2, modr2[:], 3, 4)
            pool.wait_ge(sem("mod_saved"), 32)
            pool.wait_ge(pe_used, G_IN1 + G_MERGE + G_OUT1 + G_UP)
            fetch("rows4", rowA3[:], bc(mod[5]))
            fetch("rows4", rowB3[:], bc(a["g_post_ffn"]))
            pool.wait_ge(sem("row4"), 1)
            fetch("rows5", rowB3[:], bc(a["norm_mix"]))
            pool.wait_ge(pe_used, G_IN1 + G_MERGE + G_OUT1 + G_UP + G_DOWN)
            fetch("rows5", nmeta[:], a["meta"])
            fetch("krw", krw[:], a["w_kr"])
            rsqrt_chunks(4)
            rsqrt_mean(D, [(META, 2, 3)])
            for t in range(TT):
                rsqrt_mean(D, [(P, t, t + 1)])
            pool.dma_start(a["x_dram"], x[:]).then_inc(sem("x_saved"), 16)
            pool.wait_ge(sem("nT"), 1)
            fetch("kr", grow2[:, 0], bc(a["norm_q"]))
            fetch("kr", grow2[:, 1], bc(a["norm_kv"]))
            pool.wait_ge(sem("x_saved"), 16)
            for j, name in enumerate(("lam_re", "lam_im", "log_step")):
                fetch("ssm", scol[:, j], a[name])
            rsqrt_mean(LAT, [(P, 0, 2)])
            rsqrt_mean(LAT, [(P, 3, 5), (META, 5, 6)])
            fetch("mask2", mask2[:], a["mask2"])
            pool.wait_ge(sem("latT"), 1)
            fetch("ssm_w", braw[:, 0], a["ssm_b_re"])
            fetch("ssm_w", braw[:, 1], a["ssm_b_im"])
            fetch("ssm_w", cnat[:, 0], a["ssm_c_re"])
            fetch("ssm_w", cnat[:, 1], a["ssm_c_im"])
            lr, li, mag, sn, cs = (scol[:, j] for j in (0, 1, 4, 7, 8))
            t5, t6, t9, t10, t11 = (scol[:, j] for j in (5, 6, 9, 10, 11))
            tt, ts = g.tensor_tensor, g.tensor_scalar
            pool.wait_ge(sem("trig"), 2)
            chain(g.memset(t6, -1.0))
            chain(tt(t9, lr, lr, ALU.mult))
            chain(tt(t10, li, li, ALU.mult))
            chain(tt(t9, t9, t10, ALU.add))
            chain(tt(t9, t9, t6, ALU.pow))
            chain(tt(t10, mag, cs, ALU.mult))
            chain(ts(t10, t10, 1.0, None, ALU.subtract))
            chain(tt(t11, mag, sn, ALU.mult))
            chain(tt(t5, t10, lr, ALU.mult))
            chain(tt(t6, t11, li, ALU.mult))
            chain(tt(t5, t5, t6, ALU.add))
            chain(tt(t5, t5, t9, ALU.mult))
            chain(tt(t6, t11, lr, ALU.mult))
            chain(tt(t10, t10, li, ALU.mult))
            chain(tt(t6, t6, t10, ALU.subtract))
            chain(tt(t6, t6, t9, ALU.mult))
            pool.wait_ge(sem("ld_ssm_w"), 64)
            cre, cim = (c.unsqueeze(2).to_broadcast([P, NST, 16]) for c in (t5, t6))
            chain(tt(bb[:, 0], cre, braw[:, 0], ALU.mult))
            chain(tt(btmp[:, 0], cim, braw[:, 1], ALU.mult))
            chain(tt(bb[:, 0], bb[:, 0], btmp[:, 0], ALU.subtract))
            chain(tt(bb[:, 1], cre, braw[:, 1], ALU.mult))
            chain(tt(btmp[:, 1], cim, braw[:, 0], ALU.mult))
            chain(tt(bb[:, 1], bb[:, 1], btmp[:, 1], ALU.add))
            chain(ts(cnat[:, 1], cnat[:, 1], -1.0, None, ALU.mult))

            def cmul(dst, u_, v_, t):
                tt(t, u_[1], v_[1], ALU.mult)
                chain(tt(dst[0], u_[0], v_[0], ALU.mult))
                chain(tt(dst[0], dst[0], t, ALU.subtract))
                tt(t, u_[0], v_[1], ALU.mult)
                chain(tt(dst[1], u_[1], v_[0], ALU.mult))
                chain(tt(dst[1], dst[1], t, ALU.add))

            def powers(tab, e):
                chain(g.memset(tab[:, 0, :, 0:1], 1.0))
                chain(g.memset(tab[:, 1, :, 0:1], 0.0))
                n = 1
                while n < 16:
                    wide = [c.unsqueeze(2).to_broadcast([P, NST, n]) for c in e]
                    cmul((tab[:, 0, :, n:2 * n], tab[:, 1, :, n:2 * n]), wide,
                         (tab[:, 0, :, 0:n], tab[:, 1, :, 0:n]), ptmp[:, 0, :, 0:n])
                    nxt = (ptmp[:, 1, :, 0], ptmp[:, 1, :, 1]) if n in (1, 4) else (ptmp[:, 1, :, 2], ptmp[:, 1, :, 3])
                    cmul(nxt, e, e, ptmp[:, 1, :, 4])
                    e, n = nxt, 2 * n
                return e

            e1 = (cs, sn)
            e16 = powers(Qt, e1)
            chain(g.tensor_copy(Qt[:, 0, :, 16], e16[0]))
            chain(g.tensor_copy(Qt[:, 1, :, 16], e16[1]))
            e17 = (ptmp[:, 1, :, 6], ptmp[:, 1, :, 7])
            cmul(e17, e16, e1, ptmp[:, 1, :, 5])
            powers(Pt, e17)

            def table(s):
                w = Wt[s % 2][:].rearrange("p r (c t) -> p r c t", t=TQ)
                pv = [Pt[:, r, s].unsqueeze(2).to_broadcast([P, TP, TQ]) for r in range(2)]
                qv = [Qt[:, r, s].unsqueeze(1).to_broadcast([P, TP, TQ]) for r in range(2)]
                cmul((w[:, 0], w[:, 1]), pv, qv, wtmp[:].rearrange("p (c t) -> p c t", t=TQ))
                pool.sem_inc(sem("w_made"), 1)

            pool.wait_ge(pe_used, G_BEFORE_HEADS)
            table(0)
            table(1)
            for j in range(KS):
                if j:
                    pool.wait_ge(tp_full, BLK_ROUND + 6 * (j - 1))
                for r in range(2):
                    chain(tt(blk[:, r].rearrange("p (q g c) -> p q g c", q=4, g=2),
                             bb[:, r, 4 * j:4 * j + 4].unsqueeze(2).to_broadcast([P, 4, 2, 16]),
                             bmask[:].unsqueeze(1).unsqueeze(3).to_broadcast([P, 4, 2, 16]), ALU.mult))
                    chain(tt(blk[:, 2 + r].rearrange("p (g c) -> p g c", g=2),
                             cnat[:, r, j].unsqueeze(1).to_broadcast([P, 2, 64]),
                             cmask[:].unsqueeze(2).to_broadcast([P, 2, 64]), ALU.mult))
                pool.sem_inc(sem("blk"), 1)
                for q in range(4):
                    s = 4 * j + q
                    pool.wait_ge(sem("z_made"), s + 1)
                    if s:
                        pool.wait_ge(sem("y_part"), s)
                    w = Wt[s % 2]
                    cmul((xx[:, 0], xx[:, 1]), (zz[:, 0], zz[:, 1]), (w[:, 0], w[:, 1]), wtmp[:])
                    pool.sem_inc(sem("xs"), 1)
                    if s + 2 < NST:
                        table(s + 2)
            pool.wait_ge(sem("ssm_done"), 1)
            fetch("xre", x[:], a["x_dram"])
            pool.wait_ge(sem("mixT"), 1)
            fetch("rowM", rowM[:], bc(a["norm_ffn"]))
            rsqrt_mean(D, [(P, 0, 2)])
            pool.wait_ge(pe_used, N_GROUPS - G_DOWN)
            fetch("rowF", rowF[:], bc(a["norm_final"]))
            rsqrt_chunks(8)

        @block.scalar
        def _(act):
            chain = Chain(act, sem("act_chain"))
            m, rounds, his = Tally(), Tally(), Tally()
            sc = nc.scalar

            def split():
                s = m.slot
                up = 0 if m.i is None else m.i * (m.per // 4)
                act.wait_ge(raw_in[s % 4], (up + (N_FRONT + s) // 4 + 1) * 16)
                if not m.early(2):
                    act.wait_ge(pe_used, m.n - 1)
                sc.activation(whi[:, s % 2], raw[:, s % 4], ACT.Copy).then_inc(hi_made, 1)
                m.add()

            def turn_hi(dst, w=2 * S):
                act.wait_ge(tp_full, rounds.n + 1)
                sc.activation(dst, tp[rounds.slot % 2][:, 0:w], ACT.Copy).then_inc(tp_hi, 1)
                rounds.add()

            def turns_hi(dst, n):
                for k in range(n // 2):
                    turn_hi(dst[:, 2 * k:2 * k + 2, :].rearrange("p a b -> p (a b)"))

            def squares(src, junk, where, cs, more=False):
                for k, c in enumerate(cs):
                    ins = sc.activation(junk(k), src(k), ACT.Square, accum_out=ssq[:where, c:c + 1])
                    if k < len(cs) - 1 or more:
                        chain(ins)
                return ins

            act.wait_ge(sem("ld_cond"), 16)
            sc.activation(cond[:], cond[:], ACT.Silu).then_inc(sem("cond"), 1)
            act.wait_ge(sem("ld_x"), 16)
            squares(lambda k: x[:, k], lambda k: h1[:, k], P, (0, 1)).then_inc(sem("ssq"), 1)
            split()
            split()
            turns_hi(h1T[0], KD)
            chunk = Tally()

            def in1(cn, func):
                for _ in range(4):
                    split()
                act.wait_ge(acc_free, chunk.n + 1)
                chunk.add()
                if func:
                    v = pg[:, bass.ds(cn, 1)].rearrange("p a t c -> p (a t c)")
                    sc.activation(v, v, func).then_inc(sem("p_act"), 1)

            in1(0, ACT.Gelu_apprx_tanh)
            in1(1, ACT.Gelu_apprx_tanh)
            with engine_loop(act, 2, (m, 8), (chunk, 2)) as i:
                for j in range(2):
                    in1(0, None)
            with engine_loop(act, 6, (m, 8), (chunk, 2)) as i:
                for j in range(2):
                    in1(i * 2 + 6 + j, ACT.Sigmoid)
            rounds.add(1)
            act.wait_ge(sem("v_cent"), 1)
            squares(lambda k: pg[:, 1, k], lambda k: pT1[:].rearrange("p a b -> p (a b)"), P, (0, 1)).then_inc(sem("ssq"), 1)
            rounds.add(2)
            for k in range(2):
                turn_hi(y3T[0][:, 0, 2 * k:2 * k + 2].rearrange("p a b -> p (a b)"))
            for k in range(4):
                act.wait_ge(sem("pool_y"), k + 1)
                chain(sc.activation(yp[:, k], ms[k % 2][:, S:2 * S], ACT.Copy, scale=pscale[:, k:k + 1]))
                sc.activation(y3T[0][:, 2, k], yp[:, k], ACT.Copy).then_inc(sem("yp_hi"), 1)

            units = Tally()

            def exps(sct, w):
                act.wait_ge(sem("max"), units.n + 1)
                s = units.slot % 2
                sc.activation(sct[:, s, 0:w], sct[:, s, 0:w], ACT.Exp, bias=nmax[:, s:s + 1],
                              accum_out=rsum[:, s:s + 1]).then_inc(sem("exp"), 1)
                units.add()

            for hp in range(4):
                rounds.add(1)
                for h in range(2):
                    for qt in range(2):
                        exps(sc1, (qt + 1) * P)
                        rounds.add(1)
            for k in range(2):
                turn_hi(y3T[0][:, 1, 2 * k:2 * k + 2].rearrange("p a b -> p (a b)"))
            for _ in range(G_MERGE):
                split()
            turns_hi(mgT[0], KD)

            def chunk_squares(y, n, ready):
                act.wait_ge(acc_free, ready)
                for t in range(TT):
                    ins = sc.activation(sqj[:], cols(y, n)[:, t], ACT.Square, accum_out=ssq[:, t * 4 + n:t * 4 + n + 1])
                    chain(ins)
                act.sem_inc(sem("ysq"), 1)

            def tile_squares(junk, name):
                for t in range(TT):
                    act.wait_ge(sem(name), t + 1)
                    squares(lambda k: x[:, t], lambda k: junk[:], P, (t,), True)
                    act.sem_inc(sem("ssq"), 1)

            for n in range(4):
                for q in range(4):
                    if n and q == 1:
                        chunk_squares(y1, n - 1, CH_OUT1 + n)
                    split()
            chunk_squares(y1, 3, CH_OUT1 + 4)
            tile_squares(junk2, "x1")
            turns_hi(h2T[0], KD)
            rounds.add(1)
            upc = Tally()
            act.wait_ge(sem("ld_wconv"), 16)
            act.wait_ge(sem("mod_saved"), 32)

            def up1(c, last=False):
                act.wait_ge(pe_used, upc.n * 4 + (G_IN1 + G_MERGE + G_OUT1 + 4))
                if not upc.early(1):
                    act.wait_ge(sem("hid_lo"), upc.n)
                for f in range(4):
                    ins = sc.activation(zc[:, f], bank(upc.slot)[:].rearrange("p a (b s) -> p (a b) s", s=S)[:, f],
                                        ACT.Identity, scale=wconv[:, bass.ds(c, 1), f, 2:3].rearrange("p a b -> p (a b)"),
                                        bias=wconv[:, bass.ds(c, 1), f, 3:4].rearrange("p a b -> p (a b)"))
                ins.then_inc(sem("z_mid"), 1)
                if not last:
                    split()
                act.wait_ge(sem("z_conv"), upc.n + 1)
                sc.activation(zc[:, 0:2], zc[:, 0:2], ACT.Gelu_apprx_tanh).then_inc(sem("z_gelu"), 1)
                if not last:
                    split()
                act.wait_ge(sem("z_mul"), upc.n + 1)
                sc.activation(hid[0][:, bass.ds(c * 2, 2), :], zc[:, 0:2], ACT.Copy).then_inc(sem("hid_hi"), 1)
                if not last:
                    split()
                    split()
                upc.add()

            for _ in range(4):
                split()
            up1(0)
            up1(1)
            with engine_loop(act, FC // 2 - 2, (m, 8), (upc, 2)) as i:
                for j in range(2):
                    up1(i * 2 + 2 + j)
            up1(FC - 2)
            up1(FC - 1, True)
            for n in range(4):
                for q in range(12):
                    if n and q == 3:
                        chunk_squares(y2, n - 1, CH_DOWN1 + n)
                    split()
            chunk_squares(y2, 3, CH_DOWN1 + 4)
            act.wait_ge(sem("ld_rows5"), 32)
            act.wait_ge(sem("rstd"), NORMS_META)
            squares(lambda k: nmeta[:], lambda k: sqmeta[:], META, (2,), True)
            act.sem_inc(sem("ssq"), 1)
            tile_squares(junk3, "x2")
            act.wait_ge(sem("ld_krw"), 16)
            sc.activation(krwh[:], krw[:], ACT.Copy).then_inc(sem("krw_hi"), 1)
            for k in range(KD):
                turn_hi(nT[0][:, k], L)
            rounds.add(1)
            for _ in range(8):
                split()
            act.wait_ge(sem("lat"), 1)
            squares(lambda k: qlat[:, k], lambda k: latsq[:], P, (0, 1)).then_inc(sem("ssq"), 1)
            act.wait_ge(sem("lat"), 2)
            act.wait_ge(sem("ssq"), SSQ_LAT)
            squares(lambda k: kvlat[:, k], lambda k: latsq[:], P, (3, 4), True)
            squares(lambda k: kvlat[:META, 2], lambda k: latsq[:META, :], META, (5,)).then_inc(sem("ssq"), 1)
            for _ in range(8):
                split()
            rounds.add(1)
            for k in range(2):
                turn_hi(qlT[0][:, 2 * k:2 * k + 2].rearrange("p a b -> p (a b)"))
            for k in range(4):
                turn_hi(kvT[0][:, k], L)
            act.wait_ge(sem("phase"), 1)
            sc.activation(scol[:, 7], scol[:, 7], ACT.Sin).then_inc(sem("trig"), 1)
            sc.activation(scol[:, 8], scol[:, 8], ACT.Sin).then_inc(sem("trig"), 1)
            gate = Tally()

            def gates(n):
                for _ in range(4):
                    split()
                act.wait_ge(acc_free, gate.n + CH_GATES2 + 1)
                v = gates2[:, :, bass.ds(n * C, C)]
                sc.activation(v, v, ACT.Sigmoid).then_inc(sem("g_act"), 1)
                gate.add()

            with engine_loop(act, 4, (m, 8), (gate, 2)) as i:
                for j in range(2):
                    gates(i * 2 + j)

            def turn_copy(parts):
                act.wait_ge(tp_full, rounds.n + 1)
                t = tp[rounds.slot % 2]
                for dst, np_, c0, c1 in parts:
                    ins = sc.activation(dst, t[:np_, c0:c1], ACT.Copy)
                ins.then_inc(tp_free[rounds.slot % 2], 1)
                rounds.add()

            def head_pair(first=False):
                if not first:
                    split()
                split()
                act.wait_ge(pe_used, m.n - 1)
                sc.activation(qnT[:].rearrange("p h s -> p (h s)"), acc[0][:, 0], ACT.Copy)
                sc.activation(vn2[:, 0:2], ms[0][:].rearrange("p (t d) -> p t d", t=2), ACT.Copy).then_inc(sem("qnT"), 1)
                turn_copy([(qrT[:], P, 0, S)])
                turn_copy([(bcT[:].rearrange("p a b -> p (a b)"), P, 0, C)])
                exps(sc2, META + P)
                for n in range(4):
                    w = (n % 2 + 1) * P
                    s = n % 2
                    turn_copy([(pT2[:, s, 0:w], P, 0, w), (pT2[:META, s, 2 * P:3 * P], META, 2 * P, 3 * P)])
                    if n < 3:
                        exps(sc2, META + ((n + 1) % 2 + 1) * P)

            head_pair(True)
            head_pair()
            with engine_loop(act, 3, (m, 4), (units, 8), (rounds, 12)) as i:
                for j in range(2):
                    head_pair()
            split()
            turns_hi(attT[0], KD)
            act.wait_ge(sem("att_turned"), 1)
            chain(sc.activation(ys[:], ys[:], ACT.Gelu_apprx_tanh))
            sc.activation(ysT[0][:], ys[:], ACT.Copy).then_inc(sem("ys_hi"), 1)
            with engine_loop(act, 2, (m, 8)) as i:
                for _ in range(8):
                    split()
            glu = Tally()
            with engine_loop(act, 2, (m, 8), (glu, 2)) as i:
                for j in range(2):
                    for _ in range(2):
                        split()
                    act.wait_ge(pe_used, m.n - 2)
                    sc.activation(gtmp[:, j], bank(0)[:], ACT.Sigmoid).then_inc(sem("glu_sig"), 1)
                    for _ in range(2):
                        split()
                    glu.add()
            turns_hi(mxT[0], KD)
            with engine_loop(act, 2, (m, 8)) as i:
                for _ in range(8):
                    split()
            act.wait_ge(sem("x3"), 1)
            squares(lambda k: x[:, k], lambda k: m2[:, k], P, (0, 1)).then_inc(sem("ssq"), 1)
            turns_hi(h2T[0], KD)
            up2c = Tally()

            def up2(c):
                for _ in range(4):
                    split()
                act.wait_ge(pe_used, m.n - 2)
                act.wait_ge(sem("hid_lo"), up2c.n + FC)
                sc.activation(zc[:, 0:2], bank(up2c.slot)[:, 0].rearrange("p (f s) -> p f s", s=S),
                              ACT.Silu).then_inc(sem("z_silu"), 1)
                act.wait_ge(sem("z_mul"), up2c.n + FC + 1)
                sc.activation(hid[0][:, bass.ds(c * 2, 2), :], zc[:, 0:2], ACT.Copy).then_inc(sem("hid_hi"), 1)
                up2c.add()

            with engine_loop(act, FC // 2, (m, 8), (up2c, 2)) as i:
                for j in range(2):
                    up2(i * 2 + j)
            for n in range(4):
                for q in range(12 if n < 3 else 10):
                    if n and q == 3:
                        chunk_squares(x, n - 1, CH_DOWN2 + n)
                    split()
            chunk_squares(x, 3, CH_DOWN2 + 4)

        @block.vector
        def _(dve):
            chain = Chain(dve, sem("dve_chain"))
            m, chunks, rounds, los, norms = Tally(), Tally(), Tally(), Tally(), Tally()
            v = nc.vector

            def split():
                s = m.slot
                dve.wait_ge(hi_made, m.n + 1)
                v.tensor_tensor(wlo[:, s % 2], raw[:, s % 4], whi[:, s % 2].bitcast(F32), ALU.subtract).then_inc(lo_made, 1)
                m.add()

            def finish(n=4):
                for _ in range(n):
                    split()
                dve.wait_ge(pe_used, m.n - 2)
                b = bank(chunks.slot)
                chunks.add()
                return b

            def turn_lo(lo, hi, w=2 * S):
                dve.wait_ge(tp_hi, los.n + 1)
                v.tensor_tensor(lo, tp[rounds.slot % 2][:, 0:w], hi.bitcast(F32), ALU.subtract).then_inc(tp_free[rounds.slot % 2], 1)
                los.add()
                rounds.add()

            def turns_lo(dst, n):
                for k in range(n // 2):
                    lo, hi = (d[:, 2 * k:2 * k + 2, :].rearrange("p a b -> p (a b)") for d in (dst[1], dst[0]))
                    turn_lo(lo, hi)

            def turn_copy(parts):
                dve.wait_ge(tp_full, rounds.n + 1)
                t = tp[rounds.slot % 2]
                for dst, np_, c0, c1 in parts:
                    ins = v.tensor_copy(dst, t[:np_, c0:c1])
                ins.then_inc(tp_free[rounds.slot % 2], 1)
                rounds.add()

            def turned():
                for b in range(2):
                    dve.wait_ge(tp_free[b], rounds.on_bank(b))

            def rstd_wait():
                dve.wait_ge(sem("rstd"), norms.n + 1)
                norms.add()

            def scaled(dst, src, c, row, np_=P):
                return v.scalar_tensor_tensor(dst, src, rstd[:np_, c:c + 1], row, ALU.mult, ALU.mult)

            dve.wait_ge(sem("ld_rows1"), 32)
            for n in range(2 * D // C):
                c = slice(n % 4 * C, (n % 4 + 1) * C)
                r = row1[:, n // 4, c]
                dve.wait_ge(ada_used, (n + 1) * 4)
                chain(v.tensor_tensor(r, ms[n % 2][:], r, ALU.add))
                dve.sem_inc(sem("mod_evac"), 1)
                if n < 4:
                    chain(v.scalar_tensor_tensor(r, r, 1.0, rowT1[:, c], ALU.add, ALU.mult))
                    if n == 0:
                        rstd_wait()
                for t in range(TT):
                    if n < 4:
                        chain(scaled(h1[:, t, c], x[:, t, c], t, r))
                    else:
                        v.tensor_tensor(h1[:, t, c], h1[:, t, c], r, ALU.add).then_inc(sem("h1"), 1)
            split()
            split()
            turns_lo(h1T, KD)

            adas = Tally()

            def ada_group(slots, macc, g):
                b = adas.slot % 2
                dve.wait_ge(ada_in[b], (adas.on_bank(b) + 1) * 16)
                for q in range(GK):
                    k = g * GK + q
                    if k == 0:
                        chain(v.tensor_scalar(macc[:], slots[b][:, q], cond[:, 0:1], None, ALU.mult))
                    else:
                        chain(v.scalar_tensor_tensor(macc[:], slots[b][:, q], cond[:, k:k + 1], macc[:], ALU.mult, ALU.add))
                dve.sem_inc(mod_used, 1)
                if g == GK - 1:
                    dve.sem_inc(mod_acc, 1)
                adas.add()

            def in1(cn, turn, jj, with_ada):
                for q in range(4):
                    split()
                    if with_ada and q < 3:
                        r = jj * 3 + q
                        ada_group(ada1, macc1[r // 4], r % 4)
                b = finish(0)
                dve.wait_ge(sem(f"ld_brow{jj % 2}"), (turn + 1) * 16)
                o = pg[:, bass.ds(cn, 1)].rearrange("p a t c -> p (a t) c")
                ins = v.tensor_tensor(o, b[:], brow[:, jj % 2:jj % 2 + 1, :].to_broadcast([P, TT, C]), ALU.add)
                ins.then_inc(acc_free, 1)

            with engine_loop(dve, 4, (m, 16), (chunks, 4), (adas, 12), (chain.t, 48)) as i:
                for jj in range(4):
                    in1(i * 4 + jj, i * 2 + jj // 2, jj, True)
            for jj in range(2):
                in1(16 + jj, 8, jj, False)

            def mod_bias(c0, c1, total):
                dve.wait_ge(mod_sum, total)
                v.tensor_tensor(mcol[:, c0:c1], mcol[:, c0:c1], ms[0][:, 0:c1 - c0], ALU.add).then_inc(sem("mod_cols"), 1)

            dve.wait_ge(sem("ld_mcol"), 16)
            mod_bias(0, 48, 12)
            turn_copy([(modr1, 48, 0, P)])
            dve.wait_ge(sem("ld_c1"), 64)
            dve.wait_ge(sem("ld_small"), 96)
            dve.wait_ge(sem("p_act"), 2)
            for t in range(TT):
                chain(v.reduce_sum(ssq[:, 6 + t:7 + t], pg[:, 1, t], AX.X))
                chain(v.tensor_scalar(ssq[:, 6 + t:7 + t], ssq[:, 6 + t:7 + t], 1.0 / BW, None, ALU.mult))
                ins = v.tensor_scalar(pg[:, 1, t], pg[:, 1, t], ssq[:, 6 + t:7 + t], None, ALU.subtract)
                chain(ins)
            dve.sem_inc(sem("v_cent"), 1)
            for r in range(2):
                turn_copy([(wsT[:, 4 * r:4 * r + 4].rearrange("p a b -> p (a b)"), P, 0, C)])
            rstd_wait()
            for t in range(TT):
                ins = scaled(pg[:, 1, t], pg[:, 1, t], t, sgug[:])
                chain(ins)
            dve.sem_inc(sem("v_norm"), 1)
            for t in range(TT):
                dve.wait_ge(sem("sgu_mix"), t + 1)
                o = pg[:, 1, t].rearrange("p (g d) -> p g d", g=8)
                chain(v.tensor_tensor(o, ms[t][:].rearrange("p (g d) -> p g d", g=8),
                                      sgub[:].unsqueeze(2).to_broadcast([P, 8, 64]), ALU.add))
                chain(v.tensor_tensor(pg[:, 0, t], pg[:, 1, t], pg[:, 0, t], ALU.mult))
            dve.sem_inc(sem("y_sgu"), 1)
            for k in range(2):
                turn_lo(*(d[:, 0, 2 * k:2 * k + 2].rearrange("p a b -> p (a b)") for d in (y3T[1], y3T[0])))
            for k in range(4):
                dve.wait_ge(sem("pooled"), k + 1)
                v.tensor_copy(pooledT[:, k], ms[k % 2][:, 0:S]).then_inc(sem("pooledT"), 1)
            for k in range(4):
                dve.wait_ge(sem("yp_hi"), k + 1)
                v.tensor_tensor(y3T[1][:, 2, k], yp[:, k], y3T[0][:, 2, k].bitcast(F32), ALU.subtract).then_inc(sem("yp_lo"), 1)

            units = Tally()

            def softmax_in(sct, w, scale, bias, slope, bk=None):
                s = units.slot % 2
                dve.wait_ge(sem("sc_full"), units.n + 1)
                if bk is None:
                    bk = score_banks[units.slot % 4]
                if slope is None:
                    chain(v.scalar_tensor_tensor(sct[:, s, 0:w], bk[:, 0:w], scale, bias, ALU.mult, ALU.add))
                else:
                    chain(v.tensor_scalar(sct[:, s, 0:w], bk[:, 0:w], scale, None, ALU.mult))
                    chain(v.scalar_tensor_tensor(sct[:, s, 0:w], bias, slope, sct[:, s, 0:w], ALU.mult, ALU.add))
                chain(v.reduce_max(nmax[:, s:s + 1], sct[:, s, 0:w], AX.X))
                v.tensor_scalar(nmax[:, s:s + 1], nmax[:, s:s + 1], -1.0, None, ALU.mult).then_inc(sem("max"), 1)
                units.add()

            outs = Tally()

            def unit_out(parts, dst, src):
                s = outs.slot % 2
                if parts:
                    turn_copy(parts)
                else:
                    dve.wait_ge(sem("exp"), outs.n + 1)
                chain(v.reciprocal(rinv[:, s:s + 1], rsum[:, s:s + 1]))
                dve.wait_ge(sem("pv"), outs.n + 1)
                v.tensor_scalar(dst, src, rinv[:, s:s + 1], None, ALU.mult).then_inc(sem("o_free"), 1)
                outs.add()

            slopes = [2.0 ** (-(8.0 / HEADS1) * (h + 1)) for h in range(HEADS1)]
            for hp in range(4):
                turn_copy([(qkT[:, hp % 2].rearrange("p a b -> p (a b)"), P, 0, C)])

                def unit(n):
                    h, qt = divmod(n, 2)
                    w = (qt + 1) * P
                    softmax_in(sc1, w, SCALE1, dist[:, qt, 0:w], slopes[2 * hp + h])

                unit(0)
                for n in range(4):
                    h, qt = divmod(n, 2)
                    w = (qt + 1) * P
                    if n < 3:
                        unit(n + 1)
                    head = 2 * hp + h
                    unit_out([(pT1[:, outs.slot % 2, 0:w], P, 0, w)], pg[:, 1, qt, head * DH1:(head + 1) * DH1],
                             ms[outs.slot % 2][:, 0:DH1])
            for k in range(2):
                turn_lo(*(d[:, 1, 2 * k:2 * k + 2].rearrange("p a b -> p (a b)") for d in (y3T[1], y3T[0])))
            dve.sem_inc(sem("mix_in"), 1)
            dve.wait_ge(sem("p_act"), 14)
            for n in range(4):
                for br in range(3):
                    b = finish(1)
                    gt = pg[:, 6 + 4 * br + n]
                    o = cols(merged, n)
                    if br == 0:
                        chain(v.tensor_tensor(o, b[:], gt, ALU.mult))
                        dve.sem_inc(acc_free, 1)
                    else:
                        chain(v.tensor_tensor(mtmp[:], b[:], gt, ALU.mult))
                        dve.sem_inc(acc_free, 1)
                        chain(v.tensor_tensor(o, o, mtmp[:], ALU.add))
            dve.sem_inc(sem("merged"), 1)
            turns_lo(mgT, KD)
            turned()
            dve.sem_inc(sem("mgT"), 1)
            dve.wait_ge(sem("ld_rows2"), 32)
            chain(v.tensor_tensor(rowA2[:], rowA2[:], rowB2[:], ALU.mult))

            for n in range(4):
                for g in range(4):
                    split()
                    ada_group(ada2, macc2[n], g)
                b = finish(0)
                v.tensor_copy(cols(y1, n), b[:]).then_inc(acc_free, 1)
                if n == 2:
                    dve.wait_ge(sem("ld_rows3"), 48)
                    chain(v.scalar_tensor_tensor(rowS2[:], rowS2[:], 1.0, rowG2[:], ALU.add, ALU.mult))
            dve.wait_ge(acc_free, chunks.n)

            def post(y, row, done):
                rstd_wait()
                for t in range(TT):
                    chain(scaled(y[:, t], y[:, t], t, row[:]))
                    chain(v.tensor_tensor(x[:, t], x[:, t], y[:, t], ALU.add))
                    dve.sem_inc(sem(done), 1)

            post(y1, rowA2, "x1")
            for t in range(TT):
                rstd_wait()
                chain(scaled(y1[:, t], x[:, t], t, rowS2[:]))
                chain(v.tensor_tensor(y1[:, t], y1[:, t], rowC2[:], ALU.add))
            dve.sem_inc(sem("h2"), 1)
            turns_lo(h2T, KD)
            mod_bias(48, 64, 16)
            turn_copy([(modr2[:], 16, 0, P)])
            upc = Tally()

            def up1(c, last=False):
                b = bank(chunks.slot)[:].rearrange("p a (b s) -> p (a b) s", s=S)
                chunks.add()
                dve.wait_ge(sem("z_mid"), upc.n + 1)
                for tap in (1, 0):
                    sh = 2 - tap
                    for f in range(4):
                        wv = wconv[:, bass.ds(c, 1), f, tap:tap + 1].rearrange("p a b -> p (a b)")
                        ins = v.scalar_tensor_tensor(zc[:, f, sh:S], b[:, f, 0:S - sh], wv, zc[:, f, sh:S],
                                                     ALU.mult, ALU.add)
                    chain(ins)
                dve.sem_inc(acc_free, 1)
                dve.sem_inc(sem("z_conv"), 1)
                if not last:
                    split()
                dve.wait_ge(sem("z_gelu"), upc.n + 1)
                chain(v.tensor_tensor(zc[:, 0:2], zc[:, 0:2], zc[:, 2:4], ALU.mult))
                dve.sem_inc(sem("z_mul"), 1)
                if not last:
                    split()
                dve.wait_ge(sem("hid_hi"), upc.n + 1)
                hi, lo = (d[:, bass.ds(c * 2, 2), :] for d in hid)
                v.tensor_tensor(lo, zc[:, 0:2], hi.bitcast(F32), ALU.subtract).then_inc(sem("hid_lo"), 1)
                if not last:
                    split()
                    split()
                upc.add()

            for _ in range(4):
                split()
            with engine_loop(dve, FC // 2 - 1, (m, 8), (chunks, 2), (upc, 2), (chain.t, 2 * 3)) as i:
                for j in range(2):
                    up1(i * 2 + j)
            up1(FC - 2)
            up1(FC - 1, True)
            dve.wait_ge(sem("ld_rows4"), 32)
            chain(v.tensor_tensor(rowA3[:], rowA3[:], rowB3[:], ALU.mult))
            dve.sem_inc(sem("row4"), 1)
            with engine_loop(dve, 2, (m, 24), (chunks, 2)) as i:
                for j in range(2):
                    b = finish(12)
                    v.tensor_copy(y2[:, :, bass.ds((i * 2 + j) * C, C)], b[:]).then_inc(acc_free, 1)
            dve.wait_ge(acc_free, chunks.n)
            post(y2, rowA3, "x2")
            dve.wait_ge(sem("ld_rows5"), 32)
            rstd_wait()
            chain(scaled(nmeta[:], nmeta[:], 2, rowB3[:META, :], META))
            for t in range(TT):
                rstd_wait()
                chain(scaled(n2[:, t], x[:, t], t, rowB3[:]))
            dve.sem_inc(sem("n2"), 1)
            dve.wait_ge(sem("krw_hi"), 1)
            v.tensor_tensor(krwl[:], krw[:], krwh[:].bitcast(F32), ALU.subtract).then_inc(sem("krw_lo"), 1)
            for k in range(KD):
                turn_lo(nT[1][:, k], nT[0][:, k], L)
            turned()
            dve.sem_inc(sem("nT"), 1)

            def rotate(dst, src, cos, sin, tmp):
                x1, x2 = half_of(src, 0), half_of(src, 1)
                chain(v.tensor_tensor(tmp[0], x1, cos, ALU.mult))
                chain(v.tensor_tensor(tmp[1], x2, sin, ALU.mult))
                chain(v.tensor_tensor(tmp[2], x2, cos, ALU.mult))
                chain(v.tensor_tensor(tmp[3], x1, sin, ALU.mult))
                chain(v.tensor_tensor(half_of(dst, 0), tmp[0], tmp[1], ALU.subtract))
                chain(v.tensor_tensor(half_of(dst, 1), tmp[2], tmp[3], ALU.add))

            def half_of(t, k):
                h = ROPE // 2
                return t[:, :, k * h:(k + 1) * h] if len(t.shape) == 3 else t[:, :, :, k * h:(k + 1) * h]

            dve.wait_ge(sem("kr"), 1)
            v.tensor_copy(krT[0:ROPE, :], ms[1][0:ROPE, 0:L]).then_inc(sem("kr_copied"), 1)
            dve.wait_ge(tp_full, rounds.n + 1)
            for np_, t0, t1 in ((P, 0, 2), (META, 2, 3)):
                src = tp[rounds.slot % 2][:np_, t0 * ROPE:t1 * ROPE].rearrange("p (t d) -> p t d", d=ROPE)
                rotate(krn[:np_, t0:t1, 0], src, rope[:np_, 0, t0:t1], rope[:np_, 1, t0:t1],
                       [ropet[:np_, q, t0:t1] for q in range(4)])
                chain(v.tensor_copy(krn[:np_, t0:t1, 1], krn[:np_, t0:t1, 0]))
            dve.sem_inc(tp_free[rounds.slot % 2], 1)
            rounds.add()
            b = finish()
            chain(v.tensor_copy(qlat[:], b[:]))
            dve.sem_inc(acc_free, 1)
            dve.sem_inc(sem("lat"), 1)
            b = finish()
            chain(v.tensor_copy(kvlat[:, 0:2], b[:]))
            chain(v.tensor_copy(kvlat[:META, 2], ms[0][:META, :]))
            dve.sem_inc(acc_free, 1)
            dve.sem_inc(sem("lat"), 1)
            dve.wait_ge(sem("ld_kr"), 32)
            rstd_wait()
            for t in range(TT):
                chain(scaled(qlat[:, t], qlat[:, t], t, grow2[:, 0]))
            rstd_wait()
            for t in range(TT):
                chain(scaled(kvlat[:, t], kvlat[:, t], 3 + t, grow2[:, 1]))
            chain(scaled(kvlat[:META, 2], kvlat[:META, 2], 5, grow2[:META, 1], META))
            dve.sem_inc(sem("latn"), 1)
            for n in range(2):
                b = finish()
                chain(v.tensor_copy(uT[:, 4 * n:4 * n + 2, :], b[:, :, 0:L]))
                for j in range(2):
                    chain(v.tensor_copy(uT[:, 4 * n + 2 + j], (tp, ms)[n][j][:, 0:L]))
                dve.sem_inc(acc_free, 1)
            turn_copy([(krT[:], P, 0, L)])
            for k in range(2):
                turn_lo(*(d[:, 2 * k:2 * k + 2].rearrange("p a b -> p (a b)") for d in (qlT[1], qlT[0])))
            for k in range(4):
                turn_lo(kvT[1][:, k], kvT[0][:, k], L)
            turned()
            dve.sem_inc(sem("latT"), 1)
            lr, li, stp, mag, phi, kk, sn, cs, t9, t10 = (scol[:, j] for j in (0, 1, 3, 4, 5, 6, 7, 8, 9, 10))
            tt, ts, stt = v.tensor_tensor, v.tensor_scalar, v.scalar_tensor_tensor
            magic = 12582912.0

            def exp(dst, z):
                chain(ts(kk, z, 1.4426950408889634, None, ALU.mult))
                chain(ts(kk, kk, 127.0, -127.0, ALU.min, ALU.max))
                chain(ts(kk, kk, magic, None, ALU.add))
                chain(ts(kk, kk, magic, None, ALU.subtract))
                hi_ = 0.693359375
                chain(stt(t9, kk, -hi_, z, ALU.mult, ALU.add))
                chain(stt(t9, kk, 2.12194440054690583e-4, t9, ALU.mult, ALU.add))
                chain(ts(t9, t9, 0.5, -0.5, ALU.min, ALU.max))
                chain(ts(t10, t9, 1.0 / 40320, None, ALU.mult))
                for f in (5040, 720, 120, 24, 6, 2, 1):
                    chain(stt(t10, t10, 1.0 / f, t9, ALU.add, ALU.mult))
                chain(ts(t10, t10, 1.0, None, ALU.add))
                chain(ts(kk, kk, 127.0, None, ALU.add))
                chain(v.tensor_copy(t9.bitcast(mybir.dt.int32), kk))
                chain(ts(t9.bitcast(mybir.dt.int32), t9.bitcast(mybir.dt.int32), 23, None, ALU.logical_shift_left))
                chain(tt(dst, t10, t9, ALU.mult))

            dve.wait_ge(sem("ld_ssm"), 48)
            exp(stp, scol[:, 2])
            chain(tt(mag, lr, stp, ALU.mult))
            exp(mag, mag)
            chain(tt(phi, li, stp, ALU.mult))
            chain(ts(kk, phi, 1.0 / TWO_PI, None, ALU.mult))
            chain(ts(kk, kk, magic, None, ALU.add))
            chain(ts(kk, kk, magic, None, ALU.subtract))
            c1 = 6.28125
            c2 = float(np.float32(np.round((TWO_PI - c1) * 2 ** 21) / 2 ** 21))
            c3 = float(np.float32(TWO_PI - c1 - c2))
            chain(stt(phi, kk, -c1, phi, ALU.mult, ALU.add))
            chain(stt(phi, kk, -c2, phi, ALU.mult, ALU.add))
            chain(stt(phi, kk, -c3, phi, ALU.mult, ALU.add))
            lim = 3.1415925
            chain(ts(sn, phi, lim, -lim, ALU.min, ALU.max))
            chain(ts(phi, phi, float(np.pi / 2), None, ALU.add))
            chain(ts(kk, phi, float(np.pi), None, ALU.is_gt))
            chain(stt(phi, kk, -TWO_PI, phi, ALU.mult, ALU.add))
            chain(ts(cs, phi, lim, -lim, ALU.min, ALU.max))
            dve.sem_inc(sem("phase"), 1)
            with engine_loop(dve, 4, (m, 8), (chunks, 2)) as i:
                for j in range(2):
                    b = finish()
                    v.tensor_copy(gates2[:, :, bass.ds((i * 2 + j) * C, C)], b[:]).then_inc(acc_free, 1)
            dve.wait_ge(sem("ld_mask2"), 16)
            dve.wait_ge(sem("g_act"), 8)
            pair, tile = Tally(), Tally()

            def y_sum(j):
                dve.wait_ge(sem("y_part"), tile.n)
                chain(stt(ys[:, bass.ds(j, 1), :].rearrange("p a b -> p (a b)"),
                          uT[:, bass.ds(j, 1), META:L].rearrange("p a b -> p (a b)"),
                          ssmd[:, bass.ds(j, 1)], ms[1][:, META:L], ALU.mult, ALU.add))
                dve.sem_inc(sem("y_sum"), 1)

            def rotate_in():
                dve.wait_ge(sem("bu"), tile.n + 1)
                dve.wait_ge(sem("w_made"), tile.n + 1)
                bre, bim = acc[1][:, 0, 0:L], acc[1][:, 1, 0:L]
                wr, wi = (Wt[tile.slot % 2][:, r] for r in range(2))
                tt(vv[:, 0], bre, wr, ALU.mult)
                tt(vt[:, 0], bim, wi, ALU.mult)
                tt(vv[:, 1], bim, wr, ALU.mult)
                chain(tt(vt[:, 1], bre, wi, ALU.mult))
                tt(vv[:, 0], vv[:, 0], vt[:, 0], ALU.add)
                chain(tt(vv[:, 1], vv[:, 1], vt[:, 1], ALU.subtract))
                dve.sem_inc(sem("bu_free"), 1)

            def scans(s):
                if not tile.early(1):
                    dve.wait_ge(sem("xs"), tile.n)
                mg = scol[:, 4, bass.ds(s, 1)].to_broadcast([P, L])
                for r in range(2):
                    ins = v.tensor_tensor_scan(zz[:, r], mg, vv[:, r], 0.0, ALU.mult, ALU.add)
                chain(ins)
                dve.sem_inc(sem("z_made"), 1)
                tile.add()

            def head_pair(i, j):
                first = pair.early(1)
                v.tensor_copy(uj, uT[:, bass.ds(i * 2 + j, 1), :].rearrange("p a b -> p (a b)")).then_inc(sem("uj"), 1)
                if not first:
                    split()
                split()
                dve.wait_ge(pe_used, m.n - 1)
                chunks.add(2)
                qsrc = acc[0][:, 1, 0:2 * P].rearrange("p (t h d) -> p t h d", t=2, d=ROPE)
                cosb, sinb = (rope[:, r, 0:2].unsqueeze(2).to_broadcast([P, 2, 2, 32]) for r in range(2))
                rotate(qrn[:], qsrc, cosb, sinb,
                       [qrt[:, q].rearrange("p (t h) d -> p t h d", h=2) for q in range(4)])
                dve.sem_inc(sem("q_rope"), 1)
                v.tensor_copy(knT[:], acc[1][:, :, 0:L])
                v.tensor_copy(vn2[:META, 2], acc[0][:META, 1, 2 * P:4 * P]).then_inc(acc_free, 1)
                dve.sem_inc(acc_free, 1)
                pair.add()

                def unit(n):
                    qt = n % 2
                    w = META + (qt + 1) * P
                    softmax_in(sc2, w, SCALE2, mask2[:, qt, 0:w], None, acc[0][:, n % 2])

                unit(0)
                if not first:
                    y_sum(i * 2 + j - 1)
                rotate_in()
                for n in range(4):
                    h, qt = divmod(n, 2)
                    if n < 3:
                        unit(n + 1)
                    scans((i * 2 + j) * 4 + n)
                    unit_out(None, att2[:, qt, bass.ds((i * 2 + j) * 2 * P + h * P, P)], ms[0][:, 0:P])
                    if n < 3:
                        rotate_in()
                rounds.add(6)

            for j in range(2):
                head_pair(0, j)
            with engine_loop(dve, 3, (m, 4), (chunks, 4), (pair, 2), (units, 8), (outs, 8), (rounds, 12), (tile, 8),
                             (chain.t, 62)) as i:
                for j in range(2):
                    head_pair(i + 1, j)
            split()
            y_sum(KS - 1)
            dve.sem_inc(sem("ssm_done"), 1)
            dve.wait_ge(sem("o_free"), outs.n)
            dve.sem_inc(sem("att"), 1)
            turns_lo(attT, KD)
            turned()
            dve.sem_inc(sem("att_turned"), 1)
            dve.wait_ge(sem("ys_hi"), 1)
            v.tensor_tensor(ysT[1][:], ys[:], ysT[0][:].bitcast(F32), ALU.subtract).then_inc(sem("ys_lo"), 1)
            with engine_loop(dve, 2, (m, 8), (chunks, 2), (chain.t, 2)) as i:
                for j in range(2):
                    b = finish()
                    n = (i * 2 + j) * C
                    chain(tt(mix2[:, :, bass.ds(n, C)], b[:], gates2[:, :, bass.ds(n, C)], ALU.mult))
                    dve.sem_inc(acc_free, 1)
            gl = Tally()
            with engine_loop(dve, 2, (m, 8), (chunks, 4), (gl, 2), (chain.t, 6)) as i:
                for j in range(2):
                    finish(2)
                    n = (i * 2 + j) * C
                    dve.wait_ge(sem("glu_sig"), gl.n + 1)
                    gl.add()
                    dve.sem_inc(acc_free, 1)
                    finish(2)
                    chain(tt(gtmp[:, j], bank(1)[:], gtmp[:, j], ALU.mult))
                    dve.sem_inc(acc_free, 1)
                    chain(tt(gtmp[:, j], gtmp[:, j], gates2[:, :, bass.ds(D + n, C)], ALU.mult))
                    o = mix2[:, :, bass.ds(n, C)]
                    chain(tt(o, o, gtmp[:, j], ALU.add))
            dve.sem_inc(sem("mix2"), 1)
            turns_lo(mxT, KD)
            turned()
            dve.sem_inc(sem("mixT"), 1)

            def add_to_x(times, groups):
                with engine_loop(dve, times, (m, 2 * groups), (chunks, 2)) as i:
                    for j in range(2):
                        b = finish(groups)
                        o = x[:, :, bass.ds((i * 2 + j) * C, C)]
                        tt(o, b[:], o, ALU.add).then_inc(acc_free, 1)

            dve.wait_ge(sem("ld_xre"), 16)
            add_to_x(2, 4)
            dve.wait_ge(acc_free, chunks.n)
            dve.sem_inc(sem("x3"), 1)
            dve.wait_ge(sem("ld_rowM"), 16)
            rstd_wait()
            for t in range(TT):
                chain(scaled(m2[:, t], x[:, t], t, rowM[:]))
            dve.sem_inc(sem("m2"), 1)
            turns_lo(h2T, KD)
            up2 = Tally()
            with engine_loop(dve, FC // 2, (m, 8), (chunks, 2), (up2, 2), (chain.t, 2)) as i:
                for j in range(2):
                    b = finish()
                    dve.wait_ge(sem("z_silu"), up2.n + 1)
                    chain(tt(zc[:, 0:2], b[:, 1].rearrange("p (f s) -> p f s", s=S), zc[:, 0:2], ALU.mult))
                    dve.sem_inc(acc_free, 1)
                    dve.sem_inc(sem("z_mul"), 1)
                    dve.wait_ge(sem("hid_hi"), up2.n + FC + 1)
                    hi, lo = (d[:, bass.ds((i * 2 + j) * 2, 2), :] for d in hid)
                    v.tensor_tensor(lo, zc[:, 0:2], hi.bitcast(F32), ALU.subtract).then_inc(sem("hid_lo"), 1)
                    up2.add()
            add_to_x(1, 12)
            b = finish(12)
            tt(cols(x, 2), b[:], cols(x, 2), ALU.add).then_inc(acc_free, 1)
            for _ in range(10):
                split()
            dve.wait_ge(pe_used, N_GROUPS)
            tt(cols(x, 3), bank(1)[:], cols(x, 3), ALU.add).then_inc(acc_free, 1)
            chunks.add()
            dve.wait_ge(acc_free, chunks.n)
            dve.wait_ge(sem("ld_rowF"), 16)
            rstd_wait()
            for t in range(TT):
                scaled(fin[:, t], x[:, t], t, rowF[:]).then_inc(sem("fin"), 1)

        @block.tensor
        def _(pe):
            m, chunks, rounds = Tally(), Tally(), Tally()
            mm, tr = nc.tensor.matmul, nc.tensor.transpose

            def begin_chunk():
                if not chunks.early(2):
                    pe.wait_ge(acc_free, chunks.n - 1)
                b = bank(chunks.slot)
                chunks.add()
                return b

            def begin_group():
                pe.wait_ge(lo_made, m.n + 1)
                return m.slot % 2

            def end_group(ins):
                ins.then_inc(pe_used, 1)
                m.add()

            def three(o, sh, sl, mh, ml, start, stop, share=False):
                mm(o, sl, mh, start=start, stop=False, skip_group_check=share)
                mm(o, sh, ml, start=False, stop=False, skip_group_check=share)
                return mm(o, sh, mh, start=False, stop=stop, skip_group_check=share)

            def rows_chunk(xT, tiles, groups, off=0, k0=0, meta=None, hidden=None):
                b = begin_chunk()
                k = 0
                kt = sum(groups)
                for n in groups:
                    s = begin_group()
                    if hidden and k + n == kt:
                        pe.wait_ge(sem("hid_lo"), hidden)
                    for t in range(tiles):
                        for q in range(n):
                            c0 = off + t * P
                            ins = three(b[:, t], xT[0][:, k0 + k + q, c0:c0 + P], xT[1][:, k0 + k + q, c0:c0 + P],
                                        whi[:, s, q], wlo[:, s, q], k + q == 0, k + q == kt - 1)
                    if meta is not None:
                        for q in range(n):
                            ins = three(meta[0:META, :], xT[0][:, k + q, 0:META], xT[1][:, k + q, 0:META],
                                        whi[:, s, q], wlo[:, s, q], k + q == 0, k + q == kt - 1)
                    k += n
                    end_group(ins)

            def cols_chunk(xT):
                b = begin_chunk()[:].rearrange("p a (b s) -> p (a b) s", s=S)
                for g in range(KD // GK):
                    s = begin_group()
                    for f in range(4):
                        for q in range(GK):
                            k = g * GK + q
                            ins = three(b[:, f], whi[:, s, q, f * P:(f + 1) * P], wlo[:, s, q, f * P:(f + 1) * P],
                                        xT[0][:, k], xT[1][:, k], k == 0 and f % 2 == 0, k == KD - 1, True)
                    end_group(ins)

            def turn(blocks):
                if not rounds.early(2):
                    pe.wait_ge(tp_free[rounds.slot % 2], rounds.on_bank(rounds.slot % 2))
                t = tp[rounds.slot % 2]
                for src, c in blocks:
                    n = src.shape[0]
                    w = int(np.prod(src.shape[1:]))
                    ins = tr(t[0:w, c:c + n], src, ident[0:n, 0:n])
                ins.then_inc(tp_full, 1)
                rounds.add()

            def turns(src, n):
                for k in range(n // 2):
                    turn([(src[:, t, (2 * k + q) * P:(2 * k + q + 1) * P], q * S + t * P) for q in range(2) for t in range(TT)])

            def turned():
                for b in range(2):
                    pe.wait_ge(tp_free[b], rounds.on_bank(b))

            pe.wait_ge(sem("cond"), 1)
            modc = Tally()

            def mods():
                for n in range(2):
                    if not modc.early(2):
                        pe.wait_ge(sem("mod_evac"), modc.n - 1)
                    for g in range(4):
                        pe.wait_ge(raw_in[g], (modc.n + 1) * 16)
                        for q in range(GK):
                            k = g * GK + q
                            ins = mm(ms[n][:], cond[:, k:k + 1].to_broadcast([P, P]), raw[:, g, q], start=k == 0, stop=k == KD - 1)
                        ins.then_inc(ada_used, 1)
                    modc.add()

            mods()
            with engine_loop(pe, N_FRONT // 8 - 1, (modc, 2)) as i:
                mods()
            pe.wait_ge(sem("ld_ident"), 16)
            for n in range(4):
                pe.wait_ge(sem("h1"), 2 * n + 2)
                for k in range(2 * n, 2 * n + 2):
                    turn([(h1[:, t, (2 * k + q) * P:(2 * k + q + 1) * P], q * S + t * P) for q in range(2) for t in range(TT)])
            turned()
            sums = Tally()

            def mod_product(macc, col):
                pe.wait_ge(mod_acc, sums.n + 1)
                for f in range(4):
                    ins = mm(ms[0][:, bass.ds(col + f, 1)], macc[:, f * P:(f + 1) * P], ones[:], start=True, stop=True)
                ins.then_inc(mod_sum, 1)
                sums.add()

            pe.wait_ge(sem("ones"), 1)
            for _ in range(2):
                rows_chunk(h1T, TT, [4] * 4)
            with engine_loop(pe, 4, (m, 16), (chunks, 4), (sums, 3)) as i:
                mod_product(macc1[0], i * 12)
                rows_chunk(h1T, TT, [4] * 4)
                mod_product(macc1[1], i * 12 + 4)
                rows_chunk(h1T, TT, [4] * 4)
                rows_chunk(h1T, TT, [4] * 4)
                mod_product(macc1[2], i * 12 + 8)
                rows_chunk(h1T, TT, [4] * 4)
            pe.wait_ge(sem("mod_cols"), 1)
            turn([(mcol[:, 0:48], 0)])
            pe.wait_ge(sem("sguw_m"), 1)
            for r in range(2):
                turn([(wsn[:, 4 * r + q], q * P) for q in range(4)])
            turned()
            pe.wait_ge(sem("v_norm"), 1)
            for t in range(TT):
                for g in range(8):
                    ins = mm(ms[t][:, g * 64:(g + 1) * 64], wsT[:, g], pg[:, 1, t, g * 64:(g + 1) * 64], start=True, stop=True)
                ins.then_inc(sem("sgu_mix"), 1)
            pe.wait_ge(sem("y_sgu"), 1)
            for k in range(2):
                turn([(pg[:, 0, t, (2 * k + q) * P:(2 * k + q + 1) * P], q * S + t * P) for q in range(2) for t in range(TT)])
            for k in range(4):
                if k >= 2:
                    pe.wait_ge(sem("yp_hi"), k - 1)
                for s_ in range(TT):
                    ins = mm(ms[k % 2][:, 0:S], pg[:, 5, s_, k * P:(k + 1) * P], poolm[:, k, s_], start=s_ == 0, stop=s_ == TT - 1)
                ins.then_inc(sem("pooled"), 1)
                pe.wait_ge(sem("pooledT"), k + 1)
                mm(ms[k % 2][:, S:2 * S], poolw[:, k], pooledT[:, k], start=True, stop=True).then_inc(sem("pool_y"), 1)
            pe.wait_ge(sem("yp_hi"), 4)
            pe.wait_ge(acc_free, chunks.n)
            units, outs = Tally(), Tally()
            for hp in range(4):
                turn([(pg[:, 2 + w_, t, hp * P:(hp + 1) * P], (2 * w_ + t) * P) for w_ in range(2) for t in range(TT)])
                turned()

                def scores(n):
                    h, qt = divmod(n, 2)
                    r0 = h * DH1
                    bk = score_banks[units.slot % 4]
                    if not units.early(4):
                        pe.wait_ge(sem("max"), units.n - 3)
                    mm(bk[:, 0:(qt + 1) * P], qkT[r0:r0 + DH1, hp % 2, qt],
                       qkT[r0:r0 + DH1, hp % 2, 2:3 + qt], start=True, stop=True).then_inc(sem("sc_full"), 1)
                    units.add()

                scores(0)
                for n in range(4):
                    h, qt = divmod(n, 2)
                    if n < 3:
                        scores(n + 1)
                    head, s = 2 * hp + h, outs.slot % 2
                    pe.wait_ge(sem("exp"), outs.n + 1)
                    turn([(sc1[:, s, q * P:(q + 1) * P], q * P) for q in range(qt + 1)])
                    turned()
                    if not outs.early(2):
                        pe.wait_ge(sem("o_free"), outs.n - 1)
                    for q in range(qt + 1):
                        ins = mm(ms[s][:, 0:DH1], pT1[:, s, q * P:(q + 1) * P], pg[:, 4, q, head * DH1:(head + 1) * DH1],
                                 start=q == 0, stop=q == qt)
                    ins.then_inc(sem("pv"), 1)
                    outs.add()
            pe.wait_ge(sem("o_free"), 16)
            for k in range(2):
                turn([(pg[:, 1, t, (2 * k + q) * P:(2 * k + q + 1) * P], q * S + t * P) for q in range(2) for t in range(TT)])
            turned()
            pe.wait_ge(sem("yp_lo"), 4)
            for n in range(4):
                for br in range(3):
                    rows_chunk([t[:, br] for t in y3T], TT, [4])
            pe.wait_ge(sem("merged"), 1)
            turns(merged, KD)
            turned()
            for n in range(4):
                rows_chunk(mgT, TT, [4] * 4)
                if n:
                    mod_product(macc2[n - 1], (n - 1) * 4)
            mod_product(macc2[3], 12)
            pe.wait_ge(sem("h2"), 1)
            turns(y1, KD)
            pe.wait_ge(sem("mod_cols"), 2)
            turn([(mcol[:, 48:64], 0)])
            turned()

            def up():
                with engine_loop(pe, FC // 2, (m, 8), (chunks, 2)) as i:
                    for _ in range(2):
                        cols_chunk(h2T)

            def down(hid_count):
                pe.wait_ge(sem("hid_lo"), hid_count - 1)
                with engine_loop(pe, 2, (m, 24), (chunks, 2)) as i:
                    for _ in range(2):
                        rows_chunk(hid, TT, DOWN_TILES, hidden=hid_count)

            up()
            down(FC)
            pe.wait_ge(sem("n2"), 1)
            for k in range(KD):
                c = slice(k * P, (k + 1) * P)
                turn([(nmeta[:, c], 0), (n2[:, 0, c], META), (n2[:, 1, c], META + P)])
            turned()
            pe.wait_ge(sem("krw_lo"), 1)
            for k in range(KD):
                ins = three(ms[1][0:ROPE, 0:L], krwh[:, k], krwl[:, k], nT[0][:, k], nT[1][:, k], k == 0, k == KD - 1)
            ins.then_inc(sem("kr"), 1)
            pe.wait_ge(sem("kr_copied"), 1)
            turn([(krT[0:ROPE, META:META + P], 0), (krT[0:ROPE, META + P:L], ROPE), (krT[0:ROPE, 0:META], 2 * ROPE)])
            rows_chunk(nT, TT, [4] * 4, META)
            rows_chunk(nT, TT, [4] * 4, META, meta=ms[0])
            turned()
            for n in range(2):
                b = begin_chunk()
                banks = [b[:, 0, 0:L], b[:, 1, 0:L]] + [t[:, 0:L] for t in (tp, ms)[n]]
                for g in range(KD // GK):
                    s = begin_group()
                    for f in range(4):
                        for q in range(GK):
                            k = g * GK + q
                            ins = three(banks[f], whi[:, s, q, f * P:(f + 1) * P], wlo[:, s, q, f * P:(f + 1) * P],
                                        nT[0][:, k], nT[1][:, k], k == 0, k == KD - 1)
                    end_group(ins)
            pe.wait_ge(acc_free, chunks.n - 1)
            turn([(krn[:META, 2].rearrange("p a b -> p (a b)"), 0), (krn[:, 0].rearrange("p a b -> p (a b)"), META),
                  (krn[:, 1].rearrange("p a b -> p (a b)"), META + P)])
            pe.wait_ge(sem("latn"), 1)
            for k in range(2):
                turn([(qlat[:, t, (2 * k + q) * P:(2 * k + q + 1) * P], q * S + t * P) for q in range(2) for t in range(TT)])
            for k in range(4):
                c = slice(k * P, (k + 1) * P)
                turn([(kvlat[:META, 2, c], 0), (kvlat[:, 0, c], META), (kvlat[:, 1, c], META + P)])
            with engine_loop(pe, 4, (m, 8), (chunks, 2)) as i:
                for _ in range(2):
                    rows_chunk(nT, TT, [4] * 4, META)
            pair, tile = Tally(), Tally()
            turned()

            def outputs():
                q = tile.slot % 4
                pe.wait_ge(sem("xs"), tile.n + 1)
                if q == 0 and not tile.early(1):
                    pe.wait_ge(sem("y_sum"), tile.i * (tile.per // 4) + tile.slot // 4 if tile.i is not None else tile.slot // 4)
                for r in range(2):
                    ins = mm(ms[1][q * 32:(q + 1) * 32, 0:L], bcT[:, 2 + r, q * 32:(q + 1) * 32], xx[:, r],
                             start=r == 0, stop=r == 1)
                ins.then_inc(sem("y_part"), 1)
                tile.add()

            inputs_ = Tally()

            def inputs():
                q = inputs_.slot % 4
                if not inputs_.early(1):
                    pe.wait_ge(sem("bu_free"), inputs_.n)
                rows = slice(q * 32, (q + 1) * 32)
                for r in range(2):
                    ins = mm(acc[1][:, r, 0:L], bcT[rows, r], uj[rows], start=True, stop=True)
                ins.then_inc(sem("bu"), 1)
                inputs_.add()

            def head_pair(i, j):
                first = pair.early(1)
                begin_chunk()
                s = begin_group()
                for h in range(2):
                    for q in range(GK):
                        three(acc[0][:, 0, h * S:(h + 1) * S], whi[:, s, q, h * P:(h + 1) * P], wlo[:, s, q, h * P:(h + 1) * P],
                              qlT[0][:, q], qlT[1][:, q], q == 0, q == GK - 1)
                for t in range(TT):
                    for q in range(GK):
                        ins = three(acc[0][:, 1, t * P:(t + 1) * P], qlT[0][:, q, t * P:(t + 1) * P], qlT[1][:, q, t * P:(t + 1) * P],
                                    whi[:, s, q, 2 * P:3 * P], wlo[:, s, q, 2 * P:3 * P], q == 0, q == GK - 1)
                end_group(ins)
                begin_chunk()
                s = begin_group()
                if not first:
                    pe.wait_ge(sem("bu_free"), inputs_.n)
                    pe.wait_ge(sem("o_free"), outs.n)
                for h in range(2):
                    for q in range(GK):
                        three(acc[1][:, h, 0:L], whi[:, s, q, h * P:(h + 1) * P], wlo[:, s, q, h * P:(h + 1) * P],
                              kvT[0][:, q], kvT[1][:, q], q == 0, q == GK - 1)
                for c0, n, o in ((META, P, ms[0][:, 0:S]), (META + P, P, ms[0][:, S:2 * S]),
                                 (0, META, acc[0][0:META, 1, 2 * P:4 * P])):
                    for q in range(GK):
                        ins = three(o, kvT[0][:, q, c0:c0 + n], kvT[1][:, q, c0:c0 + n],
                                    whi[:, s, q, 2 * P:4 * P], wlo[:, s, q, 2 * P:4 * P], q == 0, q == GK - 1)
                end_group(ins)
                if not first:
                    outputs()
                pe.wait_ge(sem("q_rope"), pair.n + 1)
                turn([(qrn[:, t].rearrange("p a b -> p (a b)"), t * P) for t in range(TT)])
                pe.wait_ge(sem("blk"), pair.n + 1)
                turn([(blk[:, r], r * P) for r in range(4)])
                turned()
                pe.wait_ge(acc_free, chunks.n)
                pe.wait_ge(sem("qnT"), pair.n + 1)
                pair.add()

                def scores(n):
                    h, qt = divmod(n, 2)
                    w = META + (qt + 1) * P
                    bk = acc[0][:, n % 2]
                    if n >= 2:
                        pe.wait_ge(sem("max"), units.n - 1)
                    mm(bk[:, 0:w], qnT[:, h, qt * P:(qt + 1) * P], knT[:, h, 0:w], start=True, stop=False)
                    mm(bk[:, 0:w], qrT[h * ROPE:(h + 1) * ROPE, qt * P:(qt + 1) * P],
                       krT[h * ROPE:(h + 1) * ROPE, 0:w], start=False, stop=True).then_inc(sem("sc_full"), 1)
                    units.add()

                scores(0)
                pe.wait_ge(sem("uj"), pair.n)
                inputs()
                for n in range(4):
                    h, qt = divmod(n, 2)
                    if n < 3:
                        scores(n + 1)
                    s = outs.slot % 2
                    pe.wait_ge(sem("exp"), outs.n + 1)
                    turn([(sc2[:, s, META + q * P:META + (q + 1) * P], q * P) for q in range(qt + 1)]
                         + [(sc2[:, s, 0:META], 2 * P)])
                    turned()
                    pe.wait_ge(sem("o_free"), outs.n)
                    o = ms[0][:, 0:P]
                    for q in range(qt + 1):
                        mm(o, pT2[:, s, q * P:(q + 1) * P], vn2[:, q, h * P:(h + 1) * P], start=q == 0, stop=False)
                    mm(o, pT2[:META, s, 2 * P:3 * P], vn2[:META, 2, h * P:(h + 1) * P],
                       start=False, stop=True).then_inc(sem("pv"), 1)
                    outs.add()
                    if n < 3:
                        inputs()
                        outputs()

            for j in range(2):
                head_pair(0, j)
            with engine_loop(pe, 3, (m, 4), (chunks, 4), (pair, 2), (units, 8), (outs, 8), (rounds, 12), (tile, 8),
                             (inputs_, 8)) as i:
                for j in range(2):
                    head_pair(i + 1, j)
            outputs()
            pe.wait_ge(sem("att"), 1)
            turns(att2, KD)
            turned()
            with engine_loop(pe, 2, (m, 8), (chunks, 2)) as i:
                for _ in range(2):
                    rows_chunk(attT, TT, [4] * 4)
            pe.wait_ge(sem("ys_lo"), 1)
            with engine_loop(pe, 2, (m, 8), (chunks, 4)) as i:
                for _ in range(4):
                    rows_chunk(ysT, TT, [4] * 2)
            pe.wait_ge(sem("mix2"), 1)
            turns(mix2, KD)
            turned()
            with engine_loop(pe, 2, (m, 8), (chunks, 2)) as i:
                for _ in range(2):
                    rows_chunk(mxT, TT, [4] * 4)
            pe.wait_ge(sem("m2"), 1)
            turns(m2, KD)
            turned()
            up()
            down(2 * FC)


def kernel(**inputs):
    from concourse import bacc
    from concourse.bass_utils import run_bass_kernel_spmd

    f = {k: np.asarray(v) for k, v in inputs.items()}
    g = {k: (v[0] if v.ndim > 1 and v.shape[0] == 1 else v) for k, v in f.items()}

    def groups(w, tiles=None, width=C):
        k, n = w.shape
        tiles = tiles or [GK] * (k // (P * GK))
        res = []
        for c in range(0, n, width):
            k0 = 0
            for t in tiles:
                b = np.zeros((P, GK, C), w.dtype)
                b[:, :t, :width] = w[k0 * P:(k0 + t) * P, c:c + width].reshape(t, P, width).transpose(1, 0, 2)
                res.append(b.reshape(P, GK * C))
                k0 += t
        return res

    def pairs(a_, b_, w=256):
        k = a_.shape[0]
        return np.stack([a_.reshape(k, -1, w), b_.reshape(k, -1, w)], 2).reshape(k, -1)

    def interleave(*lists):
        return [x_ for t in zip(*lists) for x_ in t]

    def by(lst, n):
        return [lst[i:i + n] for i in range(0, len(lst), n)]

    def flat(ll):
        return [x_ for l_ in ll for x_ in l_]

    w_up, w_in2 = g["w_up"], g["w_in_2"]
    wq = g["w_q_up_2"].reshape(LAT, HEADS2 // 2, 2, NOPE + ROPE)
    wq = np.concatenate([wq[..., :NOPE].reshape(LAT, HEADS2 // 2, -1), wq[..., NOPE:].reshape(LAT, HEADS2 // 2, -1),
                         np.zeros((LAT, HEADS2 // 2, P), wq.dtype)], -1).reshape(LAT, -1)
    wkv = g["w_kv_up_2"].reshape(LAT, HEADS2 // 2, 2, 2, NOPE).transpose(0, 1, 3, 2, 4).reshape(LAT, -1)
    off_kr, off_u = 2 * LAT, 2 * LAT + ROPE
    stream = (groups(g["w_in"])
              + interleave(groups(g["w_sgu_out"]), groups(g["w_moba_out"]), groups(g["w_pool_out"]))
              + groups(g["w_out"])
              + groups(pairs(w_up[:, :FF], w_up[:, FF:]))
              + groups(g["w_down"], DOWN_TILES)
              + groups(w_in2[:, :2 * LAT]) + groups(w_in2[:, off_u:])
              + interleave(groups(wq), groups(wkv))
              + groups(g["w_attn_proj_2"])
              + flat(interleave(by(groups(g["w_glu_gate_2"]), 2), by(groups(g["w_glu_val_2"]), 2)))
              + groups(g["w_out_2"])
              + groups(pairs(g["w_ffn_gate_2"], g["w_ffn_up_2"]))
              + groups(g["w_ffn_down_2"], DOWN_TILES))
    assert len(stream) == N_GROUPS
    w_ada = np.concatenate([g["w_ada"][:, D:2 * D], g["w_ada"][:, :D], g["w_ada"][:, 2 * D:]], 1)
    b_ada = g["b_ada"].reshape(-1)
    feed = {"w_stream": np.stack(stream), "ada_stream": np.stack(groups(w_ada))}
    feed["x"] = f["x"][0]
    feed["c"] = f["c"][0].reshape(KD, P).T
    feed["b_in"] = g["b_in"].reshape(1, -1)
    feed["b_ada"] = np.concatenate([b_ada[D:2 * D], b_ada[:D]])[None]
    feed["b_ada_cols"] = b_ada[2 * D:].reshape(-1, P).T
    for name in ("g_pre_mix", "g_post_mix", "g_pre_ffn", "g_post_ffn"):
        feed[name] = g[name]
    feed["sgu_g"] = g["sgu_norm_g"]
    feed["norm_mix"], feed["norm_q"], feed["norm_kv"] = g["norm_mix_2"], g["norm_q_2"], g["norm_kv_2"]
    feed["norm_ffn"], feed["norm_final"] = g["norm_ffn_2"], f["norm_final_2"]
    feed["meta"] = f["meta_tokens_2"]
    taps = np.concatenate([g["w_conv"], g["b_conv"][None]], 0).reshape(4, 2, FC, 2, P)
    feed["conv"] = taps.transpose(4, 2, 1, 3, 0).reshape(P, FC, 4, 4)
    feed["sgu_w"] = g["sgu_w"].transpose(1, 0, 2)
    feed["sgu_b"] = g["sgu_b"].T
    feed["pool_scale"] = g["pool_scale"].reshape(4, P).T
    feed["pool_w"] = g["pool_w"].transpose(1, 0, 2)
    feed["w_kr"] = w_in2[:, off_kr:off_kr + ROPE].reshape(KD, P, ROPE).transpose(1, 0, 2)
    feed["ssm_d"] = g["ssm_d_2"].reshape(KS, P).T
    st = lambda v: v.reshape(NST, P, *v.shape[2:])
    feed["lam_re"], feed["lam_im"] = st(g["ssm_lambda_re_2"]).T, st(g["ssm_lambda_im_2"]).T
    feed["log_step"] = st(np.repeat(g["ssm_log_step_2"][:, None], 64, 1)).T
    feed["ssm_b_re"], feed["ssm_b_im"] = (st(g[f"ssm_b_{r}_2"]).transpose(1, 0, 2) for r in ("re", "im"))
    feed["ssm_c_re"], feed["ssm_c_im"] = (g[f"ssm_c_{r}_2"].reshape(KS, P, 64).transpose(1, 0, 2) for r in ("re", "im"))
    one = np.float32
    feed["ident"] = np.eye(P, dtype=one)
    tok = np.arange(S)
    pm = np.zeros((4, S, S), one)
    for wi, w in enumerate((2, 4, 8, 16)):
        inside = (tok[:, None] <= tok[None]) & (tok[:, None] > tok[None] - w)
        pm[wi] = inside / np.minimum(tok + 1, w)[None] - np.eye(S)
    feed["pool_m"] = pm.reshape(4, TT, P, S).transpose(2, 0, 1, 3)
    dq = (tok[None] - tok[:, None]).astype(one)
    feed["dist"] = np.where(dq <= 0, dq, NEG).astype(one).reshape(TT, P, S).transpose(1, 0, 2)
    feed["tril"] = np.tril(np.ones((P, P), one))
    pos = np.arange(L)
    m2 = np.where(pos[None] <= tok[:, None] + META, 0.0, NEG).astype(one)
    feed["mask2"] = m2.reshape(TT, P, L).transpose(1, 0, 2)
    half = ROPE // 2
    freqs = (one(10000.0) ** (-np.arange(half, dtype=one) / one(half))).astype(one)
    ang = pos.astype(one)[:, None] * freqs[None]
    tab = np.zeros((P, 2, 3, half), one)
    for r, fn in enumerate((np.cos, np.sin)):
        v = fn(ang.astype(np.float64)).astype(one)
        tab[:, r, 0], tab[:, r, 1], tab[:META, r, 2] = v[META:META + P], v[META + P:], v[:META]
    feed["rope"] = tab
    gi = np.arange(P)
    feed["bmask"] = (gi[:, None] // 64 == np.arange(2)[None]).astype(one)
    feed["cmask"] = (gi[:, None] // 16 % 2 == np.arange(2)[None]).astype(one)

    nc = bacc.Bacc("TRN2", target_bir_lowering=False, num_devices=1)
    feed = {k: np.ascontiguousarray(v) for k, v in feed.items()}
    aps = {k: nc.dram_tensor(k, v.shape, F32, kind="ExternalInput").ap() for k, v in feed.items()}
    aps["x_dram"] = nc.dram_tensor("x_dram", (P, TT, D), F32, kind="Internal").ap()
    aps["mod_dram"] = nc.dram_tensor("mod_dram", (NMOD - 2, D), F32, kind="Internal").ap()
    out = nc.dram_tensor("out", (1, S, D), F32, kind="ExternalOutput").ap()
    block_program(nc, aps, out)
    res = run_bass_kernel_spmd(nc, [feed], core_ids=[0])
    return res.results[0]["out"]
```
